# Optimizing a Trainium2 kernel written in Bass

```python
import jax
import jax.numpy as jnp
from jax import lax
import numpy as np
import math
import jax, jax.numpy as jnp

D_MODEL = 1024
BATCH = 1
SEQ = 512
DEPTH = 2

GRID_W = 64
CTX_LEN = 256
HEAD_DIM = 64
MIX_HALF = D_MODEL // 2
N_MOD = 9
D_FF = ((8 * D_MODEL // 3 + 127) // 128) * 128
EPS = 1e-6
ROPE_THETA = 10000.0
NEG = -1e30
N_EVEN = (DEPTH + 1) // 2
N_ODD = DEPTH // 2
A_HEADS = MIX_HALF // HEAD_DIM
A_KV_HEADS = A_HEADS // 4
WINDOW = 128
A_BLOCK = 128
A_W = A_HEADS * HEAD_DIM
A_KV = A_KV_HEADS * HEAD_DIM
B_GROUPS = MIX_HALF // HEAD_DIM
B_CHUNK = 128
B_W = B_GROUPS * HEAD_DIM
EVEN_SPLIT = [A_W, A_W + A_KV, A_W + 2 * A_KV, A_W + 2 * A_KV + B_W]
EVEN_IN = A_W + 2 * A_KV + 2 * B_W
EVEN_MIX = A_W + B_W
POOL_WINDOWS = (2, 4, 8, 16)
C_GROUPS = len(POOL_WINDOWS)
C_W = MIX_HALF
C_GROUP_W = C_W // C_GROUPS
D_HEADS = MIX_HALF // HEAD_DIM
D_W = D_HEADS * HEAD_DIM
NA_ROWS = 8
NA_COLS = 16
ODD_SPLIT = [C_W, C_W + D_W, C_W + 2 * D_W]
ODD_IN = C_W + 3 * D_W
ODD_MIX = C_W + D_W


def rms_norm(x, g):
    xf = x.astype(jnp.float32)
    y = xf * lax.rsqrt(jnp.mean(xf * xf, axis=-1, keepdims=True) + EPS)
    return (y * g.astype(jnp.float32)).astype(x.dtype)

def norm_mod(h, g, shift, scale):
    return rms_norm(h, g) * (1.0 + scale) + shift

def swiglu(x, w_gu, w_down):
    gt, up = jnp.split(x @ w_gu, 2, axis=-1)
    return (jax.nn.silu(gt) * up) @ w_down

def half_ffn(h, g, shift, scale, gate, w_gu, w_down):
    return h + 0.5 * gate * swiglu(norm_mod(h, g, shift, scale), w_gu, w_down)

def axial_rope_angles(s):
    t = jnp.arange(s)
    row = (t // GRID_W).astype(jnp.float32)
    col = (t % GRID_W).astype(jnp.float32)
    m = HEAD_DIM // 4
    inv = 1.0 / (ROPE_THETA ** (jnp.arange(m, dtype=jnp.float32) / m))
    return row[:, None] * inv[None, :], col[:, None] * inv[None, :]

def rotate(x, ang):
    x1, x2 = jnp.split(x, 2, axis=-1)
    cos = jnp.cos(ang)[None, :, None, :]
    sin = jnp.sin(ang)[None, :, None, :]
    return jnp.concatenate([x1 * cos - x2 * sin, x2 * cos + x1 * sin], axis=-1)

def apply_rope_2d(x, ang_r, ang_c):
    half = HEAD_DIM // 2
    return jnp.concatenate([rotate(x[..., :half], ang_r), rotate(x[..., half:], ang_c)], axis=-1).astype(x.dtype)

def ctx_attention(q, k, v, sink):
    b, l, nq, dh = q.shape
    nkv = k.shape[2]
    g = nq // nkv
    qg = q.reshape(b, l, nkv, g, dh)
    sc = jnp.einsum('bqkgd,bskd->bkgqs', qg, k).astype(jnp.float32) * dh ** -0.5
    if sink is not None:
        s_sink = jnp.broadcast_to(sink.astype(jnp.float32).reshape(nkv, g)[None, :, :, None, None], sc.shape[:-1] + (1,))
        sc = jnp.concatenate([sc, s_sink], axis=-1)
    p = jax.nn.softmax(sc, axis=-1)[..., :l].astype(v.dtype)
    o = jnp.einsum('bkgqs,bskd->bqkgd', p, v)
    return o.reshape(b, l, nq * dh)

def window_gqa(q, k, v, k_ctx, v_ctx, sink):
    b, s, nq, dh = q.shape
    nkv = k.shape[2]
    g = nq // nkv
    nb = s // A_BLOCK
    lc = k_ctx.shape[1]
    nloc = 3 * A_BLOCK
    qb = q.reshape(b, nb, A_BLOCK, nkv, g, dh)

    def band(t):
        tb = t.reshape(b, nb, A_BLOCK, nkv, dh)
        pad = jnp.zeros_like(tb[:, :1])
        prev = jnp.concatenate([pad, tb[:, :-1]], axis=1)
        nxt = jnp.concatenate([tb[:, 1:], pad], axis=1)
        return jnp.concatenate([prev, tb, nxt], axis=2)

    kb, vb = band(k), band(v)
    scale = dh ** -0.5
    qpos = jnp.arange(nb)[:, None, None] * A_BLOCK + jnp.arange(A_BLOCK)[None, :, None]
    kpos = (jnp.arange(nb)[:, None, None] - 1) * A_BLOCK + jnp.arange(nloc)[None, None, :]
    valid = (jnp.abs(qpos - kpos) <= WINDOW) & (kpos >= 0) & (kpos < s)
    s_loc = jnp.einsum('bnqkgd,bnskd->bnkgqs', qb, kb).astype(jnp.float32) * scale
    s_loc = jnp.where(valid[None, :, None, None], s_loc, NEG)
    s_ctx = jnp.einsum('bnqkgd,bckd->bnkgqc', qb, k_ctx).astype(jnp.float32) * scale
    s_sink = jnp.broadcast_to(sink.astype(jnp.float32).reshape(nkv, g)[None, None, :, :, None, None], s_loc.shape[:-1] + (1,))
    p = jax.nn.softmax(jnp.concatenate([s_loc, s_ctx, s_sink], axis=-1), axis=-1).astype(v.dtype)
    o = (jnp.einsum('bnkgqs,bnskd->bnqkgd', p[..., :nloc], vb)
         + jnp.einsum('bnkgqc,bckd->bnqkgd', p[..., nloc:nloc + lc], v_ctx))
    return o.reshape(b, s, nq * dh)

def chunk_gmlp(bu, bv, v_gain, ws, bias):
    b, s, _ = bu.shape
    u = jax.nn.gelu(bu)
    vv = jax.nn.gelu(bv).reshape(b, s // B_CHUNK, B_CHUNK, B_GROUPS, HEAD_DIM)
    vv = rms_norm(vv, v_gain.reshape(B_GROUPS, HEAD_DIM))
    mixed = jnp.einsum('gij,bnjgd->bnigd', ws, vv) + bias.T[None, None, :, :, None]
    return u * mixed.reshape(b, s, B_W)

def multiscale_pool(xp, w_pool, c_scale):
    b, s, _ = xp.shape
    xf = xp.astype(jnp.float32)
    cs = jnp.concatenate([jnp.zeros_like(xf[:, :1]), jnp.cumsum(xf, axis=1)], axis=1)
    t = jnp.arange(s)
    outs = []
    for gi, w in enumerate(POOL_WINDOWS):
        lo = jnp.clip(t - w // 2, 0, s)
        hi = jnp.clip(t + w - w // 2, 0, s)
        csg = cs[..., gi * C_GROUP_W:(gi + 1) * C_GROUP_W]
        mean = (csg[:, hi] - csg[:, lo]) / (hi - lo).astype(jnp.float32)[None, :, None]
        outs.append(mean - xf[..., gi * C_GROUP_W:(gi + 1) * C_GROUP_W])
    pooled = jnp.stack(outs, axis=2).astype(xp.dtype)
    y = jnp.einsum('bsgc,gcd->bsgd', pooled, w_pool).reshape(b, s, C_W)
    return y * c_scale

def neighbourhood_attn(q, k, v, k_ctx, v_ctx, rpb):
    b, s, nh, dh = q.shape
    rows = s // GRID_W
    kr = min(NA_ROWS, rows)
    nqb = GRID_W // NA_COLS
    kbw = 2 * NA_COLS
    q5 = q.reshape(b, rows, GRID_W, nh, dh)
    k5 = k.reshape(b, rows, GRID_W, nh, dh)
    v5 = v.reshape(b, rows, GRID_W, nh, dh)
    qcol = np.arange(GRID_W).reshape(nqb, NA_COLS)
    qstart = np.clip(qcol - NA_COLS // 2, 0, GRID_W - NA_COLS)
    kstart = np.clip(np.arange(nqb) * NA_COLS - NA_COLS // 2, 0, GRID_W - kbw)
    kcol = kstart[:, None] + np.arange(kbw)[None, :]
    col_valid = (kcol[:, None, :] >= qstart[:, :, None]) & (kcol[:, None, :] < qstart[:, :, None] + NA_COLS)
    col_idx = np.clip(kcol[:, None, :] - qcol[:, :, None], 1 - NA_COLS, NA_COLS - 1) + NA_COLS - 1
    scale = dh ** -0.5
    nloc = kr * kbw

    def row_block(r):
        r0 = jnp.clip(r - kr // 2, 0, rows - kr)
        qr = lax.dynamic_index_in_dim(q5, r, axis=1, keepdims=False).reshape(b, nqb, NA_COLS, nh, dh)
        kblk = lax.dynamic_slice_in_dim(k5, r0, kr, axis=1)[:, :, kcol]
        vblk = lax.dynamic_slice_in_dim(v5, r0, kr, axis=1)[:, :, kcol]
        row_idx = r0 + jnp.arange(kr) - r + NA_ROWS - 1
        bias = jnp.transpose(rpb[:, row_idx][:, :, col_idx], (0, 2, 3, 1, 4))
        s_loc = jnp.einsum('bmqhd,brmkhd->bhmqrk', qr, kblk).astype(jnp.float32) * scale + bias[None].astype(jnp.float32)
        s_loc = jnp.where(col_valid[None, None, :, :, None, :], s_loc, NEG)
        s_ctx = jnp.einsum('bmqhd,bchd->bhmqc', qr, k_ctx).astype(jnp.float32) * scale
        p = jax.nn.softmax(jnp.concatenate([s_loc.reshape(b, nh, nqb, NA_COLS, nloc), s_ctx], axis=-1), axis=-1).astype(v.dtype)
        o = (jnp.einsum('bhmqrk,brmkhd->bmqhd', p[..., :nloc].reshape(s_loc.shape), vblk)
             + jnp.einsum('bhmqc,bchd->bmqhd', p[..., nloc:], v_ctx))
        return o.reshape(b, GRID_W, nh, dh)

    out = lax.map(row_block, jnp.arange(rows))
    return jnp.moveaxis(out, 0, 1).reshape(b, s, nh * dh)

def even_mixer(z, zc, w_in, w_out, q_gain, k_gain, sink, v_gain, ws, bias, ang_r, ang_c, need_ctx):
    b, s, _ = z.shape
    l = zc.shape[1]
    q, k, v, bu, bv = jnp.split(z @ w_in, EVEN_SPLIT, axis=-1)
    q = apply_rope_2d(rms_norm(q.reshape(b, s, A_HEADS, HEAD_DIM), q_gain), ang_r, ang_c)
    k = apply_rope_2d(rms_norm(k.reshape(b, s, A_KV_HEADS, HEAD_DIM), k_gain), ang_r, ang_c)
    v = v.reshape(b, s, A_KV_HEADS, HEAD_DIM)
    if need_ctx:
        qc, kc, vc, buc, bvc = jnp.split(zc @ w_in, EVEN_SPLIT, axis=-1)
    else:
        kc, vc = jnp.split(zc @ w_in[:, A_W:A_W + 2 * A_KV], 2, axis=-1)
    kc = rms_norm(kc.reshape(b, l, A_KV_HEADS, HEAD_DIM), k_gain)
    vc = vc.reshape(b, l, A_KV_HEADS, HEAD_DIM)
    y = jnp.concatenate([window_gqa(q, k, v, kc, vc, sink), chunk_gmlp(bu, bv, v_gain, ws, bias)], axis=-1) @ w_out
    yc = None
    if need_ctx:
        qc = rms_norm(qc.reshape(b, l, A_HEADS, HEAD_DIM), q_gain)
        yc = jnp.concatenate([ctx_attention(qc, kc, vc, sink), chunk_gmlp(buc, bvc, v_gain, ws, bias)], axis=-1) @ w_out
    return y, yc

def odd_mixer(z, zc, w_in, w_out, w_pool, c_scale, q_gain, k_gain, rpb, need_ctx):
    b, s, _ = z.shape
    l = zc.shape[1]
    xp, q, k, v = jnp.split(z @ w_in, ODD_SPLIT, axis=-1)
    q = rms_norm(q.reshape(b, s, D_HEADS, HEAD_DIM), q_gain)
    k = rms_norm(k.reshape(b, s, D_HEADS, HEAD_DIM), k_gain)
    v = v.reshape(b, s, D_HEADS, HEAD_DIM)
    if need_ctx:
        xpc, qc, kc, vc = jnp.split(zc @ w_in, ODD_SPLIT, axis=-1)
    else:
        kc, vc = jnp.split(zc @ w_in[:, C_W + D_W:], 2, axis=-1)
    kc = rms_norm(kc.reshape(b, l, D_HEADS, HEAD_DIM), k_gain)
    vc = vc.reshape(b, l, D_HEADS, HEAD_DIM)
    y = jnp.concatenate([multiscale_pool(xp, w_pool, c_scale), neighbourhood_attn(q, k, v, kc, vc, rpb)], axis=-1) @ w_out
    yc = None
    if need_ctx:
        qc = rms_norm(qc.reshape(b, l, D_HEADS, HEAD_DIM), q_gain)
        yc = jnp.concatenate([multiscale_pool(xpc, w_pool, c_scale), ctx_attention(qc, kc, vc, None)], axis=-1) @ w_out
    return y, yc

def first_inputs(seed: int = 0) -> dict:
    key = jax.random.key(seed)
    ks = jax.random.split(key, 24)
    f32 = jnp.float32

    def nrm(k, shape, sd):
        return jax.random.normal(k, shape, f32) * sd

    d = D_MODEL
    return {
        'x': nrm(ks[0], (BATCH, SEQ, d), 1.0),
        'c': nrm(ks[1], (BATCH, d), 1.0),
        'ctx': nrm(ks[2], (BATCH, CTX_LEN, d), 1.0),
        'c_ctx': nrm(ks[3], (d,), 1.0),
        'ada_w': nrm(ks[4], (DEPTH, d, N_MOD * d), 0.5 * d ** -0.5),
        'ada_b': nrm(ks[5], (DEPTH, N_MOD * d), 0.02),
        'norm_g': 1.0 + nrm(ks[6], (DEPTH, 3, d), 0.05),
        'ffn_w_gu': nrm(ks[7], (DEPTH, 2, d, 2 * D_FF), d ** -0.5),
        'ffn_w_down': nrm(ks[8], (DEPTH, 2, D_FF, d), D_FF ** -0.5),
        'ev_w_in': nrm(ks[9], (N_EVEN, d, EVEN_IN), d ** -0.5),
        'ev_w_out': nrm(ks[10], (N_EVEN, EVEN_MIX, d), EVEN_MIX ** -0.5),
        'a_q_gain': 1.0 + nrm(ks[11], (N_EVEN, HEAD_DIM), 0.05),
        'a_k_gain': 1.0 + nrm(ks[12], (N_EVEN, HEAD_DIM), 0.05),
        'a_sink': nrm(ks[13], (N_EVEN, A_HEADS), 0.5),
        'b_v_gain': 1.0 + nrm(ks[14], (N_EVEN, B_W), 0.05),
        'b_ws': nrm(ks[15], (N_EVEN, B_GROUPS, B_CHUNK, B_CHUNK), B_CHUNK ** -0.5),
        'b_bias': 1.0 + nrm(ks[16], (N_EVEN, B_GROUPS, B_CHUNK), 0.1),
        'od_w_in': nrm(ks[17], (N_ODD, d, ODD_IN), d ** -0.5),
        'od_w_out': nrm(ks[18], (N_ODD, ODD_MIX, d), ODD_MIX ** -0.5),
        'c_w_pool': nrm(ks[19], (N_ODD, C_GROUPS, C_GROUP_W, C_GROUP_W), C_GROUP_W ** -0.5),
        'c_scale': 1.0 + nrm(ks[20], (N_ODD, C_W), 0.1),
        'd_q_gain': 1.0 + nrm(ks[21], (N_ODD, HEAD_DIM), 0.05),
        'd_k_gain': 1.0 + nrm(ks[22], (N_ODD, HEAD_DIM), 0.05),
        'd_rpb': nrm(ks[23], (N_ODD, D_HEADS, 2 * NA_ROWS - 1, 2 * NA_COLS - 1), 0.5),
    }

def first_block(x, c, ctx, c_ctx, ada_w, ada_b, norm_g, ffn_w_gu, ffn_w_down,
              ev_w_in, ev_w_out, a_q_gain, a_k_gain, a_sink, b_v_gain, b_ws, b_bias,
              od_w_in, od_w_out, c_w_pool, c_scale, d_q_gain, d_k_gain, d_rpb):
    ang_r, ang_c = axial_rope_angles(x.shape[1])
    sc = jax.nn.silu(c)
    scc = jax.nn.silu(c_ctx)
    h, hc = x, ctx
    for li in range(DEPTH):
        need_ctx = li < DEPTH - 1
        m = jnp.split((sc @ ada_w[li] + ada_b[li])[:, None, :], N_MOD, axis=-1)
        mc = jnp.split(scc @ ada_w[li] + ada_b[li], N_MOD, axis=-1)
        h = half_ffn(h, norm_g[li, 0], m[0], m[1], m[2], ffn_w_gu[li, 0], ffn_w_down[li, 0])
        hc = half_ffn(hc, norm_g[li, 0], mc[0], mc[1], mc[2], ffn_w_gu[li, 0], ffn_w_down[li, 0])
        z = norm_mod(h, norm_g[li, 1], m[3], m[4])
        zc = norm_mod(hc, norm_g[li, 1], mc[3], mc[4])
        if li % 2 == 0:
            e = li // 2
            y, yc = even_mixer(z, zc, ev_w_in[e], ev_w_out[e], a_q_gain[e], a_k_gain[e], a_sink[e],
                               b_v_gain[e], b_ws[e], b_bias[e], ang_r, ang_c, need_ctx)
        else:
            o = li // 2
            y, yc = odd_mixer(z, zc, od_w_in[o], od_w_out[o], c_w_pool[o], c_scale[o],
                              d_q_gain[o], d_k_gain[o], d_rpb[o], need_ctx)
        h = h + m[5] * y
        h = half_ffn(h, norm_g[li, 2], m[6], m[7], m[8], ffn_w_gu[li, 1], ffn_w_down[li, 1])
        if need_ctx:
            hc = hc + mc[5] * yc
            hc = half_ffn(hc, norm_g[li, 2], mc[6], mc[7], mc[8], ffn_w_gu[li, 1], ffn_w_down[li, 1])
    return h


DEPTH_2 = 1

HEAD_DIM_2 = 128
DN_HEADS = D_MODEL // 256
DN_WIDTH = DN_HEADS * HEAD_DIM_2
CONV_WIDTH = 4
CHUNK = 64
SWA_GROUPS = ((128, 1), (512, 4), (2048, 16))
N_GROUPS = 3
SWA_HEADS = D_MODEL // 256
SWA_WIDTH = SWA_HEADS * HEAD_DIM_2
ROPE_DIM = HEAD_DIM_2 // 4
ROPE_THETA_2 = 500000.0
N_BRANCHES = 2
NEG_INF = -1e30

IN_SIZES = (3 * DN_WIDTH, DN_WIDTH, DN_HEADS, DN_HEADS,
            N_GROUPS * SWA_WIDTH, N_GROUPS * SWA_WIDTH, N_GROUPS * SWA_WIDTH, SWA_WIDTH,
            N_BRANCHES * D_MODEL)
IN_COLS = sum(IN_SIZES)


def rms_norm_2(x, w):
    xf = x.astype(jnp.float32)
    y = xf * lax.rsqrt(jnp.mean(xf * xf, axis=-1, keepdims=True) + EPS)
    return y.astype(x.dtype) * w.astype(x.dtype)

def l2_normalize(x):
    return x * lax.rsqrt(jnp.sum(x * x, axis=-1, keepdims=True) + EPS)

def causal_depthwise_conv(x, w):
    c = x.shape[-1]
    return lax.conv_general_dilated(x, w.astype(x.dtype), window_strides=(1,), padding=[(CONV_WIDTH - 1, 0)],
                                    dimension_numbers=('NWC', 'WIO', 'NWC'), feature_group_count=c)

def partial_rope(x, cos, sin):
    half = ROPE_DIM // 2
    x1, x2, xp = x[..., :half], x[..., half:ROPE_DIM], x[..., ROPE_DIM:]
    c = cos[:, None, None, :].astype(x.dtype)
    s = sin[:, None, None, :].astype(x.dtype)
    return jnp.concatenate([x1 * c - x2 * s, x2 * c + x1 * s, xp], axis=-1)

def gated_delta_rule_chunked(q, k, v, g, beta):
    B, H, T, Dk = q.shape
    Dv = v.shape[-1]
    N = T // CHUNK
    q = q.reshape(B, H, N, CHUNK, Dk)
    k = k.reshape(B, H, N, CHUNK, Dk)
    v = v.reshape(B, H, N, CHUNK, Dv)
    g = g.reshape(B, H, N, CHUNK)
    beta = beta.reshape(B, H, N, CHUNK)
    gc = jnp.cumsum(g, axis=-1)
    idx = jnp.arange(CHUNK)
    causal = idx[:, None] >= idx[None, :]
    strict = idx[:, None] > idx[None, :]
    decay = jnp.exp(jnp.where(causal, gc[..., :, None] - gc[..., None, :], -jnp.inf))
    kb = k * beta[..., None]
    lower = jnp.where(strict, jnp.einsum('bhnid,bhnjd->bhnij', kb, k) * decay, 0.0)
    eye = jnp.eye(CHUNK, dtype=q.dtype)
    tmat = lax.linalg.triangular_solve(eye + lower, jnp.broadcast_to(eye, lower.shape),
                                       left_side=True, lower=True, unit_diagonal=True)
    u = jnp.einsum('bhnij,bhnjd->bhnid', tmat, v * beta[..., None])
    w = jnp.einsum('bhnij,bhnjd->bhnid', tmat, kb * jnp.exp(gc)[..., None])
    a_intra = jnp.where(causal, jnp.einsum('bhnid,bhnjd->bhnij', q, k) * decay, 0.0)

    def step(S, inp):
        qi, ki, ui, wi, ai, gci = inp
        v_new = ui - jnp.einsum('bhck,bhkv->bhcv', wi, S)
        o = jnp.einsum('bhck,bhkv->bhcv', qi * jnp.exp(gci)[..., None], S) + jnp.einsum('bhij,bhjv->bhiv', ai, v_new)
        glast = gci[..., -1]
        S = S * jnp.exp(glast)[..., None, None] + jnp.einsum(
            'bhck,bhcv->bhkv', ki * jnp.exp(glast[..., None] - gci)[..., None], v_new)
        return S, o

    xs = tuple(jnp.moveaxis(a, 2, 0) for a in (q, k, u, w, a_intra, gc))
    s0 = jnp.zeros((B, H, Dk, Dv), q.dtype)
    _, o = lax.scan(step, s0, xs)
    return jnp.moveaxis(o, 0, 2).reshape(B, H, T, Dv)

def dilated_window_attention(q, k, v, window, dilation):
    B, T, H, Dh = q.shape
    L = T // dilation
    blk = window // dilation
    nb = -(-L // blk)
    Lp = nb * blk

    def to_sub(x):
        x = x.astype(jnp.float32).reshape(B, L, dilation, H, Dh).transpose(0, 2, 3, 1, 4)
        return jnp.pad(x, ((0, 0), (0, 0), (0, 0), (0, Lp - L), (0, 0)))

    def windows(x):
        xp = jnp.pad(x, ((0, 0), (0, 0), (0, 0), (blk, 0), (0, 0))).reshape(B, dilation, H, nb + 1, blk, Dh)
        return jnp.concatenate([xp[:, :, :, :-1], xp[:, :, :, 1:]], axis=4)

    qb = to_sub(q).reshape(B, dilation, H, nb, blk, Dh)
    kw = windows(to_sub(k))
    vw = windows(to_sub(v))
    s = jnp.einsum('brhnqd,brhnkd->brhnqk', qb, kw) * (Dh ** -0.5)
    i = jnp.arange(blk)[:, None]
    j = jnp.arange(2 * blk)[None, :]
    dist = blk + i - j
    key_pos = (jnp.arange(nb)[:, None, None] - 1) * blk + j[None]
    valid = (dist >= 0)[None] & (dist <= blk)[None] & (key_pos >= 0)
    s = jnp.where(valid, s, NEG_INF)
    lse = jax.nn.logsumexp(s, axis=-1)
    p = jnp.exp(s - lse[..., None])
    o = jnp.einsum('brhnqk,brhnkd->brhnqd', p, vw)
    o = o.reshape(B, dilation, H, Lp, Dh)[:, :, :, :L].transpose(0, 3, 1, 2, 4).reshape(B, T, H, Dh)
    lse = lse.reshape(B, dilation, H, Lp)[..., :L].transpose(0, 3, 1, 2).reshape(B, T, H)
    return o, lse

def second_inputs(seed: int = 0) -> dict:
    key = jax.random.key(seed)
    ks = jax.random.split(key, 13)
    f32 = jnp.float32
    x = jax.random.normal(ks[0], (BATCH, SEQ, D_MODEL), f32)
    norm_w = 1.0 + 0.02 * jax.random.normal(ks[1], (DEPTH_2, D_MODEL), f32)
    w_in = jax.random.normal(ks[2], (DEPTH_2, D_MODEL, IN_COLS), f32) * D_MODEL ** -0.5
    conv_w = jax.random.normal(ks[3], (DEPTH_2, CONV_WIDTH, 1, 3 * DN_WIDTH), f32) * CONV_WIDTH ** -0.5
    dn_a_log = jnp.log(jax.random.uniform(ks[4], (DEPTH_2, DN_HEADS), f32, 1.0, 16.0))
    dn_dt_bias = 0.1 * jax.random.normal(ks[5], (DEPTH_2, DN_HEADS), f32)
    dn_norm_w = 1.0 + 0.02 * jax.random.normal(ks[6], (DEPTH_2, HEAD_DIM_2), f32)
    q_norm_w = 1.0 + 0.02 * jax.random.normal(ks[7], (DEPTH_2, N_GROUPS, HEAD_DIM_2), f32)
    k_norm_w = 1.0 + 0.02 * jax.random.normal(ks[8], (DEPTH_2, N_GROUPS, HEAD_DIM_2), f32)
    w_branch_dn = jax.random.normal(ks[9], (DEPTH_2, DN_WIDTH, D_MODEL), f32) * DN_WIDTH ** -0.5
    w_branch_swa = jax.random.normal(ks[10], (DEPTH_2, SWA_WIDTH, D_MODEL), f32) * SWA_WIDTH ** -0.5
    w_out = jax.random.normal(ks[11], (DEPTH_2, D_MODEL, D_MODEL), f32) * D_MODEL ** -0.5
    return {"x": x, "norm_w": norm_w, "w_in": w_in, "conv_w": conv_w, "dn_a_log": dn_a_log,
            "dn_dt_bias": dn_dt_bias, "dn_norm_w": dn_norm_w, "q_norm_w": q_norm_w, "k_norm_w": k_norm_w,
            "w_branch_dn": w_branch_dn, "w_branch_swa": w_branch_swa, "w_out": w_out}

def second_block(x, norm_w, w_in, conv_w, dn_a_log, dn_dt_bias, dn_norm_w, q_norm_w, k_norm_w,
              w_branch_dn, w_branch_swa, w_out):
    B, T, _ = x.shape
    split_points = [int(p) for p in np.cumsum(IN_SIZES)[:-1]]
    pos = jnp.arange(T, dtype=jnp.float32)
    inv_freq = ROPE_THETA_2 ** (-jnp.arange(0, ROPE_DIM, 2, dtype=jnp.float32) / ROPE_DIM)
    ang = pos[:, None] * inv_freq[None, :]
    cos, sin = jnp.cos(ang), jnp.sin(ang)

    for layer in range(DEPTH_2):
        h = rms_norm_2(x, norm_w[layer])
        proj = h @ w_in[layer]
        (dn_qkv, dn_z, dn_b, dn_a, swa_q, swa_k, swa_v, swa_z, gates) = jnp.split(proj, split_points, axis=-1)

        qkv = jax.nn.silu(causal_depthwise_conv(dn_qkv, conv_w[layer]))
        dq, dk, dv = jnp.split(qkv.astype(jnp.float32), 3, axis=-1)
        to_heads = lambda t: t.reshape(B, T, DN_HEADS, HEAD_DIM_2).transpose(0, 2, 1, 3)
        dq = l2_normalize(to_heads(dq)) * (HEAD_DIM_2 ** -0.5)
        dk = l2_normalize(to_heads(dk))
        dv = to_heads(dv)
        beta = jax.nn.sigmoid(dn_b.astype(jnp.float32)).transpose(0, 2, 1)
        g = (-jnp.exp(dn_a_log[layer].astype(jnp.float32))
             * jax.nn.softplus(dn_a.astype(jnp.float32) + dn_dt_bias[layer].astype(jnp.float32))).transpose(0, 2, 1)
        o_dn = gated_delta_rule_chunked(dq, dk, dv, g, beta).transpose(0, 2, 1, 3).astype(x.dtype)
        o_dn = rms_norm_2(o_dn, dn_norm_w[layer]) * jax.nn.silu(dn_z.reshape(B, T, DN_HEADS, HEAD_DIM_2))
        y_dn = o_dn.reshape(B, T, DN_WIDTH) @ w_branch_dn[layer]

        grp = lambda t: t.reshape(B, T, N_GROUPS, SWA_HEADS, HEAD_DIM_2)
        sq = partial_rope(rms_norm_2(grp(swa_q), q_norm_w[layer][:, None, :]), cos, sin)
        sk = partial_rope(rms_norm_2(grp(swa_k), k_norm_w[layer][:, None, :]), cos, sin)
        sv = grp(swa_v)
        outs, lses = [], []
        for gi, (window, dilation) in enumerate(SWA_GROUPS):
            o_g, lse_g = dilated_window_attention(sq[:, :, gi], sk[:, :, gi], sv[:, :, gi], window, dilation)
            outs.append(o_g)
            lses.append(lse_g)
        alpha = jax.nn.softmax(jnp.stack(lses, axis=0), axis=0)
        o_swa = jnp.sum(alpha[..., None] * jnp.stack(outs, axis=0), axis=0).astype(x.dtype)
        o_swa = o_swa * jax.nn.silu(swa_z.reshape(B, T, SWA_HEADS, HEAD_DIM_2))
        y_swa = o_swa.reshape(B, T, SWA_WIDTH) @ w_branch_swa[layer]

        g_dn, g_swa = jnp.split(gates, 2, axis=-1)
        merged = jax.nn.sigmoid(g_dn) * y_dn + jax.nn.sigmoid(g_swa) * y_swa
        x = x + merged @ w_out[layer]
    return x


def setup_inputs(seed=0):
    out = dict(first_inputs(seed))
    for name, value in second_inputs(seed + 1).items():
        if name != "x":
            out[name + "_2"] = value
    return out


def reference(
    x, c, ctx, c_ctx, ada_w, ada_b, norm_g, ffn_w_gu, ffn_w_down, ev_w_in, ev_w_out, a_q_gain,
    a_k_gain, a_sink, b_v_gain, b_ws, b_bias, od_w_in, od_w_out, c_w_pool, c_scale, d_q_gain,
    d_k_gain, d_rpb, norm_w_2, w_in_2, conv_w_2, dn_a_log_2, dn_dt_bias_2, dn_norm_w_2,
    q_norm_w_2, k_norm_w_2, w_branch_dn_2, w_branch_swa_2, w_out_2,
):
    x = first_block(
        x, c, ctx, c_ctx, ada_w, ada_b, norm_g, ffn_w_gu, ffn_w_down, ev_w_in, ev_w_out,
        a_q_gain, a_k_gain, a_sink, b_v_gain, b_ws, b_bias, od_w_in, od_w_out, c_w_pool,
        c_scale, d_q_gain, d_k_gain, d_rpb,
    )
    return second_block(
        x, norm_w_2, w_in_2, conv_w_2, dn_a_log_2, dn_dt_bias_2, dn_norm_w_2, q_norm_w_2,
        k_norm_w_2, w_branch_dn_2, w_branch_swa_2, w_out_2,
    )


_drawn_inputs = setup_inputs


def setup_inputs(seed=0):
    import zlib

    import numpy as np

    out = dict(_drawn_inputs(seed))
    spreads = {}
    factors = {'ctx': 2.836,
     'a_q_gain': 8.0,
     'a_k_gain': 8.0,
     'a_sink': 8.0,
     'b_v_gain': 7.67,
     'b_bias': 3.44,
     'c_scale': 2.851,
     'd_q_gain': 8.0,
     'd_k_gain': 8.0,
     'd_rpb': 8.0,
     'norm_w_2': 5.685,
     'dn_dt_bias_2': 8.0,
     'dn_norm_w_2': 8.0,
     'q_norm_w_2': 8.0,
     'k_norm_w_2': 8.0}
    for name, (base, spread) in spreads.items():
        noise = np.random.default_rng([zlib.crc32(name.encode()), seed]).standard_normal(out[name].shape)
        drawn = base * np.exp(spread * noise) if base else spread * noise
        out[name] = jnp.asarray(drawn.astype(out[name].dtype))
    for name, factor in factors.items():
        out[name] = (out[name] * factor).astype(out[name].dtype)
    return out
```

```python
import concourse.bass as bass
from concourse import mybir
import numpy as np
from contextlib import ExitStack

P = 128
D = 1024
KD = D // P
TX, TC = 512, 256
T = TX + TC
DFF = 2816
NJ = DFF // P
JA = 11
JB = NJ - JA
EPS = 1e-6
NEG = -1e30
NMOD = 9
WMAX = max(JA, NJ - JA) * P
NBA = 8


class Steps:

    def __init__(self, sem, names, before=0):
        self.sem, self.names, self.before = sem, list(names), before

    def at(self, turn, name):
        return self.before + turn * len(self.names) + self.names.index(name) + 1


class Stage:

    def __init__(self, name, tiles, chunks, tokens):
        self.name, self.tiles, self.chunks, self.tokens = name, tiles, chunks, tokens


def plan():
    stages = []
    for f in range(4):
        tok = T if f < 3 else TX
        ffn = [Stage(f"ffn{f}_up_a", 2 * JA, KD, tok), Stage(f"ffn{f}_down_a", KD, JA, tok),
               Stage(f"ffn{f}_up_b", 2 * JB, KD, tok), Stage(f"ffn{f}_down_b", KD, JB, tok)]
        stages += ffn
        if f == 0:
            stages += [Stage("ev_in", 15, KD, T), Stage("ev_out", 8, KD, T)]
        if f == 2:
            stages += [Stage("od_in_x", 8, KD, TX), Stage("od_in_kv", 8, KD, T),
                       Stage("od_out", 8, KD, TX)]
    stages += [Stage("dn_in", 12, KD, TX), Stage("dn_z", 4, KD, TX)]
    stages += [Stage(f"swa{h}_in", 9, KD, TX) for h in range(4)]
    stages += [Stage("swa_z", 4, KD, TX), Stage("gates", 16, KD, TX),
               Stage("br_dn", 8, 4, TX), Stage("br_swa", 8, 4, TX), Stage("out", 8, KD, TX)]
    n = 0
    for s in stages:
        s.first = n
        n += s.tiles
    return stages


def build(nc, t):
    f32, f32r = mybir.dt.float32, mybir.dt.float32r
    ALU, ACT, AX = mybir.AluOpType, mybir.ActivationFunctionType, mybir.AxisListType
    STAGES = plan()
    ST = {s.name: s for s in STAGES}
    NTILES = STAGES[-1].first + STAGES[-1].tiles
    STAGE_OF = [s for s in STAGES for _ in range(s.tiles)]

    ctx = ExitStack()
    with ctx:
        place = {"at": (nc.sbuf_base + 63) // 64 * 64}

        def region(size):
            a = place["at"]
            place["at"] = a + (size + 63) // 64 * 64
            return a

        def sb(name, at, shape, dt=f32):
            return nc.alloc_sbuf_tensor_at(name, [P] + list(shape), dt, offset=at)

        def words(*shape):
            return 4 * int(np.prod(shape))

        H_AT = region(words(KD, T))
        ZH_AT = region(words(KD, T))
        ZL_AT = region(words(KD, T))
        RAW_AT = region(words(4, WMAX))
        WH_AT = region(words(2, WMAX))
        WL_AT = region(words(2, WMAX))
        R_SIZE = 24 * words(T)
        R_AT = region(R_SIZE)
        SCR_AT = region(words(4, T))

        def small(name, shape, dt=f32):
            return sb(name, region(words(*shape)), shape, dt)

        h = sb("h", H_AT, [KD, T])
        zh = sb("zh", ZH_AT, [KD, T], f32r)
        zl = sb("zl", ZL_AT, [KD, T], f32r)
        raw = sb("raw", RAW_AT, [4, WMAX])
        wh = sb("wh", WH_AT, [2, WMAX], f32r)
        wl = sb("wl", WL_AT, [2, WMAX], f32r)
        scr = sb("scr", SCR_AT, [4, T])
        ident = small("ident", [P])
        ones = small("ones", [P])
        ones_blk = small("ones_blk", [P])
        perm_a = small("perm_a", [P])
        perm_b = small("perm_b", [P])
        mod = small("mod", [2, NMOD, KD, 2])
        amul = small("amul", [2, 3, KD, 2])
        ngain = small("ngain", [2, 3, KD])
        eps_c = small("eps_c", [4])
        scc = small("scc", [KD, 2])
        csc = small("csc", [KD, 2])
        cols = small("cols", [64])
        nmx = small("nmx", [4])
        rsum = small("rsum", [4])
        esink = small("esink", [4])
        rinv = small("rinv", [4])
        dncol = small("dncol", [12, 16])
        psum = ctx.enter_context(nc.psum_tensor("psum", [P, 4096], f32))
        assert place["at"] <= nc.sbuf_usable_end, place["at"]

        AQ, AK, BV, DQ, DK, CS, NW2, DNW, QN, KN, SINK = 0, 1, 2, 6, 7, 8, 12, 20, 21, 24, 27

        hidh = sb("hidh", R_AT, [JA, T], f32r)
        hidl = sb("hidl", R_AT + words(JA, T), [JA, T], f32r)
        adaw = sb("adaw", R_AT, [4, KD, 512])
        xin = sb("xin", ZH_AT, [6, D])
        adarow = sb("adarow", SCR_AT, [2, 512])
        adab = sb("adab", SCR_AT + words(2, 512), [2, NMOD * KD])
        ev = sb("ev", R_AT, [15, T])
        e2 = R_AT + words(15, T)
        vdup = sb("vdup", e2, [6, 2, 2, 64])
        wst = sb("wst", e2 + words(6, 256), [8, P])
        bbias = sb("bbias", e2 + words(6, 256) + words(8, P), [4, P])
        e3 = e2 + words(6, 256) + words(8, P) + words(4, P)
        ropea = sb("ropea", e3, [2, TX])
        vvt = sb("vvt", e3, [6, 512])
        assert e3 + words(6, 512) <= R_AT + R_SIZE
        ev_s = sb("ev_s", R_AT + words(7, T), [2, 640])
        ev_pt = sb("ev_pt", R_AT + words(7, T) + words(2, 640), [2, 640])
        ev_mask = sb("ev_mask", R_AT + words(7, T) + words(4, 640), [640])
        ox = sb("ox", R_AT, [8, TX])
        okv = sb("okv", R_AT + words(8, TX), [8, T])
        o2 = R_AT + words(8, TX) + words(8, T)
        ovt = sb("ovt", o2, [6, 512])
        nbias = sb("nbias", o2 + words(6, 512), [2, 1024])
        o3 = o2 + words(6, 512) + words(2, 1024)
        od_s = sb("od_s", o3, [2, T])
        od_pt = sb("od_pt", o3 + words(2, T), [2, T])
        assert o3 + words(4, T) <= R_AT + R_SIZE
        PADP = TX + 16
        pa = sb("pa", o3, [3, PADP])
        pcnt = sb("pcnt", SCR_AT, [4, TX])
        wpool = sb("wpool", o3 + words(3, PADP), [4, P])
        ptmp = sb("ptmp", SCR_AT + words(4, TX), [2, TX])
        assert 3 * PADP + 4 * P <= 4 * T
        DW = TX + 4
        dn = sb("dn", R_AT, [12, DW])
        d2 = R_AT + words(12, DW)
        dz = sb("dz", d2, [4, TX])
        d3 = d2 + words(4, TX)
        names = ["vb", "kbe", "ke", "et", "lt", "at_", "tt", "uu", "xx", "uc", "wt", "vn", "qe"]
        dnb = {}
        for i, n_ in enumerate(names):
            dnb[n_] = sb("dn_" + n_, d3 + words(i, 512), [4, P])
        d4 = d3 + words(len(names), 512)
        state = sb("state", d4, [3, 4, P])
        d5 = d4 + words(3, 512)
        assert d5 <= R_AT + R_SIZE, (d5 - R_AT)
        dmask = sb("dmask", SCR_AT, [9, P])
        wconv = sb("wconv", SCR_AT + words(9, P), [12, 4])
        wba = sb("wba", SCR_AT + words(9, P) + words(48), [KD, NBA])
        wbah = sb("wbah", SCR_AT + words(9, P) + words(48 + 64), [KD, NBA], f32r)
        wbal = sb("wbal", SCR_AT + words(9, P) + words(48 + 128), [KD, NBA], f32r)
        cacc = sb("cacc", SCR_AT + words(9, P) + words(48 + 192), [2, TX])
        assert 9 * P + 240 + 1024 <= 4 * T
        dsq = sb("dsq", d3, [2, TX])
        drr = sb("drr", d3 + words(2, TX), [2, TX])
        odnh = sb("odnh", R_AT, [4, TX], f32r)
        odnl = sb("odnl", R_AT + words(4, TX), [4, TX], f32r)
        dno = sb("dno", R_AT + words(8, DW), [4, TX])
        sw = R_AT + words(8, TX)
        sx = sb("sx", sw, [9, TX])
        s2 = sw + words(9, TX)
        svt = sb("svt", s2, [3, 4, P])
        sw_s = sb("sw_s", s2 + words(12, P), [2, 1280])
        sw_pt = sb("sw_pt", s2 + words(12, P) + words(2, 1280), [2, 1280])
        s3 = s2 + words(12, P) + words(4, 1280)
        oswa = sb("oswa", s3, [4, TX])
        assert s3 + words(4, TX) <= R_AT + R_SIZE
        smask = sb("smask", SCR_AT, [10, P])
        ropeb = sb("ropeb", SCR_AT + words(10, P), [2, TX])
        osh = sb("osh", sw, [4, TX], f32r)
        osl = sb("osl", sw + words(4, TX), [4, TX], f32r)
        gt = sb("gt", sw + words(8, TX), [16, TX])
        outb = sb("outb", sw, [2, D])
        szt = sb("szt", s2 + words(12, P), [4, TX])

        made = {}

        def S(name):
            if name not in made:
                made[name] = ctx.enter_context(nc.semaphore(name))
            return made[name]

        raw_loaded = [S(f"raw_loaded{c}") for c in range(4)]
        w_hi, w_lo, tile_done, drained = S("w_hi"), S("w_lo"), S("tile_done"), S("drained")

        def raw_free(n):
            return n + 1

        def lo_ready(n):
            return n + 5

        def w_slot_free(n):
            return n + 1

        def sum_ready(n):
            return n + 3

        def psum_free(n):
            return n + 1

        def all_drained(stage):
            return stage.first + stage.tiles + 4

        def acc(n, tokens):
            c = n % 4
            return psum[:, c * 1024:c * 1024 + tokens]

        def segs(tokens):
            return [(0, TX)] if tokens == TX else [(0, TX), (TX, T)]

        def load_tiles(sp, stage, src):
            b = stage.first
            w = stage.chunks * P

            def one(n, row):
                sp.wait_ge(w_lo, raw_free(n["v"]))
                sp.dma_start(raw[:, n["c"], 0:w], row).then_inc(raw_loaded[n["c"]], 16)

            loops = (stage.tiles - 1) // 4 if stage.tiles >= 12 else 0
            if loops:
                with sp.Fori(0, loops) as i:
                    for c in range(4):
                        one({"v": i * 4 + (b + c), "c": (b + c) % 4},
                            src[bass.ds(i * 4 + c, 1)].rearrange("a p n -> (a p) n"))
            for k in range(4 * loops, stage.tiles):
                one({"v": b + k, "c": (b + k) % 4}, src[k])

        def run_tiles(eng, stage, one):
            b = stage.first
            loops = (stage.tiles - 1) // 4 if stage.tiles >= 12 else 0
            if loops:
                with eng.Fori(0, loops) as i:
                    for c in range(4):
                        one(i * 4 + (b + c), i * 4 + c, b + c, i)
            for k in range(4 * loops, stage.tiles):
                one(b + k, k, b + k, None)

        def split_hi(act, n, c, i):
            if i is None:
                if n >= NTILES:
                    return
                w = STAGE_OF[n].chunks * P
                turn = n // 4
            else:
                w = STAGE_OF[c].chunks * P
                turn = i + c // 4
            act.wait_ge(raw_loaded[c % 4], turn * 16 + 16)
            act.wait_ge(tile_done, w_slot_free(n))
            nc.scalar.activation(wh[:, c % 2, 0:w], raw[:, c % 4, 0:w], ACT.Copy).then_inc(w_hi, 1)

        def split_lo(dve, n, c, i):
            if i is None and n >= NTILES:
                return
            w = STAGE_OF[c if i is not None else n].chunks * P
            dve.wait_ge(w_hi, n + 1)
            nc.vector.tensor_tensor(wl[:, c % 2, 0:w], raw[:, c % 4, 0:w], wh[:, c % 2, 0:w],
                                    ALU.subtract).then_inc(w_lo, 1)

        def products(pe, stage, xh, xl, after=None):
            def one(n, k, c, i):
                pe.wait_ge(w_lo, lo_ready(n))
                pe.wait_ge(drained, psum_free(n))
                for q in range(stage.chunks):
                    if after and i is None and n == stage.first:
                        after(q)
                    for j, (w, x) in enumerate(((wh, xh), (wh, xl), (wl, xh))):
                        for s, e in segs(stage.tokens):
                            last = nc.tensor.matmul(
                                psum[:, (c % 4) * 1024 + s:(c % 4) * 1024 + e],
                                w[:, c % 2, q * P:(q + 1) * P], x[:, q, s:e],
                                start=(q == 0 and j == 0), stop=(q == stage.chunks - 1 and j == 2))
                last.then_inc(tile_done, 1)
            run_tiles(pe, stage, one)

        def act_tiles(act, stage, use=None):
            def one(n, k, c, i):
                split_hi(act, n + 1, c + 1, i)
                if use:
                    use(n, k, c, i)
            run_tiles(act, stage, one)

        def dve_tiles(dve, stage, use):
            def one(n, k, c, i):
                split_lo(dve, n + 1, c + 1, i)
                use(n, k, c, i)
            run_tiles(dve, stage, one)

        def drain_to(dve, stage, dst, lead=0):
            def use(n, k, c, i):
                dve.wait_ge(tile_done, sum_ready(n))
                o = dst[:, bass.ds(k, 1), lead:lead + stage.tokens] if i is not None else \
                    dst[:, k:k + 1, lead:lead + stage.tokens]
                a = psum[:, (c % 4) * 1024:(c % 4) * 1024 + stage.tokens].rearrange("p (a n) -> p a n", a=1)
                nc.vector.tensor_copy(o, a).then_inc(drained, 1)
            dve_tiles(dve, stage, use)

        def drain_residual(dve, stage, gate):
            def use(n, k, c, i):
                dve.wait_ge(tile_done, sum_ready(n))
                for g, (s, e) in enumerate(segs(stage.tokens)):
                    a = psum[:, (c % 4) * 1024 + s:(c % 4) * 1024 + e]
                    col = gate(k, g)
                    if col is None:
                        last = nc.vector.tensor_tensor(h[:, k, s:e], a, h[:, k, s:e], ALU.add)
                    else:
                        last = nc.vector.scalar_tensor_tensor(h[:, k, s:e], a, col, h[:, k, s:e],
                                                              ALU.mult, ALU.add)
                last.then_inc(drained, 1)
            dve_tiles(dve, stage, use)

        n_sq, n_sum, n_sd, n_r, n_t, n_zf, n_hi, n_z = [S(x) for x in
            ("norm_sq", "norm_sum", "norm_sd", "norm_r", "norm_t", "norm_zf", "norm_hi", "norm_z")]
        NPS = 3 * 1024

        def norm_pe(pe, k, tokens):
            for c in range(KD):
                pe.wait_ge(n_sq, KD * k + c + 1)
                for s, e in segs(tokens):
                    last = nc.tensor.matmul(psum[:, NPS + s:NPS + e], ones[:], scr[:, c % 2, s:e],
                                            start=c == 0, stop=c == KD - 1)
                last.then_inc(n_sum, 1)

        def norm_act(act, k, tokens, scale, bias):
            for c in range(KD):
                if c >= 2:
                    act.wait_ge(n_sum, KD * k + c - 1)
                nc.scalar.activation(scr[:, c % 2, 0:tokens], h[:, c, 0:tokens], ACT.Square)\
                    .then_inc(n_sq, 1)
            act.wait_ge(n_sum, KD * (k + 1))
            nc.scalar.activation(scr[:, 2, 0:tokens], psum[:, NPS:NPS + tokens], ACT.Sqrt,
                                 bias=eps_c[:, 0:1], scale=1.0 / D).then_inc(n_sd, 1)
            for c in range(KD):
                act.wait_ge(n_t, KD * k + c + 1)
                for g, (s, e) in enumerate(segs(tokens)):
                    last = nc.scalar.activation(scr[:, c % 2, s:e], scr[:, c % 2, s:e], ACT.Identity,
                                                bias=bias(c, g), scale=scale(c, g))
                last.then_inc(n_zf, 1)

        def norm_dve(dve, k, tokens):
            dve.wait_ge(n_sd, k + 1)
            nc.vector.reciprocal(scr[:, 3, 0:tokens], scr[:, 2, 0:tokens]).then_inc(n_r, 1)
            dve.wait_ge(n_r, k + 1)

            def scaled(c):
                nc.vector.tensor_tensor(scr[:, c % 2, 0:tokens], h[:, c, 0:tokens],
                                        scr[:, 3, 0:tokens], ALU.mult).then_inc(n_t, 1)
            scaled(0)
            scaled(1)
            for c in range(KD):
                dve.wait_ge(n_zf, KD * k + c + 1)
                nc.vector.tensor_copy(zh[:, c, 0:tokens], scr[:, c % 2, 0:tokens]).then_inc(n_hi, 1)
                dve.wait_ge(n_hi, KD * k + c + 1)
                nc.vector.tensor_tensor(zl[:, c, 0:tokens], scr[:, c % 2, 0:tokens],
                                        zh[:, c, 0:tokens], ALU.subtract).then_inc(n_z, 1)
                if c + 2 < KD:
                    dve.wait_ge(n_z, KD * k + c + 1)
                    scaled(c + 2)

        def after_norm(pe, k):
            return lambda q: pe.wait_ge(n_z, KD * k + q + 1)

        silu_done, hid_hi, hid_done = S("silu_done"), S("hid_hi"), S("hid_done")
        NORM_OF_FFN = [0, 2, 3, 5]
        NORM_OF_MIX = {0: 1, 1: 4}

        def modcol(layer, kind):
            return lambda c, g: mod[:, layer, kind, c, g:g + 1]

        def mulcol(layer, s):
            return lambda c, g: amul[:, layer, s, c, g:g + 1]

        def ffn_parts(f):
            return [(ST[f"ffn{f}_up_a"], ST[f"ffn{f}_down_a"], f * NJ),
                    (ST[f"ffn{f}_up_b"], ST[f"ffn{f}_down_b"], f * NJ + JA)]

        def ffn_sp(sp, f):
            for (up, down, _), (u, d) in zip(ffn_parts(f), (("wup_a", "wdn_a"), ("wup_b", "wdn_b"))):
                load_tiles(sp, up, t[u][f])
                load_tiles(sp, down, t[d][f])

        def ffn_pe(pe, f):
            k = NORM_OF_FFN[f]
            norm_pe(pe, k, ffn_parts(f)[0][0].tokens)
            pe.wait_ge(n_z, KD * (k + 1))
            for up, down, pairs in ffn_parts(f):
                products(pe, up, zh, zl)
                pe.wait_ge(hid_done, pairs + up.tiles // 2)
                products(pe, down, hidh, hidl)

        def ffn_act(act, f):
            k, layer, s = NORM_OF_FFN[f], f // 2, 2 * (f % 2)
            tok = ffn_parts(f)[0][0].tokens
            act.wait_ge(drained, ST[f"ffn{f}_up_a"].first + 4)
            norm_act(act, k, tok, mulcol(layer, s), modcol(layer, 3 * s))
            for up, down, pairs in ffn_parts(f):
                def silu(n, j, c, i):
                    if (c - up.first) % 2 == 0:
                        act.wait_ge(tile_done, sum_ready(n))
                        nc.scalar.activation(scr[:, (c - up.first) // 2 % 2, 0:tok], acc(c, tok),
                                             ACT.Silu).then_inc(silu_done, 1)
                act_tiles(act, up, silu)
                act_tiles(act, down)

        def ffn_dve(dve, f):
            k, layer, s = NORM_OF_FFN[f], f // 2, 2 * (f % 2)
            tok = ffn_parts(f)[0][0].tokens
            norm_dve(dve, k, tok)
            for up, down, pairs in ffn_parts(f):
                def hidden(n, j, c, i):
                    if (c - up.first) % 2 == 0:
                        return
                    b = (c - up.first) // 2 % 2
                    if i is None:
                        pair, jj = pairs + j // 2, j // 2
                        oh, ol = hidh[:, jj:jj + 1, 0:tok], hidl[:, jj:jj + 1, 0:tok]
                    else:
                        jj = i * 2 + (c - up.first) // 2
                        pair = i * 2 + (pairs + (c - up.first) // 2)
                        oh, ol = hidh[:, bass.ds(jj, 1), 0:tok], hidl[:, bass.ds(jj, 1), 0:tok]
                    p = scr[:, 2 + b:3 + b, 0:tok]
                    dve.wait_ge(tile_done, sum_ready(n))
                    dve.wait_ge(silu_done, pair + 1)
                    nc.vector.tensor_tensor(p, scr[:, b:b + 1, 0:tok],
                                            acc(c, tok).rearrange("p (a n) -> p a n", a=1),
                                            ALU.mult).then_inc(drained, 2)
                    dve.wait_ge(drained, n + 5)
                    nc.vector.tensor_copy(oh, p).then_inc(hid_hi, 1)
                    dve.wait_ge(hid_hi, pair + 1)
                    nc.vector.tensor_tensor(ol, p, oh, ALU.subtract).then_inc(hid_done, 1)
                dve_tiles(dve, up, hidden)
                drain_residual(dve, down, lambda c, g: mod[:, layer, 3 * s + 2, c, g:g + 1])

        def bc(ap, shape):
            return ap.unsqueeze(2).to_broadcast(shape)

        def mid(ap, n):
            return ap.unsqueeze(1).to_broadcast([P, n, ap.shape[-1]])

        chain = {}

        def link(eng, name, ins):
            chain[name] = chain.get(name, 0) + 1
            ins.then_inc(S(name + "_chain"), 1)
            eng.wait_ge(S(name + "_chain"), chain[name])

        consts, misc = S("consts_loaded"), S("x_loaded")
        const_loads = [(ident, "c_ident"), (ones, "c_ones"), (ones_blk, "c_ones_blk"), (perm_a, "c_perm_a"),
                       (perm_b, "c_perm_b"), (eps_c, "c_eps"), (ngain, "ngain"), (csc, "csc"),
                       (cols, "cols"), (adab, "adab")]
        ada_in = [S(f"ada_loaded{c}") for c in range(4)]
        ada_sum, ada_row, ada_tr, mod_done, silu_c = [S(x) for x in
            ("ada_sum", "ada_row", "ada_tr", "mod_done", "silu_c")]
        x_tr, x_cp = S("x_transposed"), S("x_copied")
        NADA = 2 * NMOD * D // 512
        MT = 2048

        def start_sp(sp):
            for i in range(NADA):
                if i >= 4:
                    sp.wait_ge(ada_sum, i - 3)
                sp.dma_start(adaw[:, i % 4], t["ada_w"][i]).then_inc(ada_in[i % 4], 16)

        def start_pool(pool):
            for dst, src in const_loads:
                pool.dma_start(dst[:], t[src]).then_inc(consts, 16)
            pool.dma_start(xin[:], t["xin"]).then_inc(misc, 16)

        def wait_consts(eng):
            eng.wait_ge(consts, 16 * len(const_loads))

        def start_pe(pe):
            wait_consts(pe)
            pe.wait_ge(misc, 16)
            for a in range(6):
                if a >= 1:
                    pe.wait_ge(x_cp, a)
                for c in range(KD):
                    last = nc.tensor.transpose(psum[:, 3072 + c * P:3072 + (c + 1) * P],
                                               xin[:, a, c * P:(c + 1) * P], ident[:])
                last.then_inc(x_tr, 1)
            pe.wait_ge(silu_c, 1)
            for i in range(NADA + 1):
                if i < NADA:
                    pe.wait_ge(ada_in[i % 4], 16 * (i // 4 + 1))
                    if i >= 4:
                        pe.wait_ge(ada_row, i - 3)
                    for c in range(KD):
                        last = nc.tensor.matmul(psum[0:2, i % 4 * 512:i % 4 * 512 + 512], scc[:, c, :],
                                                adaw[:, i % 4, c, :], start=c == 0, stop=c == KD - 1)
                    last.then_inc(ada_sum, 1)
                if i >= 1:
                    pe.wait_ge(ada_row, i)
                    for j in range(4):
                        m = MT + ((i - 1) * 4 + j) * 2
                        last = nc.tensor.transpose(psum[:, m:m + 2], adarow[0:2, (i - 1) % 2, j * P:(j + 1) * P],
                                                   ident[0:2, 0:2])
                    last.then_inc(ada_tr, 1)

        def start_act(act):
            wait_consts(act)
            nc.scalar.activation(scc[:], csc[:], ACT.Silu).then_inc(silu_c, 1)
            for i in range(NADA):
                act.wait_ge(ada_sum, i + 1)
                if i >= 2:
                    act.wait_ge(ada_tr, i - 1)
                nc.scalar.activation(adarow[0:2, i % 2, :], psum[0:2, i % 4 * 512:i % 4 * 512 + 512],
                                     ACT.Copy).then_inc(ada_row, 1)

        def start_dve(dve):
            for a in range(6):
                dve.wait_ge(x_tr, a + 1)
                nc.vector.tensor_copy(h[:, :, a * P:(a + 1) * P],
                                      psum[:, 3072:4096].rearrange("p (c n) -> p c n", c=KD))\
                    .then_inc(x_cp, 1)
            wait_consts(dve)
            dve.wait_ge(ada_tr, NADA)
            for layer in range(2):
                n = NMOD * KD
                link(dve, "dve", nc.vector.tensor_tensor(
                    mod[:, layer].rearrange("p k c g -> p (k c) g"),
                    psum[:, MT + layer * 2 * n:MT + (layer + 1) * 2 * n].rearrange("p (n g) -> p n g", g=2),
                    bc(adab[:, layer, :], [P, n, 2]), ALU.add))
            for layer in range(2):
                for s in range(3):
                    nc.vector.scalar_tensor_tensor(amul[:, layer, s], mod[:, layer, 3 * s + 1], 1.0,
                                                   bc(ngain[:, layer, s, :], [P, KD, 2]), ALU.add, ALU.mult)
                    if s != 1:
                        nc.vector.tensor_scalar(mod[:, layer, 3 * s + 2], mod[:, layer, 3 * s + 2], 0.5,
                                                None, ALU.mult)
            link(dve, "dve", nc.vector.tensor_copy(nmx[:, 0:1], eps_c[:, 0:1]))
            nc.vector.tensor_copy(nmx[:, 0:1], eps_c[:, 0:1]).then_inc(mod_done, 1)

        hn_sq, hn_mm, hn_sd, hn_r, hn_n, hn_rot, hn_tmp, hn_f = [S("head_" + x) for x in
            ("sq", "sum", "sd", "r", "normed", "rotated", "rot_parts", "roped")]

        class Item:

            def __init__(self, src, tokens, ones, scale, gain, rope):
                self.src, self.tokens, self.ones, self.scale = src, tokens, ones, scale
                self.gain, self.rope = gain, rope

        groups, counts = {}, {"k": 0, "r": 0}

        def group(name, items, sq, rr):
            for it in items:
                it.k, it.r = counts["k"], counts["r"]
                counts["k"] += 1
                counts["r"] += it.rope is not None
                it.sq, it.rr = sq, rr
            groups[name] = items

        HROT = 2048

        def heads_pe(pe, name):
            items = groups[name]

            def rotate(it):
                if it.rope is None:
                    return
                pe.wait_ge(hn_n, it.k + 1)
                if it.r >= 2:
                    pe.wait_ge(hn_tmp, it.r - 1)
                nc.tensor.matmul(psum[:, HROT + it.r % 2 * 512:HROT + it.r % 2 * 512 + TX], it.rope[0][:],
                                 it.src[:, 0:TX], start=True, stop=True).then_inc(hn_rot, 1)

            for i, it in enumerate(items):
                pe.wait_ge(hn_sq, it.k + 1)
                if i >= 2:
                    pe.wait_ge(hn_sd, it.k - 1)
                for s, e in segs(it.tokens):
                    last = nc.tensor.matmul(psum[:, it.k % 2 * 1024 + s:it.k % 2 * 1024 + e], it.ones[:],
                                            it.sq[:, it.k % 2, s:e], start=True, stop=True)
                last.then_inc(hn_mm, 1)
                if i >= 1:
                    rotate(items[i - 1])
            rotate(items[-1])

        def heads_act(act, name):
            items = groups[name]

            def square(it):
                if it.k >= items[0].k + 2:
                    act.wait_ge(hn_mm, it.k - 1)
                nc.scalar.activation(it.sq[:, it.k % 2, 0:it.tokens], it.src, ACT.Square).then_inc(hn_sq, 1)
            square(items[0])
            for i, it in enumerate(items):
                if i + 1 < len(items):
                    square(items[i + 1])
                act.wait_ge(hn_mm, it.k + 1)
                if i >= 2:
                    act.wait_ge(hn_n, it.k - 1)
                    j = items[i - 2]
                    if j.rope is not None:
                        act.wait_ge(hn_f, j.r + 1)
                nc.scalar.activation(it.rr[:, it.k % 2, 0:it.tokens],
                                     psum[:, it.k % 2 * 1024:it.k % 2 * 1024 + it.tokens], ACT.Sqrt,
                                     bias=eps_c[:, 0:1], scale=it.scale).then_inc(hn_sd, 1)

        def heads_dve(dve, name):
            items = groups[name]

            def norm(it):
                rr = it.rr[:, it.k % 2, 0:it.tokens]
                dve.wait_ge(hn_sd, it.k + 1)
                nc.vector.reciprocal(rr, rr).then_inc(hn_r, 1)
                dve.wait_ge(hn_r, it.k + 1)
                nc.vector.scalar_tensor_tensor(it.src, it.src, it.gain, rr, ALU.mult, ALU.mult)\
                    .then_inc(hn_n, 1)

            def rope(it):
                if it.rope is None:
                    return
                _, cos, sin = it.rope
                x, part = it.src[:, 0:TX], it.rr[:, it.k % 2, 0:TX]
                dve.wait_ge(hn_rot, it.r + 1)
                nc.vector.tensor_tensor(part, psum[:, HROT + it.r % 2 * 512:HROT + it.r % 2 * 512 + TX],
                                        sin, ALU.mult).then_inc(hn_tmp, 1)
                link(dve, "dve", nc.vector.tensor_tensor(x, x, cos, ALU.mult))
                dve.wait_ge(hn_tmp, it.r + 1)
                nc.vector.tensor_tensor(x, x, part, ALU.add).then_inc(hn_f, 1)

            for i, it in enumerate(items):
                norm(it)
                if i >= 1:
                    rope(items[i - 1])
            rope(items[-1])

        def after_heads(eng, name):
            it = groups[name][-1]
            eng.wait_ge(hn_n, it.k + 1)
            if it.r + (it.rope is not None):
                eng.wait_ge(hn_f, it.r + (it.rope is not None))

        scr_sq, scr_rr = scr[:, 0:2, :], scr[:, 2:4, :]
        rope_a = (perm_a, ropea[:, 0, :], ropea[:, 1, :])
        group("even", [Item(ev[:, m, :], T, ones_blk, 1.0 / 64, cols[:, (AQ if m < 4 else AK):(AQ if m < 4 else AK) + 1],
                            rope_a) for m in range(6)] +
              [Item(ev[:, 11 + m, :], T, ones_blk, 1.0 / 64, cols[:, BV + m:BV + m + 1], None)
               for m in range(4)], scr_sq, scr_rr)
        group("odd", [Item(ox[:, 4 + m, :], TX, ones_blk, 1.0 / 64, cols[:, DQ:DQ + 1], None) for m in range(4)] +
              [Item(okv[:, m, :], T, ones_blk, 1.0 / 64, cols[:, DK:DK + 1], None) for m in range(4)],
              scr_sq, scr_rr)
        group("dn_qk", [Item(dn[:, m, 4:DW], TX, ones, 1.0, (float(P) ** -0.5 if m < 4 else 1.0), None)
                        for m in range(8)], dsq, drr)
        group("dn_o", [Item(dn[:, m, 4:DW], TX, ones, 1.0 / P, cols[:, DNW:DNW + 1], None)
                       for m in range(4)], dsq, drr)
        rope_b = (perm_b, ropeb[:, 0, :], ropeb[:, 1, :])
        for hd in range(4):
            group(f"swa{hd}", [Item(sx[:, m, :], TX, ones, 1.0 / P,
                                    cols[:, (QN if m < 3 else KN) + m % 3:(QN if m < 3 else KN) + m % 3 + 1],
                                    rope_b) for m in range(6)],
                  sw_s[:, :, 0:TX], sw_pt[:, :, 0:TX])

        at_qk, at_s, at_e, at_p, at_t, at_pc, at_pv, at_hi, at_o = [S("att_" + x) for x in
            ("scores", "scores_read", "exp", "probs", "transposed", "probs_t", "pv", "out_hi", "out")]
        PT0, O0 = 1536, 3072

        class Unit:

            def __init__(self, keys, segs, vals, out, scale, s, pt, c0=0, sink=None, before=None):
                self.keys, self.segs, self.vals, self.out, self.scale = keys, segs, vals, out, scale
                self.s, self.pt, self.c0, self.sink, self.before = s, pt, c0, sink, before

        units = {}
        total = {"u": 0}

        def add_units(name, us):
            for u in us:
                u.u = total["u"]
                total["u"] += 1
            units[name] = us

        def att_pe(pe, name):
            us = units[name]
            for i in range(len(us) + 2):
                if i < len(us):
                    u = us[i]
                    if i >= 1:
                        pe.wait_ge(at_s, u.u)
                    for q, k, c, w in u.keys:
                        last = nc.tensor.matmul(psum[:, c:c + w], q, k, start=True, stop=True)
                    last.then_inc(at_qk, 1)
                if 1 <= i <= len(us):
                    u = us[i - 1]
                    pe.wait_ge(at_p, u.u + 1)
                    if i >= 2:
                        pe.wait_ge(at_pc, u.u)
                    for j in range(len(u.vals)):
                        last = nc.tensor.transpose(psum[:, PT0 + j * P:PT0 + (j + 1) * P],
                                                   u.s[:, u.u % 2, u.c0 + j * P:u.c0 + (j + 1) * P], ident[:])
                    last.then_inc(at_t, 1)
                if i >= 2:
                    u = us[i - 2]
                    pe.wait_ge(at_pc, u.u + 1)
                    if i >= 4:
                        pe.wait_ge(at_o, u.u - 1)
                    for j, v in enumerate(u.vals):
                        last = nc.tensor.matmul(psum[:, O0 + u.u % 2 * 512:O0 + u.u % 2 * 512 + P], v,
                                                u.pt[:, u.u % 2, j * P:(j + 1) * P],
                                                start=j == 0, stop=j == len(u.vals) - 1)
                    last.then_inc(at_pv, 1)

        def att_act(act, name):
            us = units[name]
            for i in range(len(us) + 2):
                if i < len(us):
                    u = us[i]
                    w, k = len(u.vals) * P, u.u % 4
                    act.wait_ge(at_s, u.u + 1)
                    e = nc.scalar.activation(u.s[:, u.u % 2, u.c0:u.c0 + w], u.s[:, u.u % 2, u.c0:u.c0 + w],
                                             ACT.Exp, bias=nmx[:, k:k + 1], accum_out=rsum[:, k:k + 1])
                    if u.sink is not None:
                        e = nc.scalar.activation(esink[:, k:k + 1], u.sink, ACT.Exp, bias=nmx[:, k:k + 1])
                    e.then_inc(at_e, 1)
                if 1 <= i <= len(us):
                    u = us[i - 1]
                    act.wait_ge(at_t, u.u + 1)
                    if i >= 3:
                        act.wait_ge(at_pv, u.u - 1)
                    nc.scalar.activation(u.pt[:, u.u % 2, 0:len(u.vals) * P],
                                         psum[:, PT0:PT0 + len(u.vals) * P], ACT.Copy).then_inc(at_pc, 1)
                if i >= 2 and len(us[i - 2].out) == 3:
                    u = us[i - 2]
                    act.wait_ge(at_pv, u.u + 1)
                    r = u.out[0]
                    nc.scalar.activation(u.out[1], psum[r, O0 + u.u % 2 * 512:O0 + u.u % 2 * 512 + P],
                                         ACT.Copy).then_inc(at_hi, 1)

        def att_dve(dve, name, hi_before):
            us = units[name]
            for i in range(len(us) + 2):
                if i < len(us):
                    u = us[i]
                    w, k = len(u.vals) * P, u.u % 4
                    dve.wait_ge(at_qk, u.u + 1)
                    if i >= 2:
                        dve.wait_ge(at_t, u.u - 1)
                    if u.before:
                        u.before(dve)
                    for n, (c, cw, m) in enumerate(u.segs):
                        o = u.s[:, u.u % 2, c:c + cw]
                        if m is None:
                            ins = nc.vector.tensor_scalar(o, psum[:, c:c + cw], u.scale, None, ALU.mult)
                        else:
                            ins = nc.vector.scalar_tensor_tensor(o, psum[:, c:c + cw], u.scale, m,
                                                                 ALU.mult, ALU.add)
                    link(dve, "dve", ins)
                    link(dve, "dve", nc.vector.reduce_max(nmx[:, k:k + 1], u.s[:, u.u % 2, u.c0:u.c0 + w], AX.X))
                    if u.sink is not None:
                        nc.vector.tensor_scalar(nmx[:, k:k + 1], nmx[:, k:k + 1], u.sink, -1.0,
                                                ALU.max, ALU.mult).then_inc(at_s, 1)
                    else:
                        nc.vector.tensor_scalar(nmx[:, k:k + 1], nmx[:, k:k + 1], -1.0, None,
                                                ALU.mult).then_inc(at_s, 1)
                if 1 <= i <= len(us):
                    u = us[i - 1]
                    w, k = len(u.vals) * P, u.u % 4
                    dve.wait_ge(at_e, u.u + 1)
                    if u.sink is not None:
                        link(dve, "dve", nc.vector.tensor_tensor(rsum[:, k:k + 1], rsum[:, k:k + 1],
                                                                 esink[:, k:k + 1], ALU.add))
                    link(dve, "dve", nc.vector.reciprocal(rinv[:, k:k + 1], rsum[:, k:k + 1]))
                    nc.vector.tensor_scalar(u.s[:, u.u % 2, u.c0:u.c0 + w], u.s[:, u.u % 2, u.c0:u.c0 + w],
                                            rinv[:, k:k + 1], None, ALU.mult).then_inc(at_p, 1)
                if i >= 2:
                    u = us[i - 2]
                    r = u.out[0]
                    a = psum[r, O0 + u.u % 2 * 512:O0 + u.u % 2 * 512 + P]
                    if len(u.out) == 3:
                        dve.wait_ge(at_hi, hi_before + i - 1)
                        nc.vector.tensor_tensor(u.out[2], a, u.out[1], ALU.subtract).then_inc(at_o, 1)
                    else:
                        dve.wait_ge(at_pv, u.u + 1)
                        nc.vector.tensor_copy(u.out[1], a).then_inc(at_o, 1)

        ev_loaded, ev_mask_in = S("ev_loaded"), S("ev_mask_loaded")
        gelu_done, v_tr, v_cp = S("gelu_done"), S("v_transposed"), S("v_copied")
        vv_tr, vv_cp, mx_mm, mx_d, mx_hi, cat_lo = [S(x) for x in
            ("vv_transposed", "vv_copied", "mix_sum", "mix_done", "mix_hi", "mix_lo")]
        EI, EO = ST["ev_in"], ST["ev_out"]

        def even_pool(pool):
            pool.wait_ge(tile_done, sum_ready(EI.first - 1))
            pool.dma_start(ropea[:], t["c_ropea"]).then_inc(ev_loaded, 16)
            pool.dma_start(wst[:], t["wst"]).then_inc(ev_loaded, 16)
            pool.dma_start(bbias[:], t["bbias"]).then_inc(ev_loaded, 16)
            pool.wait_ge(cat_lo, 6)
            pool.dma_start(ev_mask[:], t["c_ev_mask"]).then_inc(ev_mask_in, 16)

        def ev_units():
            us = []
            for hd in range(8):
                r0 = hd % 2 * 64
                r = slice(r0, r0 + 64)
                g = hd // 4
                q, k = ev[r, hd // 2, :], ev[r, 4 + g, :]
                sink = cols[:, SINK + hd:SINK + hd + 1]

                def val(tile):
                    return vdup[:, tile, g].rearrange("p a d -> p (a d)")
                for n in range(6):
                    s = slice(n * P, (n + 1) * P)
                    out = (r, zh[r, hd // 2, s], zl[r, hd // 2, s])
                    if n < 4:
                        lo, c0 = max(n - 1, 0), (P if n == 0 else 0)
                        keys = [(q[:, s], k[:, lo * P:(n + 1) * P], c0, (n + 1 - lo) * P),
                                (q[:, s], k[:, TX:T], 256, 256)]
                        tiles = list(range(lo, n + 1)) + [4, 5]
                        if n < 3:
                            keys.append((q[:, s], k[:, (n + 1) * P:(n + 2) * P], 512, P))
                            tiles.append(n + 1)
                        w = len(tiles) * P
                        us.append(Unit(keys=keys, c0=c0, segs=[(c0, w, ev_mask[:, c0:c0 + w])],
                                            scale=0.125, vals=[val(x) for x in tiles], sink=sink,
                                            out=out, s=ev_s, pt=ev_pt))
                    else:
                        us.append(Unit(keys=[(q[:, s], k[:, TX:T], 0, 256)], segs=[(0, 256, None)],
                                            scale=0.125, vals=[val(4), val(5)], sink=sink, out=out,
                                            s=ev_s, pt=ev_pt))
            return us

        add_units("even", ev_units())
        NU_EVEN = total["u"]

        def even_pe(pe):
            norm_pe(pe, 1, T)
            pe.wait_ge(n_z, KD * 2)
            products(pe, EI, zh, zl)
            pe.wait_ge(drained, all_drained(EI))
            for a in range(6):
                last = nc.tensor.transpose(psum[:, 3072 + a * P:3072 + (a + 1) * P],
                                           ev[:, 6, a * P:(a + 1) * P], ident[:])
            last.then_inc(v_tr, 1)
            heads_pe(pe, "even")
            after_heads(pe, "even")
            for a in range(6):
                if a >= 2:
                    pe.wait_ge(vv_cp, a - 1)
                for m in range(4):
                    last = nc.tensor.transpose(psum[:, a % 2 * 512 + m * P:a % 2 * 512 + (m + 1) * P],
                                               ev[:, 11 + m, a * P:(a + 1) * P], ident[:])
                last.then_inc(vv_tr, 1)
            pe.wait_ge(ev_loaded, 48)
            for a in range(6):
                pe.wait_ge(vv_cp, a + 1)
                if a >= 2:
                    pe.wait_ge(mx_d, a - 1)
                for m in range(4):
                    last = nc.tensor.matmul(psum[:, 1024 + a % 2 * 1024 + m * 256:1024 + a % 2 * 1024 + (m + 1) * 256],
                                            vvt[:, a, m * P:(m + 1) * P],
                                            wst[:, 2 * m:2 * m + 2, :].rearrange("p a n -> p (a n)"),
                                            start=True, stop=True)
                last.then_inc(mx_mm, 1)
            pe.wait_ge(v_cp, 1)
            pe.wait_ge(mx_d, 6)
            att_pe(pe, "even")
            pe.wait_ge(at_o, NU_EVEN)
            pe.wait_ge(cat_lo, 6)
            products(pe, EO, zh, zl)

        def even_act(act):
            act.wait_ge(drained, EI.first + 4)
            norm_act(act, 1, T, mulcol(0, 1), modcol(0, 3))
            act_tiles(act, EI)
            act.wait_ge(drained, all_drained(EI))
            nc.scalar.activation(ev[:, 7:11, :], ev[:, 7:11, :], ACT.Gelu_apprx_tanh).then_inc(gelu_done, 1)
            nc.scalar.activation(ev[:, 11:15, :], ev[:, 11:15, :], ACT.Gelu_apprx_tanh).then_inc(gelu_done, 1)
            act.wait_ge(gelu_done, 2)
            heads_act(act, "even")
            for a in range(6):
                act.wait_ge(vv_tr, a + 1)
                nc.scalar.activation(vvt[:, a, :], psum[:, a % 2 * 512:a % 2 * 512 + 512], ACT.Copy)\
                    .then_inc(vv_cp, 1)
            for a in range(6):
                act.wait_ge(mx_d, a + 1)
                nc.scalar.activation(zh[:, 4:8, a * P:(a + 1) * P],
                                     scr[:, a % 2, 0:512].rearrange("p (m n) -> p m n", m=4), ACT.Copy)\
                    .then_inc(mx_hi, 1)
            att_act(act, "even")
            act_tiles(act, EO)

        def even_dve(dve):
            norm_dve(dve, 1, T)
            drain_to(dve, EI, ev)
            dve.wait_ge(v_tr, 1)
            for d in range(2):
                last = nc.vector.tensor_copy(vdup[:, :, :, d, :],
                                             psum[:, 3072:3072 + 768].rearrange("p (a g d) -> p a g d", a=6, g=2))
            last.then_inc(v_cp, 1)
            dve.wait_ge(ev_loaded, 48)
            heads_dve(dve, "even")
            dve.wait_ge(gelu_done, 2)
            for a in range(6):
                dve.wait_ge(mx_mm, a + 1)
                b = scr[:, a % 2, 0:512].rearrange("p (m n) -> p m n", m=4)
                mix = psum[:, 1024 + a % 2 * 1024:2048 + a % 2 * 1024].rearrange("p (m two n) -> p m two n", m=4, two=2)
                for g in range(2):
                    r = slice(64 * g, 64 * g + 64)
                    ins = nc.vector.tensor_tensor(b[r], mix[r, :, g, :], bbias[r], ALU.add)
                    link(dve, "dve", ins)
                nc.vector.tensor_tensor(b, b, ev[:, 7:11, a * P:(a + 1) * P], ALU.mult).then_inc(mx_d, 1)
                dve.wait_ge(mx_hi, a + 1)
                nc.vector.tensor_tensor(zl[:, 4:8, a * P:(a + 1) * P], b, zh[:, 4:8, a * P:(a + 1) * P],
                                        ALU.subtract).then_inc(cat_lo, 1)
            dve.wait_ge(ev_mask_in, 16)
            dve.wait_ge(cat_lo, 6)
            att_dve(dve, "even", 0)
            drain_residual(dve, EO, lambda c, g: mod[:, 0, 5, c, g:g + 1])

        OX, OKV, OO = ST["od_in_x"], ST["od_in_kv"], ST["od_out"]
        od_loaded = S("od_loaded")
        nb_in = [S("nb_loaded0"), S("nb_loaded1")]
        ovt_tr, ovt_cp, pool_in, pool_mm, pool_hi, pool_lo = [S(x) for x in
            ("odv_transposed", "odv_copied", "pooled", "pool_sum", "pool_hi", "pool_lo")]

        def od_units():
            us = []
            for hd in range(8):
                r = slice(hd % 2 * 64, hd % 2 * 64 + 64)
                m = hd // 2
                for n in range(4):
                    s = slice(n * P, (n + 1) * P)
                    q = ox[r, 4 + m, s]
                    off = (NA_R - 1 - 2 * n) * GW
                    before = None
                    if n == 0:
                        def before(dve, hd=hd):
                            dve.wait_ge(nb_in[hd % 2], 16 * (hd // 2 + 1))
                    us.append(Unit(keys=[(q, okv[r, m, 0:TX], 0, TX), (q, okv[r, m, TX:T], TX, TC)],
                                        segs=[(0, TX, nbias[:, hd % 2, off:off + TX]), (TX, TC, None)],
                                        scale=0.125, before=before, s=od_s, pt=od_pt,
                                        vals=[ovt[:, a, m * P:(m + 1) * P] for a in range(6)],
                                        out=(r, zh[r, 4 + m, s], zl[r, 4 + m, s])))
            return us

        GW, NA_R = 64, 8
        add_units("odd", od_units())
        NU_ODD = total["u"]

        def odd_pool(pool):
            pool.wait_ge(n_z, KD * 5)
            pool.wait_ge(tile_done, sum_ready(OX.first - 1))
            pool.dma_start(wpool[:], t["wpool"]).then_inc(od_loaded, 16)
            pool.dma_start(pcnt[:], t["c_pcnt"]).then_inc(od_loaded, 16)
            for hd in range(8):
                if hd >= 2:
                    pool.wait_ge(at_s, NU_EVEN + 4 * (hd - 1))
                pool.dma_start(nbias[:, hd % 2, :], t["nbias"][hd]).then_inc(nb_in[hd % 2], 16)

        def odd_pe(pe):
            norm_pe(pe, 4, T)
            pe.wait_ge(n_z, KD * 5)
            products(pe, OX, zh, zl)
            products(pe, OKV, zh, zl)
            pe.wait_ge(drained, all_drained(OKV))
            for a in range(6):
                if a >= 2:
                    pe.wait_ge(ovt_cp, a - 1)
                for m in range(4):
                    last = nc.tensor.transpose(psum[:, 3072 + a % 2 * 512 + m * P:3072 + a % 2 * 512 + (m + 1) * P],
                                               okv[:, 4 + m, a * P:(a + 1) * P], ident[:])
                last.then_inc(ovt_tr, 1)
            pe.wait_ge(od_loaded, 32)
            for g in range(4):
                pe.wait_ge(pool_in, g + 1)
                nc.tensor.matmul(psum[:, g * 512:g * 512 + TX], wpool[:, g, :], ptmp[:, g % 2, :],
                                 start=True, stop=True).then_inc(pool_mm, 1)
            pe.wait_ge(pool_lo, 4)
            heads_pe(pe, "odd")
            after_heads(pe, "odd")
            pe.wait_ge(ovt_cp, 6)
            att_pe(pe, "odd")
            pe.wait_ge(at_o, NU_ODD)
            products(pe, OO, zh, zl)

        def odd_act(act):
            act.wait_ge(drained, OX.first + 4)
            norm_act(act, 4, T, mulcol(1, 1), modcol(1, 3))
            act_tiles(act, OX)
            act_tiles(act, OKV)
            for g in range(4):
                act.wait_ge(pool_mm, g + 1)
                nc.scalar.activation(zh[:, g, 0:TX], psum[:, g * 512:g * 512 + TX], ACT.Copy,
                                     scale=cols[:, CS + g:CS + g + 1]).then_inc(pool_hi, 1)
            act.wait_ge(pool_lo, 4)
            heads_act(act, "odd")
            att_act(act, "odd")
            act_tiles(act, OO)

        def odd_dve(dve):
            norm_dve(dve, 4, T)
            drain_to(dve, OX, ox)
            drain_to(dve, OKV, okv)
            for a in range(6):
                dve.wait_ge(ovt_tr, a + 1)
                nc.vector.tensor_copy(ovt[:, a, :], psum[:, 3072 + a % 2 * 512:3072 + a % 2 * 512 + 512])\
                    .then_inc(ovt_cp, 1)
            dve.wait_ge(drained, all_drained(OKV))
            for j in range(3):
                link(dve, "dve", nc.vector.memset(pa[:, j, :], 0.0))
            dve.wait_ge(od_loaded, 32)

            def pool_out(g):
                dve.wait_ge(pool_hi, g + 1)
                nc.vector.scalar_tensor_tensor(zl[:, g, 0:TX], psum[:, g * 512:g * 512 + TX],
                                               cols[:, CS + g:CS + g + 1], zh[:, g, 0:TX],
                                               ALU.mult, ALU.subtract).then_inc(pool_lo, 1)
            for g in range(4):
                w = 2 << g
                link(dve, "dve", nc.vector.tensor_copy(pa[:, 0, 8:8 + TX], ox[:, g, :]))
                src, n = 0, PADP
                for level in range(g + 1):
                    dst = 1 + level % 2
                    n -= 1 << level
                    link(dve, "dve", nc.vector.tensor_tensor(pa[:, dst, 0:n], pa[:, src, 0:n],
                                                             pa[:, src, (1 << level):(1 << level) + n], ALU.add))
                    src = dst
                if g >= 2:
                    dve.wait_ge(pool_mm, g - 1)
                link(dve, "dve", nc.vector.tensor_tensor(ptmp[:, g % 2, :], pa[:, src, 8 - w // 2:8 - w // 2 + TX],
                                                         pcnt[:, g, :], ALU.mult))
                nc.vector.tensor_tensor(ptmp[:, g % 2, :], ptmp[:, g % 2, :], ox[:, g, :], ALU.subtract)\
                    .then_inc(pool_in, 1)
                if g >= 1:
                    pool_out(g - 1)
            pool_out(3)
            heads_dve(dve, "odd")
            att_dve(dve, "odd", NU_EVEN)
            drain_residual(dve, OO, lambda c, g: mod[:, 1, 5, c, g:g + 1])

        DI, DZ = ST["dn_in"], ST["dn_z"]
        dn_loaded, conv_d, conv_s, ba_mm, ba_w, z_silu, gates_d, dn_fin, dn_hi, dn_lo = [S(x) for x in
            ("dn_loaded", "conv_done", "conv_silu", "ba_sum", "ba_split", "z_silu", "decay_done",
             "dn_gated", "dn_hi", "dn_lo")]
        s_zero = S("state_zero")
        ALOG, DTB = 35, 39
        BETA, SPX, SPM, SPE, GG, EAL, NAB = 0, 1, 2, 3, 4, 5, 6
        SM = 7

        pe_n = ["col", "row", "kk", "tm", "ut", "x1", "tu1", "x2", "tu2", "x3", "tu3", "x4", "tu4",
                "x5", "tu5", "uw", "ws0", "up0", "ws1", "up1", "o"]
        act_n = ["gc", "eg", "er", "et", "tt", "x1", "x2", "x3", "x4", "x5", "uw", "o"]
        dve_n = ["gb", "dl", "be", "et", "el", "lt", "vb", "u1", "c1", "tu1", "c2", "tu2", "c3", "tu3",
                 "c4", "tu4", "c5", "tu5", "v0", "s0", "v1", "s1"]
        dp, da, dd = (Steps(S("dn_pe"), pe_n), Steps(S("dn_act"), act_n), Steps(S("dn_dve"), dve_n))

        def bank(b, n=512):
            return psum[:, b * 512:b * 512 + n]

        def bank4(b):
            return bank(b).rearrange("p (h n) -> p h n", h=4)

        def dn_pool(pool):
            pool.wait_ge(n_z, KD * 7)
            pool.dma_start(dmask[:], t["c_dmask"]).then_inc(dn_loaded, 16)
            pool.dma_start(wconv[:], t["wconv"]).then_inc(dn_loaded, 16)
            pool.dma_start(wba[:], t["wba"]).then_inc(dn_loaded, 16)

        MASKT, CUM, BLK = dmask[:, 0, :], dmask[:, 1, :], dmask[:, 2, :]

        def dn_tile_pe(pe, a):
            def w(steps, name, turn=a):
                pe.wait_ge(steps.sem, steps.at(turn, name))

            def done(ins):
                ins.then_inc(dp.sem, 1)
            tok = slice(4 + a * P, 4 + (a + 1) * P)
            if a:
                w(dd, "s1", a - 1)
                w(da, "o", a - 1)
            g4 = dncol[:, GG, a * 4:a * 4 + 4]
            nc.tensor.matmul(psum[:, 0:4], CUM, g4, start=True, stop=True)
            done(nc.tensor.matmul(psum[:, 4:8], BLK, g4, start=True, stop=True))
            w(dd, "gb")
            for hd in range(4):
                nc.tensor.matmul(bank4(1)[:, hd], dnb["xx"][:, hd], CUM, start=True, stop=True)
                last = nc.tensor.matmul(bank4(2)[:, hd], dnb["uc"][:, hd], ident[:], start=True, stop=True)
            done(last)
            for hd in range(4):
                q, k = dn[:, hd, tok], dn[:, 4 + hd, tok]
                nc.tensor.matmul(bank4(3)[:, hd], k, k, start=True, stop=True)
                last = nc.tensor.matmul(bank4(4)[:, hd], k, q, start=True, stop=True)
            done(last)
            for hd in range(4):
                nc.tensor.transpose(bank4(5)[:, hd], dn[:, 4 + hd, tok], ident[:])
                last = nc.tensor.transpose(bank4(6)[:, hd], dn[:, 8 + hd, tok], ident[:])
            done(last)
            w(dd, "u1")
            for hd in range(4):
                last = nc.tensor.transpose(bank4(7)[:, hd], dnb["uu"][:, hd], ident[:])
            done(last)
            for lv in range(1, 6):
                w(dd, f"c{lv}")
                if lv == 1:
                    w(da, "tt")
                else:
                    w(dd, f"tu{lv - 1}")
                for hd in range(4):
                    last = nc.tensor.matmul(bank4(0)[:, hd], dnb["uc"][:, hd], dnb["tt"][:, hd],
                                            start=True, stop=True)
                done(last)
                w(da, f"x{lv}")
                for hd in range(4):
                    last = nc.tensor.matmul(bank4(1)[:, hd], dnb["xx"][:, hd], dnb["uu"][:, hd],
                                            start=True, stop=True)
                if lv < 5:
                    for hd in range(4):
                        last = nc.tensor.matmul(bank4(2)[:, hd], dnb["uu"][:, hd], dnb["xx"][:, hd],
                                                start=True, stop=True)
                done(last)
            w(dd, "tu5")
            for hd in range(4):
                nc.tensor.matmul(bank4(3)[:, hd], dnb["uu"][:, hd], dnb["vb"][:, hd], start=True, stop=True)
                last = nc.tensor.matmul(bank4(4)[:, hd], dnb["kbe"][:, hd], dnb["uu"][:, hd],
                                        start=True, stop=True)
            done(last)
            w(da, "uw")
            for half in range(2):
                st = state[:, (2 * a + half) % 3]
                if a == 0 and half == 0:
                    pe.wait_ge(s_zero, 1)
                elif half:
                    w(dd, "s0")
                for hd in range(4):
                    last = nc.tensor.matmul(bank4(5 + 2 * half)[:, hd], dnb["wt"][:, hd], st[:, hd],
                                            start=True, stop=True)
                done(last)
                w(dd, f"v{half}")
                r = slice(64 * half, 64 * half + 64)
                for hd in range(4):
                    last = nc.tensor.matmul(bank4((6 + 2 * half) % 8)[:, hd], dnb["ke"][r, hd], dnb["vn"][r, hd],
                                            start=True, stop=True)
                done(last)
            for hd in range(4):
                o = bank4(1)[:, hd]
                nc.tensor.matmul(o, dnb["vn"][:, hd], dnb["at_"][:, hd], start=True, stop=False)
                for half in range(2):
                    c = slice(64 * half, 64 * half + 64)
                    last = nc.tensor.matmul(o[:, c], state[:, (2 * a + half) % 3, hd], dnb["qe"][:, hd, c],
                                            start=False, stop=half == 1)
            done(last)

        def dn_tile_act(act, a):
            def w(steps, name, turn=a):
                act.wait_ge(steps.sem, steps.at(turn, name))

            def run(out, in_, f=ACT.Copy, **kw):
                nc.scalar.activation(out, in_, f, **kw).then_inc(da.sem, 1)
            w(dp, "col")
            run(dncol[:, SM, 0:8], psum[:, 0:8])
            w(dd, "dl")
            nc.scalar.activation(dncol[:, SM + 1, 0:4], dncol[:, SM, 0:4], ACT.Exp)
            run(dncol[:, SM + 1, 4:8], dncol[:, SM, 8:12], ACT.Exp)
            w(dp, "row")
            if a:
                w(dp, "ws1", a - 1)
            run(dnb["wt"][:], bank4(1), ACT.Exp)
            w(dd, "et")
            run(dnb["et"][:], dnb["et"][:], ACT.Exp)
            w(dp, "ut")
            run(dnb["tt"][:], bank4(7))
            for lv in range(1, 6):
                w(dp, f"x{lv}")
                run(dnb["xx"][:], bank4(0))
            w(dp, "uw")
            nc.scalar.activation(dnb["xx"][:], bank4(3), ACT.Copy)
            run(dnb["wt"][:], bank4(4))
            w(dp, "o")
            run(dn[:, 0:4, 4 + a * P:4 + (a + 1) * P], bank4(1))

        def dn_tile_dve(dve, a):
            def w(steps, name, turn=a):
                dve.wait_ge(steps.sem, steps.at(turn, name))

            def done(ins, name):
                ins.then_inc(dd.sem, 1)
                dve.wait_ge(dd.sem, dd.at(a, name))
            tt = nc.vector.tensor_tensor
            full = [P, 4, P]
            tok = slice(4 + a * P, 4 + (a + 1) * P)
            g4, b4 = dncol[:, GG, a * 4:a * 4 + 4], dncol[:, BETA, a * 4:a * 4 + 4]
            if a:
                w(dp, "o", a - 1)
            nc.vector.tensor_copy(dnb["xx"][:], bc(g4, full))
            done(nc.vector.tensor_copy(dnb["uc"][:], bc(b4, full)), "gb")
            w(da, "gc")
            done(tt(dncol[:, SM, 8:12], dncol[:, SM, 4:8], dncol[:, SM, 0:4], ALU.subtract), "dl")
            w(da, "eg")
            done(tt(dncol[:, SM + 1, 8:12], dncol[:, SM + 1, 0:4], b4, ALU.mult), "be")
            w(dp, "row")
            w(da, "er")
            for hd in range(4):
                last = nc.vector.scalar_tensor_tensor(dnb["et"][:, hd], bank4(1)[:, hd],
                                                      dncol[:, SM, hd:hd + 1], MASKT, ALU.subtract, ALU.add)
            done(last, "et")
            nc.vector.tensor_copy(dncol[:, SM + 2, 0:8].rearrange("p (h s) -> p h s", h=4), dnb["wt"][:, :, 63:128:64])
            done(tt(dnb["qe"][:], dn[:, 0:4, tok], dnb["wt"][:], ALU.mult), "el")
            w(da, "et")
            w(dp, "kk")
            link(dve, "dve", tt(dnb["lt"][:], dnb["et"][:], bank4(2), ALU.mult))
            tt(dnb["at_"][:], dnb["et"][:], bank4(4), ALU.mult)
            done(tt(dnb["lt"][:], dnb["lt"][:], bank4(3), ALU.mult), "lt")
            w(dp, "tm")
            tt(dnb["vb"][:], bank4(6), bc(b4, full), ALU.mult)
            tt(dnb["kbe"][:], bank4(5), bc(dncol[:, SM + 1, 8:12], full), ALU.mult)
            done(tt(dnb["ke"][:], bank4(5), bc(dncol[:, SM + 1, 4:8], full), ALU.mult), "vb")
            link(dve, "dve", tt(dnb["uc"][:], dnb["lt"][:], mid(dmask[:, 3, :], 4), ALU.mult))
            done(tt(dnb["uu"][:], mid(ident[:, :], 4), dnb["uc"][:], ALU.subtract), "u1")
            for lv in range(1, 6):
                if lv > 1:
                    w(dp, f"x{lv - 1}")
                done(tt(dnb["uc"][:], dnb["lt"][:], mid(dmask[:, 3 + lv, :], 4), ALU.mult), f"c{lv}")
                w(dp, f"tu{lv}")
                if lv < 5:
                    tt(dnb["tt"][:], dnb["tt"][:], bank4(2), ALU.subtract)
                done(tt(dnb["uu"][:], dnb["uu"][:], bank4(1), ALU.subtract), f"tu{lv}")
            for half in range(2):
                r = slice(64 * half, 64 * half + 64)
                s0, s1 = state[:, (2 * a + half) % 3], state[:, (2 * a + half + 1) % 3]
                w(dp, f"ws{half}")
                w(da, "uw")
                done(tt(dnb["vn"][r], dnb["xx"][r], bank4(5 + 2 * half)[r], ALU.subtract), f"v{half}")
                w(dp, "x5")
                el = dncol[:, SM + 2, 0:8].rearrange("p (h s) -> p h s", h=4)[:, :, half]
                link(dve, "dve", tt(dnb["uc"][:], s0, bc(el, full), ALU.mult))
                w(dp, f"up{half}")
                done(tt(s1, dnb["uc"][:], bank4((6 + 2 * half) % 8), ALU.add), f"s{half}")

        def dn_pe(pe):
            norm_pe(pe, 6, TX)
            pe.wait_ge(n_z, KD * 7)
            products(pe, DI, zh, zl)
            products(pe, DZ, zh, zl)
            pe.wait_ge(drained, all_drained(DZ))
            pe.wait_ge(ba_w, 2)
            for a in range(4):
                s = slice(a * P, (a + 1) * P)
                for c in range(KD):
                    for j, (x, w) in enumerate(((zh, wbah), (zh, wbal), (zl, wbah))):
                        last = nc.tensor.matmul(psum[:, 3072 + a * NBA:3072 + (a + 1) * NBA], x[:, c, s], w[:, c, :],
                                                start=(c == 0 and j == 0), stop=(c == KD - 1 and j == 2))
            last.then_inc(ba_mm, 1)
            heads_pe(pe, "dn_qk")
            after_heads(pe, "dn_qk")
            pe.wait_ge(gates_d, 1)
            for a in range(4):
                dn_tile_pe(pe, a)
            pe.wait_ge(dd.sem, dd.at(3, "s1"))
            pe.wait_ge(da.sem, da.at(3, "o"))
            heads_pe(pe, "dn_o")

        def dn_act(act):
            act.wait_ge(drained, DI.first + 4)
            norm_act(act, 6, TX, lambda c, g: cols[:, NW2 + c:NW2 + c + 1], lambda c, g: eps_c[:, 2:3])
            act_tiles(act, DI)
            act_tiles(act, DZ)
            act.wait_ge(dn_loaded, 48)
            nc.scalar.activation(wbah[:], wba[:], ACT.Copy).then_inc(ba_w, 1)
            for m in range(12):
                act.wait_ge(conv_d, m + 1)
                nc.scalar.activation(dn[:, m, 4:DW], cacc[:, m % 2, :], ACT.Silu).then_inc(conv_s, 1)
            act.wait_ge(drained, all_drained(DZ))
            nc.scalar.activation(dz[:], dz[:], ACT.Silu).then_inc(z_silu, 1)
            act.wait_ge(conv_s, 12)
            heads_act(act, "dn_qk")
            act.wait_ge(ba_mm, 1)
            ba = psum[:, 3072:3072 + 4 * NBA].rearrange("p (a n) -> p a n", a=4)
            row = lambda r: dncol[:, r, :].rearrange("p (a n) -> p a n", a=4)
            nc.scalar.activation(row(BETA), ba[:, :, 0:4], ACT.Sigmoid).then_inc(sp_s, 1)
            act.wait_ge(sp_d, 1)
            link(act, "act", nc.scalar.activation(dncol[:, SPE, :], dncol[:, SPM, :], ACT.Exp))
            nc.scalar.activation(dncol[:, EAL, 0:4], cols[:, ALOG:ALOG + 4], ACT.Exp)
            nc.scalar.activation(dncol[:, SPE, :], dncol[:, SPE, :], ACT.Ln, bias=eps_c[:, 1:2]).then_inc(sp_s, 1)
            for a in range(4):
                dn_tile_act(act, a)
            act.wait_ge(da.sem, da.at(3, "o"))
            heads_act(act, "dn_o")
            act.wait_ge(dn_fin, 1)
            nc.scalar.activation(odnh[:], dz[:], ACT.Copy).then_inc(dn_hi, 1)

        sp_s, sp_d = S("softplus_act"), S("softplus_dve")

        def dn_dve(dve):
            norm_dve(dve, 6, TX)
            dve.wait_ge(n_z, KD * 7)
            nc.vector.memset(dn[:, :, 0:4], 0.0)
            drain_to(dve, DI, dn, lead=4)
            drain_to(dve, DZ, dz)
            dve.wait_ge(dn_loaded, 48)
            dve.wait_ge(ba_w, 1)
            nc.vector.tensor_tensor(wbal[:], wba[:], wbah[:], ALU.subtract).then_inc(ba_w, 1)
            dve.wait_ge(drained, all_drained(DZ))
            for m in range(12):
                if m >= 2:
                    dve.wait_ge(conv_s, m - 1)
                c = cacc[:, m % 2, :]
                link(dve, "dve", nc.vector.tensor_scalar(c, dn[:, m, 1:1 + TX], wconv[:, m, 0:1], None, ALU.mult))
                for j in range(1, 4):
                    ins = nc.vector.scalar_tensor_tensor(c, dn[:, m, 1 + j:1 + j + TX], wconv[:, m, j:j + 1], c,
                                                         ALU.mult, ALU.add)
                    if j < 3:
                        link(dve, "dve", ins)
                ins.then_inc(conv_d, 1)
            heads_dve(dve, "dn_qk")
            dve.wait_ge(ba_mm, 1)
            ba = psum[:, 3072:3072 + 4 * NBA].rearrange("p (a n) -> p a n", a=4)
            row = lambda r: dncol[:, r, :].rearrange("p (a n) -> p a n", a=4)
            dve.wait_ge(sp_s, 1)
            link(dve, "dve", nc.vector.tensor_tensor(row(SPX), ba[:, :, 4:8], mid(cols[:, DTB:DTB + 4], 4), ALU.add))
            link(dve, "dve", nc.vector.tensor_scalar(dncol[:, NAB, :], dncol[:, SPX, :], -1.0, None, ALU.mult))
            nc.vector.tensor_tensor(dncol[:, SPM, :], dncol[:, SPX, :], dncol[:, NAB, :], ALU.min).then_inc(sp_d, 1)
            link(dve, "dve", nc.vector.tensor_scalar(dncol[:, SPX, :], dncol[:, SPX, :], 0.0, -1.0, ALU.max, ALU.mult))
            dve.wait_ge(sp_s, 2)
            link(dve, "dve", nc.vector.tensor_tensor(dncol[:, SPX, :], dncol[:, SPX, :], dncol[:, SPE, :], ALU.subtract))
            nc.vector.memset(state[:, 0], 0.0).then_inc(s_zero, 1)
            ins = nc.vector.tensor_tensor(row(GG), row(SPX), mid(dncol[:, EAL, 0:4], 4), ALU.mult)
            ins.then_inc(gates_d, 1)
            dve.wait_ge(gates_d, 1)
            dve.wait_ge(s_zero, 1)
            for a in range(4):
                dn_tile_dve(dve, a)
            dve.wait_ge(da.sem, da.at(3, "o"))
            heads_dve(dve, "dn_o")
            after_heads(dve, "dn_o")
            dve.wait_ge(z_silu, 1)
            nc.vector.tensor_tensor(dz[:], dz[:], dn[:, 0:4, 4:DW], ALU.mult).then_inc(dn_fin, 1)
            dve.wait_ge(dn_hi, 1)
            nc.vector.tensor_tensor(odnl[:], dz[:], odnh[:], ALU.subtract).then_inc(dn_lo, 1)
            dve.wait_ge(dn_lo, 1)

        SW = [ST[f"swa{hd}_in"] for hd in range(4)]
        sw_loaded, svt_tr, svt_cp = S("sw_loaded"), S("swv_transposed"), S("swv_copied")

        def sw_units(hd):
            us = []
            for n in range(4):
                s = slice(n * P, (n + 1) * P)
                lo, n0 = max(n - 1, 0), min(n + 1, 2)
                blocks = [(0, a) for a in range(lo, n + 1)] + [(g, a) for g in (1, 2) for a in range(n + 1)]
                keys = []
                for j, (g, a) in enumerate(blocks):
                    if j and j % 4 and blocks[j - 1][0] == g:
                        q, k, c, w = keys.pop()
                        first = blocks[j - w // P][1]
                        keys.append((q, sx[:, 3 + g, first * P:(a + 1) * P], c, w + P))
                    else:
                        keys.append((sx[:, g, s], sx[:, 3 + g, a * P:(a + 1) * P], j * P, P))
                sg = [(0, n0 * P, smask[:, 2 - n0:2, :].rearrange("p a n -> p (a n)"))]
                for g in (1, 2):
                    e = 2 + 4 * g
                    sg.append(((n0 + (g - 1) * (n + 1)) * P, (n + 1) * P,
                               smask[:, e - n - 1:e, :].rearrange("p a n -> p (a n)")))
                us.append(Unit(keys=keys, segs=sg, scale=float(P) ** -0.5, s=sw_s, pt=sw_pt,
                                    vals=[svt[:, g, a, :] for g, a in blocks],
                                    out=(slice(0, P), oswa[:, hd, s])))
            return us

        for hd in range(4):
            add_units(f"swa{hd}", sw_units(hd))

        def swa_pool(pool):
            pool.wait_ge(dn_lo, 1)
            pool.dma_start(smask[:], t["c_smask"]).then_inc(sw_loaded, 16)
            pool.dma_start(ropeb[:], t["c_ropeb"]).then_inc(sw_loaded, 16)

        def swa_pe(pe):
            pe.wait_ge(dn_lo, 1)
            for hd in range(4):
                products(pe, SW[hd], zh, zl)
                pe.wait_ge(drained, all_drained(SW[hd]))
                for g in range(3):
                    if g >= 2:
                        pe.wait_ge(svt_cp, 3 * hd + g - 1)
                    for a in range(4):
                        last = nc.tensor.transpose(psum[:, 3072 + g % 2 * 512 + a * P:3072 + g % 2 * 512 + (a + 1) * P],
                                                   sx[:, 6 + g, a * P:(a + 1) * P], ident[:])
                    last.then_inc(svt_tr, 1)
                heads_pe(pe, f"swa{hd}")
                after_heads(pe, f"swa{hd}")
                pe.wait_ge(svt_cp, 3 * hd + 3)
                att_pe(pe, f"swa{hd}")
                pe.wait_ge(at_o, NU_ODD + 4 * (hd + 1))

        def swa_act(act):
            for hd in range(4):
                act_tiles(act, SW[hd])
                act.wait_ge(drained, all_drained(SW[hd]))
                heads_act(act, f"swa{hd}")
                att_act(act, f"swa{hd}")

        def swa_dve(dve):
            for hd in range(4):
                drain_to(dve, SW[hd], sx)
                for g in range(3):
                    dve.wait_ge(svt_tr, 3 * hd + g + 1)
                    nc.vector.tensor_copy(svt[:, g], psum[:, 3072 + g % 2 * 512:3584 + g % 2 * 512]
                                          .rearrange("p (a n) -> p a n", a=4)).then_inc(svt_cp, 1)
                dve.wait_ge(sw_loaded, 32)
                heads_dve(dve, f"swa{hd}")
                att_dve(dve, f"swa{hd}", NU_ODD)

        SZ, GA, BD, BS, OU = ST["swa_z"], ST["gates"], ST["br_dn"], ST["br_swa"], ST["out"]
        sz_silu, sz_m, os_hi, os_lo, g_sig, mg_d, mg_hi, mg_lo, o_tr, o_cp, o_st = [S(x) for x in
            ("swz_silu", "sw_gated", "sw_hi", "sw_lo", "gates_sig", "merged", "merged_hi", "merged_lo",
             "out_transposed", "out_copied", "out_stored0")]
        o_st = [o_st, S("out_stored1")]

        def tail_pe(pe):
            products(pe, SZ, zh, zl)
            pe.wait_ge(os_lo, 1)
            products(pe, GA, zh, zl)
            products(pe, BD, odnh, odnl)
            products(pe, BS, osh, osl)
            pe.wait_ge(mg_lo, KD)
            products(pe, OU, zh, zl)
            pe.wait_ge(drained, all_drained(OU))
            for a in range(4):
                if a >= 2:
                    pe.wait_ge(o_cp, a - 1)
                for c in range(KD):
                    last = nc.tensor.transpose(psum[:, a % 2 * 1024 + c * P:a % 2 * 1024 + (c + 1) * P],
                                               h[:, c, a * P:(a + 1) * P], ident[:])
                last.then_inc(o_tr, 1)

        def tail_act(act):
            act_tiles(act, SZ)
            act.wait_ge(drained, all_drained(SZ))
            nc.scalar.activation(szt[:], szt[:], ACT.Silu).then_inc(sz_silu, 1)
            act.wait_ge(sz_m, 1)
            nc.scalar.activation(osh[:], oswa[:], ACT.Copy).then_inc(os_hi, 1)
            act_tiles(act, GA)
            act.wait_ge(drained, all_drained(GA))
            for j in range(4):
                nc.scalar.activation(gt[:, 4 * j:4 * j + 4, :], gt[:, 4 * j:4 * j + 4, :], ACT.Sigmoid)\
                    .then_inc(g_sig, 1)
            act_tiles(act, BD)

            def upper(n, k, c, i):
                act.wait_ge(mg_d, k + 1)
                nc.scalar.activation(zh[:, k, 0:TX], gt[:, k, :], ACT.Copy).then_inc(mg_hi, 1)
            act_tiles(act, BS, upper)
            act_tiles(act, OU)

        def tail_dve(dve):
            drain_to(dve, SZ, szt)
            dve.wait_ge(sz_silu, 1)
            nc.vector.tensor_tensor(oswa[:], oswa[:], szt[:], ALU.mult).then_inc(sz_m, 1)
            dve.wait_ge(os_hi, 1)
            nc.vector.tensor_tensor(osl[:], oswa[:], osh[:], ALU.subtract).then_inc(os_lo, 1)
            dve.wait_ge(os_lo, 1)
            drain_to(dve, GA, gt)
            dve.wait_ge(g_sig, 4)

            def gate_dn(n, k, c, i):
                dve.wait_ge(tile_done, sum_ready(n))
                nc.vector.tensor_tensor(gt[:, k, :], acc(c, TX), gt[:, k, :], ALU.mult).then_inc(drained, 1)
            dve_tiles(dve, BD, gate_dn)

            def gate_swa(n, k, c, i):
                dve.wait_ge(tile_done, sum_ready(n))
                nc.vector.tensor_tensor(gt[:, 8 + k, :], acc(c, TX), gt[:, 8 + k, :], ALU.mult)\
                    .then_inc(drained, 1)
                dve.wait_ge(drained, n + 5)
                nc.vector.tensor_tensor(gt[:, k, :], gt[:, k, :], gt[:, 8 + k, :], ALU.add).then_inc(mg_d, 1)
                dve.wait_ge(mg_hi, k + 1)
                nc.vector.tensor_tensor(zl[:, k, 0:TX], gt[:, k, :], zh[:, k, 0:TX], ALU.subtract)\
                    .then_inc(mg_lo, 1)
            dve_tiles(dve, BS, gate_swa)
            drain_residual(dve, OU, lambda c, g: None)
            for a in range(4):
                dve.wait_ge(o_tr, a + 1)
                if a >= 2:
                    dve.wait_ge(o_st[a % 2], 16)
                nc.vector.tensor_copy(outb[:, a % 2, :], psum[:, a % 2 * 1024:a % 2 * 1024 + 1024])\
                    .then_inc(o_cp, 1)

        def tail_sp(sp):
            for a in range(4):
                sp.wait_ge(o_cp, a + 1)
                sp.dma_start(t["out"][a * P:(a + 1) * P, :], outb[:, a % 2, :]).then_inc(o_st[a % 2], 16)
            sp.wait_ge(o_st[0], 32)
            sp.wait_ge(o_st[1], 32)

        block = ctx.enter_context(nc.Block())

        @block.sync
        def _(sp):
            start_sp(sp)
            ffn_sp(sp, 0)
            load_tiles(sp, EI, t["ev_in"])
            load_tiles(sp, EO, t["ev_out"])
            ffn_sp(sp, 1)
            ffn_sp(sp, 2)
            load_tiles(sp, OX, t["od_in"][0:8])
            load_tiles(sp, OKV, t["od_in"][8:16])
            load_tiles(sp, OO, t["od_out"])
            ffn_sp(sp, 3)
            load_tiles(sp, DI, t["w2_dn"])
            load_tiles(sp, DZ, t["w2_z"])
            for hd in range(4):
                load_tiles(sp, SW[hd], t["w2_sw"][hd])
            load_tiles(sp, SZ, t["w2_sz"])
            load_tiles(sp, GA, t["w2_ga"])
            load_tiles(sp, BD, t["w2_bd"])
            load_tiles(sp, BS, t["w2_bs"])
            load_tiles(sp, OU, t["w2_out"])
            tail_sp(sp)

        @block.gpsimd
        def _(pool):
            start_pool(pool)
            even_pool(pool)
            odd_pool(pool)
            dn_pool(pool)
            swa_pool(pool)

        @block.scalar
        def _(act):
            start_act(act)
            split_hi(act, 0, 0, None)
            act.wait_ge(mod_done, 1)
            ffn_act(act, 0)
            even_act(act)
            ffn_act(act, 1)
            ffn_act(act, 2)
            odd_act(act)
            ffn_act(act, 3)
            dn_act(act)
            swa_act(act)
            tail_act(act)

        @block.vector
        def _(dve):
            dve.sem_inc(w_lo, 4)
            start_dve(dve)
            split_lo(dve, 0, 0, None)
            ffn_dve(dve, 0)
            even_dve(dve)
            ffn_dve(dve, 1)
            ffn_dve(dve, 2)
            odd_dve(dve)
            ffn_dve(dve, 3)
            dn_dve(dve)
            swa_dve(dve)
            tail_dve(dve)

        @block.tensor
        def _(pe):
            pe.sem_inc(tile_done, 2)
            pe.sem_inc(drained, 4)
            start_pe(pe)
            ffn_pe(pe, 0)
            even_pe(pe)
            ffn_pe(pe, 1)
            ffn_pe(pe, 2)
            odd_pe(pe)
            ffn_pe(pe, 3)
            dn_pe(pe)
            swa_pe(pe)
            tail_pe(pe)


def shape_constants():
    f = np.float32
    i = np.arange(P)
    c = {"c_ident": np.eye(P, dtype=f), "c_ones": np.ones((P, P), f),
         "c_ones_blk": (i[:, None] // 64 == i[None] // 64).astype(f)}

    def partners(heads, half):
        w = np.zeros((P, P), f)
        for first in heads:
            for m in range(half):
                w[first + m + half, first + m] = -1.0
                w[first + m, first + m + half] = 1.0
        return w
    c["c_perm_a"] = partners(range(0, P, 32), 16)
    c["c_perm_b"] = partners([0], 16)
    c["c_eps"] = np.tile(np.array([EPS, 1.0, 0.0, 0.0], f), (P, 1))
    tok = np.arange(TX)
    m = 16
    inv = (1.0 / (np.float32(10000.0) ** (np.arange(m, dtype=f) / f(m)))).astype(f)
    row, col = (tok // 64).astype(f), (tok % 64).astype(f)
    ang = np.zeros((P, TX), f)
    for p in range(P):
        d = p % 64
        ang[p] = (row if d < 32 else col) * inv[d % 16]
    c["c_ropea"] = np.stack([np.cos(ang), np.sin(ang)], 1).astype(f)
    invb = (np.float32(500000.0) ** (-np.arange(0, 32, 2, dtype=f) / f(32))).astype(f)
    angb = np.zeros((P, TX), f)
    for p in range(32):
        angb[p] = tok.astype(f) * invb[p % 16]
    c["c_ropeb"] = np.stack([np.cos(angb), np.sin(angb)], 1).astype(f)
    q, k = i[:, None], i[None]
    z = np.zeros((P, P), f)

    def neg(valid):
        return np.where(valid, f(0), f(NEG)).astype(f)
    c["c_ev_mask"] = np.concatenate([neg(k >= q), z, z, z, neg(k <= q)], 1)
    sm = [neg(k >= q), neg(k <= q)]
    for dil in (4, 16):
        same = (q - k) % dil == 0
        sm += [neg(same)] * 3 + [neg(same & (k <= q))]
    c["c_smask"] = np.stack(sm, 1)
    cnt = np.zeros((4, TX), f)
    for g, w in enumerate((2, 4, 8, 16)):
        lo, hi = np.clip(tok - w // 2, 0, TX), np.clip(tok + w - w // 2, 0, TX)
        cnt[g] = f(1) / (hi - lo).astype(f)
    c["c_pcnt"] = np.broadcast_to(cnt[None], (P, 4, TX)).copy()
    same = q // 64 == k // 64
    dm = [neg(same & (k >= q)), (same & (k >= q)).astype(f), same.astype(f)]
    for lv in range(6):
        b = 1 << lv
        dm.append(((k // (2 * b) == q // (2 * b)) & (k // b % 2 == 1) & (q // b % 2 == 0)).astype(f))
    c["c_dmask"] = np.stack(dm, 1).astype(f)
    return c


def tiles(w, chunks):
    k, n = w.shape
    return np.ascontiguousarray(w.reshape(chunks, P, n // P, P).transpose(2, 1, 0, 3).reshape(n // P, P, chunks * P))


def lay_out(inp):
    f = {k: np.asarray(v) for k, v in inp.items()}
    a = shape_constants()
    a["xin"] = np.ascontiguousarray(np.concatenate([f["x"][0], f["ctx"][0]]).reshape(6, P, D).transpose(1, 0, 2))
    a["csc"] = np.ascontiguousarray(np.stack([f["c"][0], f["c_ctx"]], -1).reshape(KD, P, 2).transpose(1, 0, 2))
    a["ada_w"] = np.ascontiguousarray(
        f["ada_w"].reshape(2, KD, P, 18, 512).transpose(0, 3, 2, 1, 4).reshape(36, P, KD, 512))
    a["adab"] = np.ascontiguousarray(f["ada_b"].reshape(2, NMOD * KD, P).transpose(2, 0, 1))
    a["ngain"] = np.ascontiguousarray(f["norm_g"].reshape(2, 3, KD, P).transpose(3, 0, 1, 2))

    gu, wd = f["ffn_w_gu"].reshape(4, D, 2 * DFF), f["ffn_w_down"].reshape(4, DFF, D)
    up = np.stack([np.stack([tiles(g[:, :DFF], KD), tiles(g[:, DFF:], KD)], 1) for g in gu])
    a["wup_a"] = np.ascontiguousarray(up[:, :JA].reshape(4, 2 * JA, P, D))
    a["wup_b"] = np.ascontiguousarray(up[:, JA:].reshape(4, 2 * JB, P, D))
    a["wdn_a"] = np.stack([tiles(w[:JA * P], JA) for w in wd])
    a["wdn_b"] = np.stack([tiles(w[JA * P:], JB) for w in wd])

    w = f["ev_w_in"][0]
    k0, k1 = w[:, 512:576], w[:, 576:640]
    a["ev_in"] = tiles(np.concatenate([w[:, :512], k0, k0, k1, k1, w[:, 640:]], 1), KD)
    a["ev_out"] = tiles(f["ev_w_out"][0], KD)
    a["wst"] = np.ascontiguousarray(f["b_ws"][0].transpose(2, 0, 1))
    a["bbias"] = np.ascontiguousarray(np.repeat(f["b_bias"][0].reshape(4, 2, P).transpose(1, 0, 2), 64, 0))
    a["od_in"] = tiles(f["od_w_in"][0], KD)
    a["od_out"] = tiles(f["od_w_out"][0], KD)
    a["wpool"] = np.ascontiguousarray(f["c_w_pool"][0].transpose(1, 0, 2))
    rpb = f["d_rpb"][0]
    half, cq, dr, ck = np.ix_(np.arange(2), np.arange(64), np.arange(16), np.arange(64))
    start = np.clip(cq - 8, 0, 48)
    di, ci = dr - half, ck - cq + 15
    ok = (di >= 0) & (di < 15) & (ck >= start) & (ck < start + 16)
    nb = rpb[:, np.clip(di, 0, 14), np.clip(ci, 0, 30)]
    a["nbias"] = np.ascontiguousarray(np.where(ok, nb, np.float32(NEG)).reshape(8, P, 1024))

    w2 = f["w_in_2"][0]
    a["w2_dn"] = tiles(w2[:, 0:1536], KD)
    a["w2_z"] = tiles(w2[:, 1536:2048], KD)
    a["wba"] = np.ascontiguousarray(w2[:, 2048:2056].reshape(KD, P, NBA).transpose(1, 0, 2))
    qkv = w2[:, 2056:2056 + 4608].reshape(D, 3, 3, 4, P)
    a["w2_sw"] = np.stack([tiles(qkv[:, :, :, hd].reshape(D, 9 * P), KD) for hd in range(4)])
    a["w2_sz"] = tiles(w2[:, 6664:7176], KD)
    a["w2_ga"] = tiles(w2[:, 7176:9224], KD)
    a["w2_bd"] = tiles(f["w_branch_dn_2"][0], 4)
    a["w2_bs"] = tiles(f["w_branch_swa_2"][0], 4)
    a["w2_out"] = tiles(f["w_out_2"][0], KD)
    a["wconv"] = np.ascontiguousarray(f["conv_w_2"][0, :, 0].reshape(4, 12, P).transpose(2, 1, 0))

    def down(v):
        return np.asarray(v).reshape(-1, P).T

    def wide(v):
        return np.broadcast_to(np.asarray(v).reshape(1, -1), (P, np.asarray(v).size))
    cols = [np.tile(f["a_q_gain"][0], 2)[:, None], np.tile(f["a_k_gain"][0], 2)[:, None],
            down(f["b_v_gain"][0]), np.tile(f["d_q_gain"][0], 2)[:, None], np.tile(f["d_k_gain"][0], 2)[:, None],
            down(f["c_scale"][0]), down(f["norm_w_2"][0]), down(f["dn_norm_w_2"][0]),
            down(f["q_norm_w_2"][0]), down(f["k_norm_w_2"][0]), wide(f["a_sink"][0]),
            wide(f["dn_a_log_2"][0]), wide(f["dn_dt_bias_2"][0])]
    c = np.concatenate(cols, 1)
    a["cols"] = np.ascontiguousarray(np.concatenate([c, np.zeros((P, 64 - c.shape[1]), np.float32)], 1))
    return a


def kernel(**inputs):
    import concourse.bacc as bacc
    from concourse.bass_utils import run_bass_kernel_spmd

    arrays = lay_out(inputs)
    nc = bacc.Bacc("TRN2", target_bir_lowering=False, num_devices=1)
    t = {k: nc.dram_tensor("in_" + k, v.shape, mybir.dt.from_np(v.dtype), kind="ExternalInput").ap()
         for k, v in arrays.items()}
    t["out"] = nc.dram_tensor("out_x", (TX, D), mybir.dt.float32, kind="ExternalOutput").ap()
    build(nc, t)
    r = run_bass_kernel_spmd(nc, [{"in_" + k: v for k, v in arrays.items()}], core_ids=[0])
    return np.asarray(r.results[0]["out_x"]).reshape(1, TX, D)
```

```python
import concourse.bass as bass
from concourse import mybir
import numpy as np
from contextlib import ExitStack

P = 128
D = 1024
KD = D // P
TX, TC = 512, 256
T = TX + TC
DFF = 2816
NJ = DFF // P
JA = 11
JB = NJ - JA
EPS = 1e-6
NEG = -1e30
NMOD = 9
WMAX = max(JA, NJ - JA) * P
NBA = 8


class Steps:

    def __init__(self, sem, names, before=0):
        self.sem, self.names, self.before = sem, list(names), before

    def at(self, turn, name):
        return self.before + turn * len(self.names) + self.names.index(name) + 1


class Stage:

    def __init__(self, name, tiles, chunks, tokens, head=0, loop=True):
        self.name, self.tiles, self.chunks, self.tokens = name, tiles, chunks, tokens
        self.head = head
        self.loops = (tiles - 1 - head) // 4 if tiles >= 12 and loop else 0


def plan():
    stages = []
    for f in range(4):
        tok = T if f < 3 else TX
        ffn = [Stage(f"ffn{f}_up_a", 2 * JA, KD, tok, head=2), Stage(f"ffn{f}_down_a", KD, JA, tok),
               Stage(f"ffn{f}_up_b", 2 * JB, KD, tok), Stage(f"ffn{f}_down_b", KD, JB, tok)]
        stages += ffn
        if f == 0:
            stages += [Stage("ev_in", 15, KD, T, head=2), Stage("ev_out", 8, KD, T)]
        if f == 2:
            stages += [Stage("od_in_x", 8, KD, TX), Stage("od_in_kv", 8, KD, T),
                       Stage("od_out", 8, KD, TX)]
    stages += [Stage("dn_in", 12, KD, TX, head=2, loop=False), Stage("dn_z", 4, KD, TX)]
    stages += [Stage(f"swa{h}_in", 9, KD, TX) for h in range(4)]
    stages += [Stage("swa_z", 4, KD, TX), Stage("gates", 16, KD, TX),
               Stage("br_dn", 8, 4, TX), Stage("br_swa", 8, 4, TX), Stage("out", 8, KD, TX)]
    n = 0
    for s in stages:
        s.first = n
        n += s.tiles
    return stages


def build(nc, t):
    f32, f32r = mybir.dt.float32, mybir.dt.float32r
    ALU, ACT, AX = mybir.AluOpType, mybir.ActivationFunctionType, mybir.AxisListType
    STAGES = plan()
    ST = {s.name: s for s in STAGES}
    NTILES = STAGES[-1].first + STAGES[-1].tiles
    STAGE_OF = [s for s in STAGES for _ in range(s.tiles)]

    ctx = ExitStack()
    with ctx:
        place = {"at": (nc.sbuf_base + 63) // 64 * 64}

        def region(size):
            a = place["at"]
            place["at"] = a + (size + 63) // 64 * 64
            return a

        def sb(name, at, shape, dt=f32):
            return nc.alloc_sbuf_tensor_at(name, [P] + list(shape), dt, offset=at)

        def words(*shape):
            return 4 * int(np.prod(shape))

        H_AT = region(words(KD, T))
        ZH_AT = region(words(KD, T))
        ZL_AT = region(words(KD, T))
        RAW_AT = region(words(4, WMAX))
        WH_AT = region(words(2, WMAX))
        WL_AT = region(words(2, WMAX))
        R_SIZE = 24 * words(T)
        R_AT = region(R_SIZE)
        SCR_AT = region(words(4, T))

        def small(name, shape, dt=f32):
            return sb(name, region(words(*shape)), shape, dt)

        h = sb("h", H_AT, [KD, T])
        zh = sb("zh", ZH_AT, [KD, T], f32r)
        zl = sb("zl", ZL_AT, [KD, T], f32r)
        raw = sb("raw", RAW_AT, [4, WMAX])
        wh = sb("wh", WH_AT, [2, WMAX], f32r)
        wl = sb("wl", WL_AT, [2, WMAX], f32r)
        scr = sb("scr", SCR_AT, [4, T])
        ident = small("ident", [P])
        ones = small("ones", [P])
        sel64 = small("sel64", [38])
        sel128 = small("sel128", [38])
        perm_a = small("perm_a", [P])
        perm_b = small("perm_b", [P])
        mod = small("mod", [2, NMOD, KD, 2])
        amul = small("amul", [2, 3, KD, 2])
        ngain = small("ngain", [2, 3, KD])
        eps_c = small("eps_c", [4])
        scc = small("scc", [KD, 2])
        csc = small("csc", [KD, 2])
        cols = small("cols", [64])
        pickT = small("pickT", [2, P])
        nmx = small("nmx", [4])
        rsum = small("rsum", [4])
        esink = small("esink", [4])
        rinv = small("rinv", [4])
        dncol = small("dncol", [12, 16])
        psum = ctx.enter_context(nc.psum_tensor("psum", [P, 4096], f32))
        assert place["at"] <= nc.sbuf_usable_end, place["at"]

        AQ, AK, BV, DQ, DK, CS, NW2, DNW, QN, KN, SINK = 0, 1, 2, 6, 7, 8, 12, 20, 21, 24, 27

        hidh = sb("hidh", R_AT, [JA, T], f32r)
        hidl = sb("hidl", R_AT + words(JA, T), [JA, T], f32r)
        adaw = sb("adaw", R_AT, [4, KD, 512])
        xin = sb("xin", ZH_AT, [6, D])
        adarow = sb("adarow", ZL_AT, [2, 512])
        adab = sb("adab", ZL_AT + words(2, 512), [2, NMOD * KD])
        ev = sb("ev", R_AT, [15, T])
        e2 = R_AT + words(15, T)
        vdup = sb("vdup", e2, [6, 2, 2, 64])
        wst = sb("wst", e2 + words(6, 256), [8, P])
        bbias = sb("bbias", e2 + words(6, 256) + words(8, P), [4, P])
        e3 = e2 + words(6, 256) + words(8, P) + words(4, P)
        ropea = sb("ropea", e3, [2, TX])
        vvt = sb("vvt", e3, [6, 512])
        assert e3 + words(6, 512) <= R_AT + R_SIZE
        ev_s = sb("ev_s", R_AT + words(7, T), [2, 640])
        ev_pt = sb("ev_pt", R_AT + words(7, T) + words(2, 640), [2, 640])
        ev_mask = sb("ev_mask", R_AT + words(7, T) + words(4, 640), [640])
        ox = sb("ox", R_AT, [8, TX])
        okv = sb("okv", R_AT + words(8, TX), [8, T])
        o2 = R_AT + words(8, TX) + words(8, T)
        ovt = sb("ovt", o2, [6, 512])
        nbias = sb("nbias", o2 + words(6, 512), [2, 1024])
        o3 = o2 + words(6, 512) + words(2, 1024)
        od_s = sb("od_s", o3, [2, T])
        od_pt = sb("od_pt", o3 + words(2, T), [2, T])
        assert o3 + words(4, T) <= R_AT + R_SIZE
        PADP = TX + 16
        pa = sb("pa", o3, [3, PADP])
        pcnt = sb("pcnt", SCR_AT, [4, TX])
        wpool = sb("wpool", o3 + words(3, PADP), [4, P])
        assert 3 * PADP + 4 * P <= 4 * T
        DW = TX + 4
        dn = sb("dn", R_AT, [12, DW])
        d2 = R_AT + words(12, DW)
        dz = sb("dz", d2, [4, TX])
        d3 = d2 + words(4, TX)
        names = ["vb", "kbe", "ke", "et", "lt", "at_", "tt", "uu", "xx", "uc", "wt", "vn", "qe"]
        dnb = {}
        for i, n_ in enumerate(names):
            dnb[n_] = sb("dn_" + n_, d3 + words(i, 512), [4, P])
        d4 = d3 + words(len(names), 512)
        state = sb("state", d4, [3, 4, P])
        d5 = d4 + words(3, 512)
        assert d5 <= R_AT + R_SIZE, (d5 - R_AT)
        dmask = sb("dmask", SCR_AT, [9, P])
        wconv = sb("wconv", SCR_AT + words(9, P), [12, 4])
        wba = sb("wba", SCR_AT + words(9, P) + words(48), [KD, NBA])
        wbah = sb("wbah", SCR_AT + words(9, P) + words(48 + 64), [KD, NBA], f32r)
        wbal = sb("wbal", SCR_AT + words(9, P) + words(48 + 128), [KD, NBA], f32r)
        cacc = sb("cacc", SCR_AT + words(9, P) + words(48 + 192), [2, TX])
        assert 9 * P + 240 + 1024 <= 4 * T
        dsq = sb("dsq", d3, [2, TX])
        drr = sb("drr", d3 + words(2, TX), [2, TX])
        odnh = sb("odnh", R_AT, [4, TX], f32r)
        odnl = sb("odnl", R_AT + words(4, TX), [4, TX], f32r)
        dno = sb("dno", R_AT + words(8, DW), [4, TX])
        sw = R_AT + words(8, TX)
        sx = sb("sx", sw, [9, TX])
        s2 = sw + words(9, TX)
        svt = sb("svt", s2, [3, 4, P])
        sw_s = sb("sw_s", s2 + words(12, P), [2, 1280])
        sw_pt = sb("sw_pt", s2 + words(12, P) + words(2, 1280), [2, 1280])
        s3 = s2 + words(12, P) + words(4, 1280)
        oswa = sb("oswa", s3, [4, TX])
        assert s3 + words(4, TX) <= R_AT + R_SIZE
        smask = sb("smask", SCR_AT, [10, P])
        ropeb = sb("ropeb", SCR_AT + words(10, P), [2, TX])
        osh = sb("osh", sw, [4, TX], f32r)
        osl = sb("osl", sw + words(4, TX), [4, TX], f32r)
        gt = sb("gt", sw + words(8, TX), [16, TX])
        outb = sb("outb", sw, [2, D])
        szt = sb("szt", s2 + words(12, P), [4, TX])

        made = {}

        def S(name):
            if name not in made:
                made[name] = ctx.enter_context(nc.semaphore(name))
            return made[name]

        raw_loaded = [S(f"raw_loaded{c}") for c in range(4)]
        w_hi, w_lo, tile_done, drained = S("w_hi"), S("w_lo"), S("tile_done"), S("drained")

        def raw_free(n):
            return n + 1

        def lo_ready(n):
            return n + 5

        def w_slot_free(n):
            return n + 1

        def sum_ready(n):
            return n + 3

        def psum_free(n):
            return n + 1

        def all_drained(stage):
            return stage.first + stage.tiles + 4

        def acc(n, tokens):
            c = n % 4
            return psum[:, c * 1024:c * 1024 + tokens]

        def segs(tokens):
            return [(0, TX)] if tokens == TX else [(0, TX), (TX, T)]

        def load_tiles(sp, stage, src):
            b = stage.first
            w = stage.chunks * P

            def one(n, row):
                sp.wait_ge(w_lo, raw_free(n["v"]))
                sp.dma_start(raw[:, n["c"], 0:w], row).then_inc(raw_loaded[n["c"]], 16)

            for k in range(stage.head):
                one({"v": b + k, "c": (b + k) % 4}, src[k])
            if stage.loops:
                with sp.Fori(0, stage.loops) as i:
                    for c in range(stage.head, stage.head + 4):
                        one({"v": i * 4 + (b + c), "c": (b + c) % 4},
                            src[bass.ds(i * 4 + c, 1)].rearrange("a p n -> (a p) n"))
            for k in range(stage.head + 4 * stage.loops, stage.tiles):
                one({"v": b + k, "c": (b + k) % 4}, src[k])

        def run_tiles(eng, stage, one, done=0):
            b = stage.first
            for k in range(done, stage.head):
                one(b + k, k, b + k, None)
            if stage.loops:
                with eng.Fori(0, stage.loops) as i:
                    for c in range(stage.head, stage.head + 4):
                        one(i * 4 + (b + c), i * 4 + c, b + c, i)
            for k in range(max(done, stage.head + 4 * stage.loops), stage.tiles):
                one(b + k, k, b + k, None)

        def split_hi(act, n, c, i):
            if i is None:
                if n >= NTILES:
                    return
                w = STAGE_OF[n].chunks * P
                turn = n // 4
            else:
                w = STAGE_OF[c].chunks * P
                turn = i + c // 4
            act.wait_ge(raw_loaded[c % 4], turn * 16 + 16)
            act.wait_ge(tile_done, w_slot_free(n))
            nc.scalar.activation(wh[:, c % 2, 0:w], raw[:, c % 4, 0:w], ACT.Copy).then_inc(w_hi, 1)

        def split_lo(dve, n, c, i):
            if i is None and n >= NTILES:
                return
            w = STAGE_OF[c if i is not None else n].chunks * P
            dve.wait_ge(w_hi, n + 1)
            nc.vector.tensor_tensor(wl[:, c % 2, 0:w], raw[:, c % 4, 0:w], wh[:, c % 2, 0:w],
                                    ALU.subtract).then_inc(w_lo, 1)

        def products(pe, stage, xh, xl, chunk_ready=None):
            def chunk(c, q):
                for j, (w, x) in enumerate(((wh, xh), (wh, xl), (wl, xh))):
                    for s, e in segs(stage.tokens):
                        last = nc.tensor.matmul(
                            psum[:, (c % 4) * 1024 + s:(c % 4) * 1024 + e],
                            w[:, c % 2, q * P:(q + 1) * P], x[:, q, s:e],
                            start=(q == 0 and j == 0), stop=(q == stage.chunks - 1 and j == 2))
                return last

            def weights(n):
                pe.wait_ge(w_lo, lo_ready(n))
                pe.wait_ge(drained, psum_free(n))

            def one(n, k, c, i):
                weights(n)
                for q in range(stage.chunks):
                    last = chunk(c, q)
                last.then_inc(tile_done, 1)

            if chunk_ready:
                pair = (stage.first, stage.first + 1)
                for n in pair:
                    weights(n)
                for q in range(stage.chunks):
                    chunk_ready(q)
                    for n in pair:
                        last = chunk(n, q)
                        if q == stage.chunks - 1:
                            last.then_inc(tile_done, 1)
            run_tiles(pe, stage, one, done=2 if chunk_ready else 0)

        def act_tiles(act, stage, use=None, early=False):
            def one(n, k, c, i):
                if not (early and i is None and k == 0):
                    split_hi(act, n + 1, c + 1, i)
                if use:
                    use(n, k, c, i)
            run_tiles(act, stage, one)

        def dve_tiles(dve, stage, use, early=False):
            def one(n, k, c, i):
                if not (early and i is None and k == 0):
                    split_lo(dve, n + 1, c + 1, i)
                use(n, k, c, i)
            run_tiles(dve, stage, one)

        def drain_to(dve, stage, dst, lead=0, early=False, then=None):
            def use(n, k, c, i):
                dve.wait_ge(tile_done, sum_ready(n))
                o = dst[:, bass.ds(k, 1), lead:lead + stage.tokens] if i is not None else \
                    dst[:, k:k + 1, lead:lead + stage.tokens]
                a = psum[:, (c % 4) * 1024:(c % 4) * 1024 + stage.tokens].rearrange("p (a n) -> p a n", a=1)
                nc.vector.tensor_copy(o, a).then_inc(drained, 1)
                if then:
                    then(n, k)
            dve_tiles(dve, stage, use, early)

        def drain_residual(dve, stage, gate, norm=None):
            def use(n, k, c, i):
                dve.wait_ge(tile_done, sum_ready(n))
                for g, (s, e) in enumerate(segs(stage.tokens)):
                    a = psum[:, (c % 4) * 1024 + s:(c % 4) * 1024 + e]
                    col = gate(k, g)
                    if col is None:
                        last = nc.vector.tensor_tensor(h[:, k, s:e], a, h[:, k, s:e], ALU.add)
                    else:
                        last = nc.vector.scalar_tensor_tensor(h[:, k, s:e], a, col, h[:, k, s:e],
                                                              ALU.mult, ALU.add)
                last.then_inc(drained, 1)
                if norm is not None and k >= 1:
                    add_squares(dve, norm, k - 1, stage.tokens)
            dve_tiles(dve, stage, use)
            if norm is not None:
                add_squares(dve, norm, KD - 1, stage.tokens)

        n_sq, n_add, n_sum, n_sd, n_r, n_t, n_zf, n_hi, n_z = [S(x) for x in
            ("norm_sq", "norm_added", "norm_sum", "norm_sd", "norm_r", "norm_t", "norm_zf", "norm_hi", "norm_z")]
        NPS = 3 * 1024
        SQ_ALL, ROOT = 2, 3

        def square(act, k, c, tokens):
            if c >= 2:
                act.wait_ge(n_add, KD * k + c - 1)
            nc.scalar.activation(scr[:, c % 2, 0:tokens], h[:, c, 0:tokens], ACT.Square).then_inc(n_sq, 1)

        def squares_of(act, k, stage):
            def use(n, c, _, i):
                act.wait_ge(drained, n + 5)
                square(act, k, c, stage.tokens)
            return use

        def add_squares(dve, k, c, tokens):
            dve.wait_ge(n_sq, KD * k + c + 1)
            s = scr[:, SQ_ALL, 0:tokens]
            if c == 0:
                nc.vector.tensor_copy(s, scr[:, 0, 0:tokens]).then_inc(n_add, 1)
            else:
                dve.wait_ge(n_add, KD * k + c)
                nc.vector.tensor_tensor(s, s, scr[:, c % 2, 0:tokens], ALU.add).then_inc(n_add, 1)

        def norm_pe(pe, k, tokens):
            pe.wait_ge(n_add, KD * (k + 1))
            for s, e in segs(tokens):
                last = nc.tensor.matmul(psum[:, NPS + s:NPS + e], ones[:], scr[:, SQ_ALL, s:e],
                                        start=True, stop=True)
            last.then_inc(n_sum, 1)

        def norm_act(act, k, tokens, scale, bias):
            act.wait_ge(n_sum, k + 1)
            nc.scalar.activation(scr[:, ROOT, 0:tokens], psum[:, NPS:NPS + tokens], ACT.Sqrt,
                                 bias=eps_c[:, 0:1], scale=1.0 / D).then_inc(n_sd, 1)
            for c in range(KD):
                act.wait_ge(n_t, KD * k + c + 1)
                for g, (s, e) in enumerate(segs(tokens)):
                    last = nc.scalar.activation(scr[:, c % 2, s:e], scr[:, c % 2, s:e], ACT.Identity,
                                                bias=bias(c, g), scale=scale(c, g))
                last.then_inc(n_zf, 1)
                act.wait_ge(n_zf, KD * k + c + 1)
                nc.scalar.activation(zh[:, c, 0:tokens], scr[:, c % 2, 0:tokens], ACT.Copy).then_inc(n_hi, 1)

        def norm_dve(dve, k, tokens):
            root = scr[:, ROOT, 0:tokens]
            dve.wait_ge(n_sd, k + 1)
            nc.vector.reciprocal(root, root).then_inc(n_r, 1)
            dve.wait_ge(n_r, k + 1)

            def scaled(c):
                nc.vector.tensor_tensor(scr[:, c % 2, 0:tokens], h[:, c, 0:tokens],
                                        root, ALU.mult).then_inc(n_t, 1)
            scaled(0)
            scaled(1)
            for c in range(KD):
                dve.wait_ge(n_hi, KD * k + c + 1)
                nc.vector.tensor_tensor(zl[:, c, 0:tokens], scr[:, c % 2, 0:tokens],
                                        zh[:, c, 0:tokens], ALU.subtract).then_inc(n_z, 1)
                if c + 2 < KD:
                    dve.wait_ge(n_z, KD * k + c + 1)
                    scaled(c + 2)

        def after_norm(pe, k):
            return lambda q: pe.wait_ge(n_z, KD * k + q + 1)

        silu_done, hid_hi, hid_done = S("silu_done"), S("hid_hi"), S("hid_done")
        NORM_OF_FFN = [0, 2, 3, 5]
        NORM_OF_MIX = {0: 1, 1: 4}

        def modcol(layer, kind):
            return lambda c, g: mod[:, layer, kind, c, g:g + 1]

        def mulcol(layer, s):
            return lambda c, g: amul[:, layer, s, c, g:g + 1]

        def ffn_parts(f):
            return [(ST[f"ffn{f}_up_a"], ST[f"ffn{f}_down_a"], f * NJ),
                    (ST[f"ffn{f}_up_b"], ST[f"ffn{f}_down_b"], f * NJ + JA)]

        def ffn_sp(sp, f):
            for (up, down, _), (u, d) in zip(ffn_parts(f), (("wup_a", "wdn_a"), ("wup_b", "wdn_b"))):
                load_tiles(sp, up, t[u][f])
                load_tiles(sp, down, t[d][f])

        def ffn_pe(pe, f):
            k = NORM_OF_FFN[f]
            norm_pe(pe, k, ffn_parts(f)[0][0].tokens)
            for up, down, pairs in ffn_parts(f):
                products(pe, up, zh, zl, after_norm(pe, k) if pairs == f * NJ else None)
                pe.wait_ge(hid_done, pairs + up.tiles // 2)
                products(pe, down, hidh, hidl)

        def ffn_act(act, f):
            k, layer, s = NORM_OF_FFN[f], f // 2, 2 * (f % 2)
            tok = ffn_parts(f)[0][0].tokens
            split_hi(act, ST[f"ffn{f}_up_a"].first + 1, ST[f"ffn{f}_up_a"].first + 1, None)
            norm_act(act, k, tok, mulcol(layer, s), modcol(layer, 3 * s))
            for up, down, pairs in ffn_parts(f):
                def silu(n, j, c, i):
                    if (c - up.first) % 2 == 0:
                        act.wait_ge(tile_done, sum_ready(n))
                        nc.scalar.activation(scr[:, (c - up.first) // 2 % 2, 0:tok], acc(c, tok),
                                             ACT.Silu).then_inc(silu_done, 1)
                first = pairs == f * NJ
                act_tiles(act, up, silu, early=first)
                act_tiles(act, down, None if first else squares_of(act, k + 1, down))

        def ffn_dve(dve, f):
            k, layer, s = NORM_OF_FFN[f], f // 2, 2 * (f % 2)
            tok = ffn_parts(f)[0][0].tokens
            split_lo(dve, ST[f"ffn{f}_up_a"].first + 1, ST[f"ffn{f}_up_a"].first + 1, None)
            norm_dve(dve, k, tok)
            for up, down, pairs in ffn_parts(f):
                first = pairs == f * NJ
                def hidden(n, j, c, i):
                    if (c - up.first) % 2 == 0:
                        return
                    b = (c - up.first) // 2 % 2
                    if i is None:
                        pair, jj = pairs + j // 2, j // 2
                        oh, ol = hidh[:, jj:jj + 1, 0:tok], hidl[:, jj:jj + 1, 0:tok]
                    else:
                        jj = i * 2 + (c - up.first) // 2
                        pair = i * 2 + (pairs + (c - up.first) // 2)
                        oh, ol = hidh[:, bass.ds(jj, 1), 0:tok], hidl[:, bass.ds(jj, 1), 0:tok]
                    p = scr[:, 2 + b:3 + b, 0:tok]
                    dve.wait_ge(tile_done, sum_ready(n))
                    dve.wait_ge(silu_done, pair + 1)
                    nc.vector.tensor_tensor(p, scr[:, b:b + 1, 0:tok],
                                            acc(c, tok).rearrange("p (a n) -> p a n", a=1),
                                            ALU.mult).then_inc(drained, 2)
                    dve.wait_ge(drained, n + 5)
                    nc.vector.tensor_copy(oh, p).then_inc(hid_hi, 1)
                    dve.wait_ge(hid_hi, pair + 1)
                    nc.vector.tensor_tensor(ol, p, oh, ALU.subtract).then_inc(hid_done, 1)
                dve_tiles(dve, up, hidden, early=first)
                drain_residual(dve, down, lambda c, g: mod[:, layer, 3 * s + 2, c, g:g + 1],
                               None if first else k + 1)

        def bc(ap, shape):
            return ap.unsqueeze(2).to_broadcast(shape)

        def mid(ap, n):
            return ap.unsqueeze(1).to_broadcast([P, n, ap.shape[-1]])

        chain = {}

        def link(eng, name, ins):
            chain[name] = chain.get(name, 0) + 1
            ins.then_inc(S(name + "_chain"), 1)
            eng.wait_ge(S(name + "_chain"), chain[name])

        consts, misc = S("consts_loaded"), S("x_loaded")
        first_loads = [(csc, "csc"), (ident, "c_ident")]
        first_in = S("first_loaded")
        const_loads = [(ones, "c_ones"), (sel64, "c_sel64"), (sel128, "c_sel128"), (perm_a, "c_perm_a"),
                       (perm_b, "c_perm_b"), (eps_c, "c_eps"), (ngain, "ngain"),
                       (cols, "cols"), (adab, "adab")]
        ada_in = [S(f"ada_loaded{c}") for c in range(4)]
        ada_sum, ada_row, ada_tr, mod_done, silu_c = [S(x) for x in
            ("ada_sum", "ada_row", "ada_tr", "mod_done", "silu_c")]
        x_tr, x_cp = S("x_transposed"), S("x_copied")
        NADA = 2 * NMOD * D // 512
        MT = 2048

        def start_sp(sp):
            for dst, src in first_loads:
                sp.dma_start(dst[:], t[src]).then_inc(first_in, 16)
            for i in range(NADA):
                if i >= 4:
                    sp.wait_ge(ada_sum, i - 3)
                sp.dma_start(adaw[:, i % 4], t["ada_w"][i]).then_inc(ada_in[i % 4], 16)

        def start_pool(pool):
            for dst, src in const_loads:
                pool.dma_start(dst[:], t[src]).then_inc(consts, 16)
            pool.dma_start(xin[:], t["xin"]).then_inc(misc, 16)

        def wait_consts(eng):
            eng.wait_ge(consts, 16 * len(const_loads))

        def start_pe(pe):
            def transpose_rows(a):
                pe.wait_ge(misc, 16)
                if a >= 1:
                    pe.wait_ge(x_cp, a)
                for c in range(KD):
                    last = nc.tensor.transpose(psum[:, 3072 + c * P:3072 + (c + 1) * P],
                                               xin[:, a, c * P:(c + 1) * P], ident[:])
                last.then_inc(x_tr, 1)

            pe.wait_ge(first_in, 16 * len(first_loads))
            pe.wait_ge(silu_c, 1)
            for i in range(NADA + 1):
                if i < NADA:
                    pe.wait_ge(ada_in[i % 4], 16 * (i // 4 + 1))
                    if i >= 4:
                        pe.wait_ge(ada_row, i - 3)
                    for c in range(KD):
                        last = nc.tensor.matmul(psum[0:2, i % 4 * 512:i % 4 * 512 + 512], scc[:, c, :],
                                                adaw[:, i % 4, c, :], start=c == 0, stop=c == KD - 1)
                    last.then_inc(ada_sum, 1)
                if i >= 1:
                    pe.wait_ge(ada_row, i)
                    for j in range(4):
                        m = MT + ((i - 1) * 4 + j) * 2
                        last = nc.tensor.transpose(psum[:, m:m + 2], adarow[0:2, (i - 1) % 2, j * P:(j + 1) * P],
                                                   ident[0:2, 0:2])
                    last.then_inc(ada_tr, 1)
                if 10 <= i < 16:
                    transpose_rows(i - 10)
            wait_consts(pe)

        def start_act(act):
            act.wait_ge(first_in, 16 * len(first_loads))
            nc.scalar.activation(scc[:], csc[:], ACT.Silu).then_inc(silu_c, 1)
            for i in range(NADA):
                act.wait_ge(ada_sum, i + 1)
                if i >= 2:
                    act.wait_ge(ada_tr, i - 1)
                nc.scalar.activation(adarow[0:2, i % 2, :], psum[0:2, i % 4 * 512:i % 4 * 512 + 512],
                                     ACT.Copy).then_inc(ada_row, 1)
                if i >= 20 and i < 20 + KD:
                    act.wait_ge(x_cp, 6)
                    square(act, 0, i - 20, T)
            wait_consts(act)

        def start_dve(dve):
            for a in range(6):
                dve.wait_ge(x_tr, a + 1)
                nc.vector.tensor_copy(h[:, :, a * P:(a + 1) * P],
                                      psum[:, 3072:4096].rearrange("p (c n) -> p c n", c=KD))\
                    .then_inc(x_cp, 1)
            dve.wait_ge(x_cp, 6)
            for c in range(KD):
                add_squares(dve, 0, c, T)
            wait_consts(dve)
            dve.wait_ge(ada_tr, NADA)
            for layer in range(2):
                n = NMOD * KD
                link(dve, "dve", nc.vector.tensor_tensor(
                    mod[:, layer].rearrange("p k c g -> p (k c) g"),
                    psum[:, MT + layer * 2 * n:MT + (layer + 1) * 2 * n].rearrange("p (n g) -> p n g", g=2),
                    bc(adab[:, layer, :], [P, n, 2]), ALU.add))
            for layer in range(2):
                for s in range(3):
                    nc.vector.scalar_tensor_tensor(amul[:, layer, s], mod[:, layer, 3 * s + 1], 1.0,
                                                   bc(ngain[:, layer, s, :], [P, KD, 2]), ALU.add, ALU.mult)
                    if s != 1:
                        nc.vector.tensor_scalar(mod[:, layer, 3 * s + 2], mod[:, layer, 3 * s + 2], 0.5,
                                                None, ALU.mult)
            link(dve, "dve", nc.vector.tensor_copy(nmx[:, 0:1], eps_c[:, 0:1]))
            nc.vector.tensor_copy(nmx[:, 0:1], eps_c[:, 0:1]).then_inc(mod_done, 1)

        hn_sq, hn_mm, hn_sd, hn_r, hn_bc, hn_n, hn_rot, hn_tmp, hn_f = [S("head_" + x) for x in
            ("sq", "sum", "root", "r", "spread", "normed", "rotated", "rot_parts", "roped")]
        NR = 20

        class Item:

            def __init__(self, src, tokens, gain, rope):
                self.src, self.tokens, self.gain, self.rope = src, tokens, gain, rope

        class Group:

            def __init__(self, number, items, width, mean, sq, rr):
                self.number, self.items, self.width, self.mean, self.sq, self.rr = number, items, width, mean, sq, rr
                self.tokens = max(it.tokens for it in items)

            def pick(self, i):
                return sel64[:, 18 - 2 * i:38 - 2 * i] if self.width == 64 else sel128[:, 18 - i:38 - i]

            def spread(self, i):
                if self.width == 64:
                    return pickT[0:NR, self.items[i].k % 2, :]
                return ident[0:NR, i:i + 1].to_broadcast([NR, P])

        groups, counts = {}, {"k": 0, "r": 0}
        hn_pick = S("head_picker")

        def make_picker(gr, i):
            if gr.width == 64 and i < len(gr.items):
                nc.vector.tensor_copy(pickT[0:NR, gr.items[i].k % 2, :].rearrange("p (a n) -> p a n", a=2),
                                      ident[0:NR, 2 * i:2 * i + 2].unsqueeze(2).to_broadcast([NR, 2, 64]))\
                    .then_inc(hn_pick, 1)

        def group(name, items, width, mean, sq, rr):
            for it in items:
                it.k, it.r = counts["k"], counts["r"]
                counts["k"] += 1
                counts["r"] += it.rope is not None
            groups[name] = Group(len(groups), items, width, mean, sq, rr)

        HROT = 2048

        def spread_at(it):
            c = 3072 if it.k % 2 else 1024
            return psum[:, c:c + it.tokens]

        def rot_at(it):
            return psum[:, HROT + it.r % 2 * 512:HROT + it.r % 2 * 512 + TX]

        def heads_pe(pe, name):
            gr = groups[name]
            items = gr.items

            def rotate(it):
                if it.rope is None:
                    return
                pe.wait_ge(hn_n, it.k + 1)
                if it.r >= 2:
                    pe.wait_ge(hn_tmp, it.r - 1)
                nc.tensor.matmul(rot_at(it), it.rope[0][:], it.src[:, 0:TX], start=True, stop=True)\
                    .then_inc(hn_rot, 1)

            for i, it in enumerate(items):
                pe.wait_ge(hn_sq, it.k + 1)
                for s, e in segs(it.tokens):
                    ends = [x for x in items if x.tokens >= e][-1]
                    last = nc.tensor.matmul(psum[0:NR, s:e], gr.pick(i), gr.sq[:, it.k % 2, s:e],
                                            start=i == 0, stop=it is ends)
                last.then_inc(hn_mm, 1)
            pe.wait_ge(hn_r, gr.number + 1)
            for i, it in enumerate(items):
                if i >= 2:
                    pe.wait_ge(hn_n, it.k - 1)
                if gr.width == 64:
                    pe.wait_ge(hn_pick, it.k + 1)
                for s, e in segs(it.tokens):
                    last = nc.tensor.matmul(spread_at(it)[:, s:e], gr.spread(i), gr.rr[0:NR, 0, s:e],
                                            start=True, stop=True)
                last.then_inc(hn_bc, 1)
                if i >= 1:
                    rotate(items[i - 1])
            rotate(items[-1])

        def heads_act(act, name):
            gr = groups[name]
            for i, it in enumerate(gr.items):
                if i >= 2:
                    act.wait_ge(hn_mm, it.k - 1)
                nc.scalar.activation(gr.sq[:, it.k % 2, 0:it.tokens], it.src, ACT.Square).then_inc(hn_sq, 1)
            act.wait_ge(hn_mm, gr.items[-1].k + 1)
            nc.scalar.activation(gr.rr[0:NR, 0, 0:gr.tokens], psum[0:NR, 0:gr.tokens], ACT.Sqrt,
                                 bias=eps_c[0:NR, 0:1], scale=gr.mean).then_inc(hn_sd, 1)

        def heads_dve(dve, name):
            gr = groups[name]
            items = gr.items

            def rope(it):
                if it.rope is None:
                    return
                _, cos, sin = it.rope
                x, part = it.src[:, 0:TX], gr.rr[:, 1, 0:TX]
                dve.wait_ge(hn_rot, it.r + 1)
                nc.vector.tensor_tensor(part, rot_at(it), sin, ALU.mult).then_inc(hn_tmp, 1)
                link(dve, "dve", nc.vector.tensor_tensor(x, x, cos, ALU.mult))
                dve.wait_ge(hn_tmp, it.r + 1)
                nc.vector.tensor_tensor(x, x, part, ALU.add).then_inc(hn_f, 1)
                dve.wait_ge(hn_f, it.r + 1)

            rr = gr.rr[0:NR, 0, 0:gr.tokens]
            make_picker(gr, 0)
            make_picker(gr, 1)
            dve.wait_ge(hn_sd, gr.number + 1)
            nc.vector.reciprocal(rr, rr).then_inc(hn_r, 1)
            for i, it in enumerate(items):
                dve.wait_ge(hn_bc, it.k + 1)
                nc.vector.scalar_tensor_tensor(it.src, it.src, it.gain, spread_at(it), ALU.mult, ALU.mult)\
                    .then_inc(hn_n, 1)
                make_picker(gr, i + 2)
                if i >= 1:
                    rope(items[i - 1])
            dve.wait_ge(hn_n, items[-1].k + 1)
            rope(items[-1])

        def after_heads(eng, name):
            it = groups[name].items[-1]
            eng.wait_ge(hn_n, it.k + 1)
            if it.r + (it.rope is not None):
                eng.wait_ge(hn_f, it.r + (it.rope is not None))

        scr_sq, scr_rr = scr[:, 0:2, :], scr[:, 2:4, :]
        rope_a = (perm_a, ropea[:, 0, :], ropea[:, 1, :])
        group("even", [Item(ev[:, m, :], T, cols[:, (AQ if m < 4 else AK):(AQ if m < 4 else AK) + 1],
                            rope_a) for m in range(6)] +
              [Item(ev[:, 11 + m, :], T, cols[:, BV + m:BV + m + 1], None) for m in range(4)],
              64, 1.0 / 64, scr_sq, scr_rr)
        group("odd", [Item(okv[:, m, :], T, cols[:, DK:DK + 1], None) for m in range(4)] +
              [Item(ox[:, 4 + m, :], TX, cols[:, DQ:DQ + 1], None) for m in range(4)],
              64, 1.0 / 64, scr_sq, scr_rr)
        group("dn_qk", [Item(dn[:, m, 4:DW], TX, (float(P) ** -0.5 if m < 4 else 1.0), None)
                        for m in range(8)], 128, 1.0, dsq, drr)
        group("dn_o", [Item(dn[:, m, 4:DW], TX, cols[:, DNW:DNW + 1], None) for m in range(4)],
              128, 1.0 / P, dsq, drr)
        rope_b = (perm_b, ropeb[:, 0, :], ropeb[:, 1, :])
        for hd in range(4):
            group(f"swa{hd}", [Item(sx[:, m, :], TX,
                                    cols[:, (QN if m < 3 else KN) + m % 3:(QN if m < 3 else KN) + m % 3 + 1],
                                    rope_b) for m in range(6)],
                  128, 1.0 / P, sw_s[:, :, 0:TX], sw_pt[:, :, 0:TX])

        at_qk, at_s, at_e, at_p, at_t, at_pc, at_pv, at_hi, at_o = [S("att_" + x) for x in
            ("scores", "scores_read", "exp", "probs", "transposed", "probs_t", "pv", "out_hi", "out")]
        PT0, O0 = 1536, 3072

        class Unit:

            def __init__(self, keys, segs, vals, out, scale, s, pt, c0=0, sink=None, before=None):
                self.keys, self.segs, self.vals, self.out, self.scale = keys, segs, vals, out, scale
                self.s, self.pt, self.c0, self.sink, self.before = s, pt, c0, sink, before

        units = {}
        total = {"u": 0}

        def add_units(name, us):
            for u in us:
                u.u = total["u"]
                total["u"] += 1
            units[name] = us

        def att_pe(pe, name):
            us = units[name]
            for i in range(len(us) + 2):
                if i < len(us):
                    u = us[i]
                    if i >= 1:
                        pe.wait_ge(at_s, u.u)
                    for q, k, c, w in u.keys:
                        last = nc.tensor.matmul(psum[:, c:c + w], q, k, start=True, stop=True)
                    last.then_inc(at_qk, 1)
                if 1 <= i <= len(us):
                    u = us[i - 1]
                    pe.wait_ge(at_p, u.u + 1)
                    if i >= 2:
                        pe.wait_ge(at_pc, u.u)
                    for j in range(len(u.vals)):
                        last = nc.tensor.transpose(psum[:, PT0 + j * P:PT0 + (j + 1) * P],
                                                   u.s[:, u.u % 2, u.c0 + j * P:u.c0 + (j + 1) * P], ident[:])
                    last.then_inc(at_t, 1)
                if i >= 2:
                    u = us[i - 2]
                    pe.wait_ge(at_pc, u.u + 1)
                    if i >= 4:
                        pe.wait_ge(at_o, u.u - 1)
                    for j, v in enumerate(u.vals):
                        last = nc.tensor.matmul(psum[:, O0 + u.u % 2 * 512:O0 + u.u % 2 * 512 + P], v,
                                                u.pt[:, u.u % 2, j * P:(j + 1) * P],
                                                start=j == 0, stop=j == len(u.vals) - 1)
                    last.then_inc(at_pv, 1)

        def att_act(act, name):
            us = units[name]
            for i in range(len(us) + 2):
                if 1 <= i <= len(us):
                    u = us[i - 1]
                    act.wait_ge(at_t, u.u + 1)
                    if i >= 3:
                        act.wait_ge(at_pv, u.u - 1)
                    nc.scalar.activation(u.pt[:, u.u % 2, 0:len(u.vals) * P],
                                         psum[:, PT0:PT0 + len(u.vals) * P], ACT.Copy).then_inc(at_pc, 1)
                if i < len(us):
                    u = us[i]
                    w, k = len(u.vals) * P, u.u % 4
                    act.wait_ge(at_s, u.u + 1)
                    e = nc.scalar.activation(u.s[:, u.u % 2, u.c0:u.c0 + w], u.s[:, u.u % 2, u.c0:u.c0 + w],
                                             ACT.Exp, bias=nmx[:, k:k + 1], accum_out=rsum[:, k:k + 1])
                    if u.sink is not None:
                        e = nc.scalar.activation(esink[:, k:k + 1], u.sink, ACT.Exp, bias=nmx[:, k:k + 1])
                    e.then_inc(at_e, 1)
                if i >= 2 and len(us[i - 2].out) == 3:
                    u = us[i - 2]
                    act.wait_ge(at_pv, u.u + 1)
                    r = u.out[0]
                    nc.scalar.activation(u.out[1], psum[r, O0 + u.u % 2 * 512:O0 + u.u % 2 * 512 + P],
                                         ACT.Copy).then_inc(at_hi, 1)

        def att_dve(dve, name, hi_before):
            us = units[name]
            for i in range(len(us) + 2):
                if i < len(us):
                    u = us[i]
                    w, k = len(u.vals) * P, u.u % 4
                    buf = u.s[:, u.u % 2, u.c0:u.c0 + w]
                    dve.wait_ge(at_qk, u.u + 1)
                    if i >= 2:
                        dve.wait_ge(at_t, u.u - 1)
                    if u.before:
                        u.before(dve)
                    for n, (c, cw, m) in enumerate(u.segs):
                        o = u.s[:, u.u % 2, c:c + cw]
                        if m is None:
                            ins = nc.vector.tensor_scalar(o, psum[:, c:c + cw], u.scale, None, ALU.mult)
                        else:
                            ins = nc.vector.scalar_tensor_tensor(o, psum[:, c:c + cw], u.scale, m,
                                                                 ALU.mult, ALU.add)
                    link(dve, "dve", ins)
                    link(dve, "dve", nc.vector.reduce_max(nmx[:, k:k + 1], buf, AX.X))
                    if u.sink is not None:
                        nc.vector.tensor_scalar(nmx[:, k:k + 1], nmx[:, k:k + 1], u.sink, -1.0,
                                                ALU.max, ALU.mult).then_inc(at_s, 1)
                    else:
                        nc.vector.tensor_scalar(nmx[:, k:k + 1], nmx[:, k:k + 1], -1.0, None,
                                                ALU.mult).then_inc(at_s, 1)
                    dve.wait_ge(at_e, u.u + 1)
                    if u.sink is not None:
                        link(dve, "dve", nc.vector.tensor_tensor(rsum[:, k:k + 1], rsum[:, k:k + 1],
                                                                 esink[:, k:k + 1], ALU.add))
                    link(dve, "dve", nc.vector.reciprocal(rinv[:, k:k + 1], rsum[:, k:k + 1]))
                    nc.vector.tensor_scalar(buf, buf, rinv[:, k:k + 1], None, ALU.mult).then_inc(at_p, 1)
                if i >= 2:
                    u = us[i - 2]
                    r = u.out[0]
                    a = psum[r, O0 + u.u % 2 * 512:O0 + u.u % 2 * 512 + P]
                    if len(u.out) == 3:
                        dve.wait_ge(at_hi, hi_before + i - 1)
                        nc.vector.tensor_tensor(u.out[2], a, u.out[1], ALU.subtract).then_inc(at_o, 1)
                    else:
                        dve.wait_ge(at_pv, u.u + 1)
                        nc.vector.tensor_copy(u.out[1], a).then_inc(at_o, 1)

        ev_loaded, ev_mask_in = S("ev_loaded"), S("ev_mask_loaded")
        gelu_done, v_tr, v_cp = S("gelu_done"), S("v_transposed"), S("v_copied")
        vv_tr, vv_cp, mx_mm, mx_d, mx_hi, cat_lo = [S(x) for x in
            ("vv_transposed", "vv_copied", "mix_sum", "mix_done", "mix_hi", "mix_lo")]
        EI, EO = ST["ev_in"], ST["ev_out"]

        def even_pool(pool):
            pool.wait_ge(tile_done, sum_ready(EI.first - 1))
            pool.dma_start(ropea[:], t["c_ropea"]).then_inc(ev_loaded, 16)
            pool.dma_start(wst[:], t["wst"]).then_inc(ev_loaded, 16)
            pool.dma_start(bbias[:], t["bbias"]).then_inc(ev_loaded, 16)
            pool.wait_ge(cat_lo, 6)
            pool.dma_start(ev_mask[:], t["c_ev_mask"]).then_inc(ev_mask_in, 16)

        def ev_units():
            us = []
            for hd in range(8):
                r0 = hd % 2 * 64
                r = slice(r0, r0 + 64)
                g = hd // 4
                q, k = ev[r, hd // 2, :], ev[r, 4 + g, :]
                sink = cols[:, SINK + hd:SINK + hd + 1]

                def val(tile):
                    return vdup[:, tile, g].rearrange("p a d -> p (a d)")
                for n in range(6):
                    s = slice(n * P, (n + 1) * P)
                    out = (r, zh[r, hd // 2, s], zl[r, hd // 2, s])
                    if n < 4:
                        lo, c0 = max(n - 1, 0), (P if n == 0 else 0)
                        keys = [(q[:, s], k[:, lo * P:(n + 1) * P], c0, (n + 1 - lo) * P),
                                (q[:, s], k[:, TX:T], 256, 256)]
                        tiles = list(range(lo, n + 1)) + [4, 5]
                        if n < 3:
                            keys.append((q[:, s], k[:, (n + 1) * P:(n + 2) * P], 512, P))
                            tiles.append(n + 1)
                        w = len(tiles) * P
                        us.append(Unit(keys=keys, c0=c0, segs=[(c0, w, ev_mask[:, c0:c0 + w])],
                                            scale=0.125, vals=[val(x) for x in tiles], sink=sink,
                                            out=out, s=ev_s, pt=ev_pt))
                    else:
                        us.append(Unit(keys=[(q[:, s], k[:, TX:T], 0, 256)], segs=[(0, 256, None)],
                                            scale=0.125, vals=[val(4), val(5)], sink=sink, out=out,
                                            s=ev_s, pt=ev_pt))
            return us

        add_units("even", ev_units())
        NU_EVEN = total["u"]

        def even_pe(pe):
            norm_pe(pe, 1, T)
            products(pe, EI, zh, zl, after_norm(pe, 1))
            pe.wait_ge(drained, all_drained(EI))
            for a in range(6):
                last = nc.tensor.transpose(psum[:, 3072 + a * P:3072 + (a + 1) * P],
                                           ev[:, 6, a * P:(a + 1) * P], ident[:])
            last.then_inc(v_tr, 1)
            heads_pe(pe, "even")
            after_heads(pe, "even")
            for a in range(6):
                if a >= 2:
                    pe.wait_ge(vv_cp, a - 1)
                for m in range(4):
                    last = nc.tensor.transpose(psum[:, a % 2 * 512 + m * P:a % 2 * 512 + (m + 1) * P],
                                               ev[:, 11 + m, a * P:(a + 1) * P], ident[:])
                last.then_inc(vv_tr, 1)
            pe.wait_ge(ev_loaded, 48)
            for a in range(6):
                pe.wait_ge(vv_cp, a + 1)
                if a >= 2:
                    pe.wait_ge(mx_d, a - 1)
                for m in range(4):
                    last = nc.tensor.matmul(psum[:, 1024 + a % 2 * 1024 + m * 256:1024 + a % 2 * 1024 + (m + 1) * 256],
                                            vvt[:, a, m * P:(m + 1) * P],
                                            wst[:, 2 * m:2 * m + 2, :].rearrange("p a n -> p (a n)"),
                                            start=True, stop=True)
                last.then_inc(mx_mm, 1)
            pe.wait_ge(v_cp, 1)
            pe.wait_ge(mx_d, 6)
            att_pe(pe, "even")
            pe.wait_ge(at_o, NU_EVEN)
            pe.wait_ge(cat_lo, 6)
            products(pe, EO, zh, zl)

        def even_act(act):
            split_hi(act, EI.first + 1, EI.first + 1, None)
            norm_act(act, 1, T, mulcol(0, 1), modcol(0, 3))
            act_tiles(act, EI, early=True)
            act.wait_ge(drained, all_drained(EI))
            nc.scalar.activation(ev[:, 7:11, :], ev[:, 7:11, :], ACT.Gelu_apprx_tanh).then_inc(gelu_done, 1)
            nc.scalar.activation(ev[:, 11:15, :], ev[:, 11:15, :], ACT.Gelu_apprx_tanh).then_inc(gelu_done, 1)
            act.wait_ge(gelu_done, 2)
            heads_act(act, "even")
            for a in range(6):
                act.wait_ge(vv_tr, a + 1)
                nc.scalar.activation(vvt[:, a, :], psum[:, a % 2 * 512:a % 2 * 512 + 512], ACT.Copy)\
                    .then_inc(vv_cp, 1)
            for a in range(6):
                act.wait_ge(mx_d, a + 1)
                nc.scalar.activation(zh[:, 4:8, a * P:(a + 1) * P],
                                     scr[:, a % 2, 0:512].rearrange("p (m n) -> p m n", m=4), ACT.Copy)\
                    .then_inc(mx_hi, 1)
            att_act(act, "even")
            act_tiles(act, EO, squares_of(act, 2, EO))

        def even_dve(dve):
            split_lo(dve, EI.first + 1, EI.first + 1, None)
            norm_dve(dve, 1, T)
            drain_to(dve, EI, ev, early=True)
            dve.wait_ge(v_tr, 1)
            for d in range(2):
                last = nc.vector.tensor_copy(vdup[:, :, :, d, :],
                                             psum[:, 3072:3072 + 768].rearrange("p (a g d) -> p a g d", a=6, g=2))
            last.then_inc(v_cp, 1)
            dve.wait_ge(ev_loaded, 48)
            heads_dve(dve, "even")
            dve.wait_ge(gelu_done, 2)
            for a in range(6):
                dve.wait_ge(mx_mm, a + 1)
                b = scr[:, a % 2, 0:512].rearrange("p (m n) -> p m n", m=4)
                mix = psum[:, 1024 + a % 2 * 1024:2048 + a % 2 * 1024].rearrange("p (m two n) -> p m two n", m=4, two=2)
                for g in range(2):
                    r = slice(64 * g, 64 * g + 64)
                    ins = nc.vector.tensor_tensor(b[r], mix[r, :, g, :], bbias[r], ALU.add)
                    link(dve, "dve", ins)
                nc.vector.tensor_tensor(b, b, ev[:, 7:11, a * P:(a + 1) * P], ALU.mult).then_inc(mx_d, 1)
                dve.wait_ge(mx_hi, a + 1)
                nc.vector.tensor_tensor(zl[:, 4:8, a * P:(a + 1) * P], b, zh[:, 4:8, a * P:(a + 1) * P],
                                        ALU.subtract).then_inc(cat_lo, 1)
            dve.wait_ge(ev_mask_in, 16)
            dve.wait_ge(cat_lo, 6)
            att_dve(dve, "even", 0)
            drain_residual(dve, EO, lambda c, g: mod[:, 0, 5, c, g:g + 1], 2)

        OX, OKV, OO = ST["od_in_x"], ST["od_in_kv"], ST["od_out"]
        od_loaded = S("od_loaded")
        nb_in = [S("nb_loaded0"), S("nb_loaded1")]
        ovt_tr, ovt_cp, pool_in, pool_mm, pool_hi, pool_lo = [S(x) for x in
            ("odv_transposed", "odv_copied", "pooled", "pool_sum", "pool_hi", "pool_lo")]

        def od_units():
            us = []
            for hd in range(8):
                r = slice(hd % 2 * 64, hd % 2 * 64 + 64)
                m = hd // 2
                for n in range(4):
                    s = slice(n * P, (n + 1) * P)
                    q = ox[r, 4 + m, s]
                    off = (NA_R - 1 - 2 * n) * GW
                    before = None
                    if n == 0:
                        def before(dve, hd=hd):
                            dve.wait_ge(nb_in[hd % 2], 16 * (hd // 2 + 1))
                    us.append(Unit(keys=[(q, okv[r, m, 0:TX], 0, TX), (q, okv[r, m, TX:T], TX, TC)],
                                        segs=[(0, TX, nbias[:, hd % 2, off:off + TX]), (TX, TC, None)],
                                        scale=0.125, before=before, s=od_s, pt=od_pt,
                                        vals=[ovt[:, a, m * P:(m + 1) * P] for a in range(6)],
                                        out=(r, zh[r, 4 + m, s], zl[r, 4 + m, s])))
            return us

        GW, NA_R = 64, 8
        add_units("odd", od_units())
        NU_ODD = total["u"]

        def odd_pool(pool):
            pool.wait_ge(n_z, KD * 5)
            pool.wait_ge(tile_done, sum_ready(OX.first - 1))
            pool.dma_start(wpool[:], t["wpool"]).then_inc(od_loaded, 16)
            pool.dma_start(pcnt[:], t["c_pcnt"]).then_inc(od_loaded, 16)
            for hd in range(8):
                if hd >= 2:
                    pool.wait_ge(at_s, NU_EVEN + 4 * (hd - 1))
                pool.dma_start(nbias[:, hd % 2, :], t["nbias"][hd]).then_inc(nb_in[hd % 2], 16)

        def odd_pe(pe):
            norm_pe(pe, 4, T)
            products(pe, OX, zh, zl, after_norm(pe, 4))
            products(pe, OKV, zh, zl)
            pe.wait_ge(drained, all_drained(OKV))
            for a in range(6):
                if a >= 2:
                    pe.wait_ge(ovt_cp, a - 1)
                for m in range(4):
                    last = nc.tensor.transpose(psum[:, 3072 + a % 2 * 512 + m * P:3072 + a % 2 * 512 + (m + 1) * P],
                                               okv[:, 4 + m, a * P:(a + 1) * P], ident[:])
                last.then_inc(ovt_tr, 1)
            pe.wait_ge(od_loaded, 32)
            for g in range(4):
                pe.wait_ge(pool_in, g + 1)
                nc.tensor.matmul(psum[:, g * 512:g * 512 + TX], wpool[:, g, :], ox[:, g, :],
                                 start=True, stop=True).then_inc(pool_mm, 1)
            pe.wait_ge(pool_lo, 4)
            heads_pe(pe, "odd")
            after_heads(pe, "odd")
            pe.wait_ge(ovt_cp, 6)
            att_pe(pe, "odd")
            pe.wait_ge(at_o, NU_ODD)
            products(pe, OO, zh, zl)

        def odd_act(act):
            split_hi(act, OX.first + 1, OX.first + 1, None)
            norm_act(act, 4, T, mulcol(1, 1), modcol(1, 3))
            act_tiles(act, OX, early=True)
            act_tiles(act, OKV)
            for g in range(4):
                act.wait_ge(pool_mm, g + 1)
                nc.scalar.activation(zh[:, g, 0:TX], psum[:, g * 512:g * 512 + TX], ACT.Copy,
                                     scale=cols[:, CS + g:CS + g + 1]).then_inc(pool_hi, 1)
            act.wait_ge(pool_lo, 4)
            heads_act(act, "odd")
            att_act(act, "odd")
            act_tiles(act, OO, squares_of(act, 5, OO))

        def odd_dve(dve):
            split_lo(dve, OX.first + 1, OX.first + 1, None)
            norm_dve(dve, 4, T)
            drain_to(dve, OX, ox, early=True)
            dve.wait_ge(drained, all_drained(OX))
            for j in range(3):
                link(dve, "dve", nc.vector.memset(pa[:, j, :], 0.0))

            def pool_group(n, g):
                if g >= 4:
                    return
                if g == 0:
                    dve.wait_ge(od_loaded, 32)
                w = 2 << g
                link(dve, "dve", nc.vector.tensor_copy(pa[:, 0, 8:8 + TX], ox[:, g, :]))
                src, n = 0, PADP
                for level in range(g + 1):
                    dst = 1 + level % 2
                    n -= 1 << level
                    link(dve, "dve", nc.vector.tensor_tensor(pa[:, dst, 0:n], pa[:, src, 0:n],
                                                             pa[:, src, (1 << level):(1 << level) + n], ALU.add))
                    src = dst
                mean = pa[:, src, 8 - w // 2:8 - w // 2 + TX]
                link(dve, "dve", nc.vector.tensor_tensor(mean, mean, pcnt[:, g, :], ALU.mult))
                nc.vector.tensor_tensor(ox[:, g, :], mean, ox[:, g, :], ALU.subtract).then_inc(pool_in, 1)
                dve.wait_ge(pool_in, g + 1)
            drain_to(dve, OKV, okv, then=pool_group)
            for a in range(6):
                dve.wait_ge(ovt_tr, a + 1)
                nc.vector.tensor_copy(ovt[:, a, :], psum[:, 3072 + a % 2 * 512:3072 + a % 2 * 512 + 512])\
                    .then_inc(ovt_cp, 1)
            def pool_out(g):
                dve.wait_ge(pool_hi, g + 1)
                nc.vector.scalar_tensor_tensor(zl[:, g, 0:TX], psum[:, g * 512:g * 512 + TX],
                                               cols[:, CS + g:CS + g + 1], zh[:, g, 0:TX],
                                               ALU.mult, ALU.subtract).then_inc(pool_lo, 1)
            for g in range(4):
                pool_out(g)
            heads_dve(dve, "odd")
            att_dve(dve, "odd", NU_EVEN)
            drain_residual(dve, OO, lambda c, g: mod[:, 1, 5, c, g:g + 1], 5)

        DI, DZ = ST["dn_in"], ST["dn_z"]
        dn_loaded, conv_d, conv_s, ba_mm, ba_w, z_silu, gates_d, dn_fin, dn_hi, dn_lo = [S(x) for x in
            ("dn_loaded", "conv_done", "conv_silu", "ba_sum", "ba_split", "z_silu", "decay_done",
             "dn_gated", "dn_hi", "dn_lo")]
        s_zero = S("state_zero")
        BA0 = 1536
        ALOG, DTB = 35, 39
        BETA, SPX, SPM, SPE, GG, EAL, NAB = 0, 1, 2, 3, 4, 5, 6
        SM = 7

        pe_n = ["col", "row", "kk", "tm", "ut", "x1", "tu1", "x2", "tu2", "x3", "tu3", "x4", "tu4",
                "x5", "tu5", "uw", "ws0", "up0", "ws1", "up1", "o"]
        act_n = ["gc", "eg", "er", "et", "tt", "x1", "x2", "x3", "x4", "x5", "uw", "o"]
        dve_n = ["gb", "dl", "be", "et", "el", "lt", "vb", "u1", "c1", "tu1", "c2", "tu2", "c3", "tu3",
                 "c4", "tu4", "c5", "tu5", "v0", "s0", "v1", "s1"]
        dp, da, dd = (Steps(S("dn_pe"), pe_n), Steps(S("dn_act"), act_n), Steps(S("dn_dve"), dve_n))

        def bank(b, n=512):
            return psum[:, b * 512:b * 512 + n]

        def bank4(b):
            return bank(b).rearrange("p (h n) -> p h n", h=4)

        def dn_pool(pool):
            pool.wait_ge(n_z, KD * 7)
            pool.dma_start(dmask[:], t["c_dmask"]).then_inc(dn_loaded, 16)
            pool.dma_start(wconv[:], t["wconv"]).then_inc(dn_loaded, 16)
            pool.dma_start(wba[:], t["wba"]).then_inc(dn_loaded, 16)

        MASKT, CUM, BLK = dmask[:, 0, :], dmask[:, 1, :], dmask[:, 2, :]

        def dn_tile_pe(pe, a):
            def w(steps, name, turn=a):
                pe.wait_ge(steps.sem, steps.at(turn, name))

            def done(ins):
                ins.then_inc(dp.sem, 1)
            tok = slice(4 + a * P, 4 + (a + 1) * P)
            if a:
                w(dd, "s1", a - 1)
                w(da, "o", a - 1)
            g4 = dncol[:, GG, a * 4:a * 4 + 4]
            nc.tensor.matmul(psum[:, 0:4], CUM, g4, start=True, stop=True)
            done(nc.tensor.matmul(psum[:, 4:8], BLK, g4, start=True, stop=True))
            w(dd, "gb")
            for hd in range(4):
                nc.tensor.matmul(bank4(1)[:, hd], dnb["xx"][:, hd], CUM, start=True, stop=True)
                last = nc.tensor.matmul(bank4(2)[:, hd], dnb["uc"][:, hd], ident[:], start=True, stop=True)
            done(last)
            for hd in range(4):
                q, k = dn[:, hd, tok], dn[:, 4 + hd, tok]
                nc.tensor.matmul(bank4(3)[:, hd], k, k, start=True, stop=True)
                last = nc.tensor.matmul(bank4(4)[:, hd], k, q, start=True, stop=True)
            done(last)
            for hd in range(4):
                nc.tensor.transpose(bank4(5)[:, hd], dn[:, 4 + hd, tok], ident[:])
                last = nc.tensor.transpose(bank4(6)[:, hd], dn[:, 8 + hd, tok], ident[:])
            done(last)
            w(dd, "u1")
            for hd in range(4):
                last = nc.tensor.transpose(bank4(7)[:, hd], dnb["uu"][:, hd], ident[:])
            done(last)
            for lv in range(1, 6):
                w(dd, f"c{lv}")
                if lv == 1:
                    w(da, "tt")
                else:
                    w(dd, f"tu{lv - 1}")
                for hd in range(4):
                    last = nc.tensor.matmul(bank4(0)[:, hd], dnb["uc"][:, hd], dnb["tt"][:, hd],
                                            start=True, stop=True)
                done(last)
                w(da, f"x{lv}")
                for hd in range(4):
                    last = nc.tensor.matmul(bank4(1)[:, hd], dnb["xx"][:, hd], dnb["uu"][:, hd],
                                            start=True, stop=True)
                if lv < 5:
                    for hd in range(4):
                        last = nc.tensor.matmul(bank4(2)[:, hd], dnb["uu"][:, hd], dnb["xx"][:, hd],
                                                start=True, stop=True)
                done(last)
            w(dd, "tu5")
            for hd in range(4):
                nc.tensor.matmul(bank4(3)[:, hd], dnb["uu"][:, hd], dnb["vb"][:, hd], start=True, stop=True)
                last = nc.tensor.matmul(bank4(4)[:, hd], dnb["kbe"][:, hd], dnb["uu"][:, hd],
                                        start=True, stop=True)
            done(last)
            w(da, "uw")
            for half in range(2):
                st = state[:, (2 * a + half) % 3]
                if a == 0 and half == 0:
                    pe.wait_ge(s_zero, 1)
                elif half:
                    w(dd, "s0")
                for hd in range(4):
                    last = nc.tensor.matmul(bank4(5 + 2 * half)[:, hd], dnb["wt"][:, hd], st[:, hd],
                                            start=True, stop=True)
                done(last)
                w(dd, f"v{half}")
                r = slice(64 * half, 64 * half + 64)
                for hd in range(4):
                    last = nc.tensor.matmul(bank4((6 + 2 * half) % 8)[:, hd], dnb["ke"][r, hd], dnb["vn"][r, hd],
                                            start=True, stop=True)
                done(last)
            for hd in range(4):
                o = bank4(1)[:, hd]
                nc.tensor.matmul(o, dnb["vn"][:, hd], dnb["at_"][:, hd], start=True, stop=False)
                for half in range(2):
                    c = slice(64 * half, 64 * half + 64)
                    last = nc.tensor.matmul(o[:, c], state[:, (2 * a + half) % 3, hd], dnb["qe"][:, hd, c],
                                            start=False, stop=half == 1)
            done(last)

        def dn_tile_act(act, a):
            def w(steps, name, turn=a):
                act.wait_ge(steps.sem, steps.at(turn, name))

            def run(out, in_, f=ACT.Copy, **kw):
                nc.scalar.activation(out, in_, f, **kw).then_inc(da.sem, 1)
            w(dp, "col")
            run(dncol[:, SM, 0:8], psum[:, 0:8])
            w(dd, "dl")
            nc.scalar.activation(dncol[:, SM + 1, 0:4], dncol[:, SM, 0:4], ACT.Exp)
            run(dncol[:, SM + 1, 4:8], dncol[:, SM, 8:12], ACT.Exp)
            w(dp, "row")
            if a:
                w(dp, "ws1", a - 1)
            run(dnb["wt"][:], bank4(1), ACT.Exp)
            w(dd, "et")
            run(dnb["et"][:], dnb["et"][:], ACT.Exp)
            w(dp, "ut")
            run(dnb["tt"][:], bank4(7))
            for lv in range(1, 6):
                w(dp, f"x{lv}")
                run(dnb["xx"][:], bank4(0))
            w(dp, "uw")
            nc.scalar.activation(dnb["xx"][:], bank4(3), ACT.Copy)
            run(dnb["wt"][:], bank4(4))
            w(dp, "o")
            run(dn[:, 0:4, 4 + a * P:4 + (a + 1) * P], bank4(1))

        def dn_tile_dve(dve, a):
            def w(steps, name, turn=a):
                dve.wait_ge(steps.sem, steps.at(turn, name))

            def done(ins, name):
                ins.then_inc(dd.sem, 1)
                dve.wait_ge(dd.sem, dd.at(a, name))
            tt = nc.vector.tensor_tensor
            full = [P, 4, P]
            tok = slice(4 + a * P, 4 + (a + 1) * P)
            g4, b4 = dncol[:, GG, a * 4:a * 4 + 4], dncol[:, BETA, a * 4:a * 4 + 4]
            if a:
                w(dp, "o", a - 1)
            nc.vector.tensor_copy(dnb["xx"][:], bc(g4, full))
            done(nc.vector.tensor_copy(dnb["uc"][:], bc(b4, full)), "gb")
            w(da, "gc")
            done(tt(dncol[:, SM, 8:12], dncol[:, SM, 4:8], dncol[:, SM, 0:4], ALU.subtract), "dl")
            w(da, "eg")
            done(tt(dncol[:, SM + 1, 8:12], dncol[:, SM + 1, 0:4], b4, ALU.mult), "be")
            w(dp, "row")
            w(da, "er")
            for hd in range(4):
                last = nc.vector.scalar_tensor_tensor(dnb["et"][:, hd], bank4(1)[:, hd],
                                                      dncol[:, SM, hd:hd + 1], MASKT, ALU.subtract, ALU.add)
            done(last, "et")
            nc.vector.tensor_copy(dncol[:, SM + 2, 0:8].rearrange("p (h s) -> p h s", h=4), dnb["wt"][:, :, 63:128:64])
            done(tt(dnb["qe"][:], dn[:, 0:4, tok], dnb["wt"][:], ALU.mult), "el")
            w(da, "et")
            w(dp, "kk")
            link(dve, "dve", tt(dnb["lt"][:], dnb["et"][:], bank4(2), ALU.mult))
            tt(dnb["at_"][:], dnb["et"][:], bank4(4), ALU.mult)
            done(tt(dnb["lt"][:], dnb["lt"][:], bank4(3), ALU.mult), "lt")
            w(dp, "tm")
            tt(dnb["vb"][:], bank4(6), bc(b4, full), ALU.mult)
            tt(dnb["kbe"][:], bank4(5), bc(dncol[:, SM + 1, 8:12], full), ALU.mult)
            done(tt(dnb["ke"][:], bank4(5), bc(dncol[:, SM + 1, 4:8], full), ALU.mult), "vb")
            link(dve, "dve", tt(dnb["uc"][:], dnb["lt"][:], mid(dmask[:, 3, :], 4), ALU.mult))
            done(tt(dnb["uu"][:], mid(ident[:, :], 4), dnb["uc"][:], ALU.subtract), "u1")
            for lv in range(1, 6):
                if lv > 1:
                    w(dp, f"x{lv - 1}")
                done(tt(dnb["uc"][:], dnb["lt"][:], mid(dmask[:, 3 + lv, :], 4), ALU.mult), f"c{lv}")
                w(dp, f"tu{lv}")
                if lv < 5:
                    tt(dnb["tt"][:], dnb["tt"][:], bank4(2), ALU.subtract)
                done(tt(dnb["uu"][:], dnb["uu"][:], bank4(1), ALU.subtract), f"tu{lv}")
            for half in range(2):
                r = slice(64 * half, 64 * half + 64)
                s0, s1 = state[:, (2 * a + half) % 3], state[:, (2 * a + half + 1) % 3]
                w(dp, f"ws{half}")
                w(da, "uw")
                done(tt(dnb["vn"][r], dnb["xx"][r], bank4(5 + 2 * half)[r], ALU.subtract), f"v{half}")
                w(dp, "x5")
                el = dncol[:, SM + 2, 0:8].rearrange("p (h s) -> p h s", h=4)[:, :, half]
                link(dve, "dve", tt(dnb["uc"][:], s0, bc(el, full), ALU.mult))
                w(dp, f"up{half}")
                done(tt(s1, dnb["uc"][:], bank4((6 + 2 * half) % 8), ALU.add), f"s{half}")

        def dn_pe(pe):
            norm_pe(pe, 6, TX)
            products(pe, DI, zh, zl, after_norm(pe, 6))
            products(pe, DZ, zh, zl)
            pe.wait_ge(drained, all_drained(DZ))
            pe.wait_ge(ba_w, 2)
            for a in range(4):
                s = slice(a * P, (a + 1) * P)
                for c in range(KD):
                    for j, (x, w) in enumerate(((zh, wbah), (zh, wbal), (zl, wbah))):
                        last = nc.tensor.matmul(psum[:, BA0 + a * NBA:BA0 + (a + 1) * NBA], x[:, c, s], w[:, c, :],
                                                start=(c == 0 and j == 0), stop=(c == KD - 1 and j == 2))
            last.then_inc(ba_mm, 1)
            heads_pe(pe, "dn_qk")
            after_heads(pe, "dn_qk")
            pe.wait_ge(gates_d, 1)
            for a in range(4):
                dn_tile_pe(pe, a)
            pe.wait_ge(dd.sem, dd.at(3, "s1"))
            pe.wait_ge(da.sem, da.at(3, "o"))
            heads_pe(pe, "dn_o")

        def dn_act(act):
            split_hi(act, DI.first + 1, DI.first + 1, None)
            norm_act(act, 6, TX, lambda c, g: cols[:, NW2 + c:NW2 + c + 1], lambda c, g: eps_c[:, 2:3])
            def conv_silu(m):
                act.wait_ge(conv_d, m + 1)
                nc.scalar.activation(dn[:, m, 4:DW], cacc[:, m % 2, :], ACT.Silu).then_inc(conv_s, 1)
            act_tiles(act, DI, lambda n, k, c, i: conv_silu(k - 1) if k else None, early=True)
            act.wait_ge(dn_loaded, 48)
            nc.scalar.activation(wbah[:], wba[:], ACT.Copy).then_inc(ba_w, 1)
            act_tiles(act, DZ, lambda n, k, c, i: conv_silu(11) if k == 0 else None)
            act.wait_ge(drained, all_drained(DZ))
            nc.scalar.activation(dz[:], dz[:], ACT.Silu).then_inc(z_silu, 1)
            act.wait_ge(conv_s, 12)
            heads_act(act, "dn_qk")
            act.wait_ge(ba_mm, 1)
            ba = psum[:, BA0:BA0 + 4 * NBA].rearrange("p (a n) -> p a n", a=4)
            row = lambda r: dncol[:, r, :].rearrange("p (a n) -> p a n", a=4)
            nc.scalar.activation(row(BETA), ba[:, :, 0:4], ACT.Sigmoid).then_inc(sp_s, 1)
            act.wait_ge(sp_d, 1)
            link(act, "act", nc.scalar.activation(dncol[:, SPE, :], dncol[:, SPM, :], ACT.Exp))
            nc.scalar.activation(dncol[:, EAL, 0:4], cols[:, ALOG:ALOG + 4], ACT.Exp)
            nc.scalar.activation(dncol[:, SPE, :], dncol[:, SPE, :], ACT.Ln, bias=eps_c[:, 1:2]).then_inc(sp_s, 1)
            for a in range(4):
                dn_tile_act(act, a)
            act.wait_ge(da.sem, da.at(3, "o"))
            heads_act(act, "dn_o")
            act.wait_ge(dn_fin, 1)
            nc.scalar.activation(odnh[:], dz[:], ACT.Copy).then_inc(dn_hi, 1)

        sp_s, sp_d = S("softplus_act"), S("softplus_dve")

        def dn_dve(dve):
            split_lo(dve, DI.first + 1, DI.first + 1, None)
            norm_dve(dve, 6, TX)
            dve.wait_ge(n_z, KD * 7)
            link(dve, "dve", nc.vector.memset(dn[:, :, 0:4], 0.0))

            def conv(n, m):
                if m == 0:
                    dve.wait_ge(dn_loaded, 48)
                dve.wait_ge(drained, n + 5)
                if m >= 2:
                    dve.wait_ge(conv_s, m - 1)
                c = cacc[:, m % 2, :]
                link(dve, "dve", nc.vector.tensor_scalar(c, dn[:, m, 1:1 + TX], wconv[:, m, 0:1], None, ALU.mult))
                for j in range(1, 4):
                    ins = nc.vector.scalar_tensor_tensor(c, dn[:, m, 1 + j:1 + j + TX], wconv[:, m, j:j + 1], c,
                                                         ALU.mult, ALU.add)
                    if j < 3:
                        link(dve, "dve", ins)
                ins.then_inc(conv_d, 1)
            drain_to(dve, DI, dn, lead=4, early=True, then=conv)
            drain_to(dve, DZ, dz)
            dve.wait_ge(ba_w, 1)
            nc.vector.tensor_tensor(wbal[:], wba[:], wbah[:], ALU.subtract).then_inc(ba_w, 1)
            heads_dve(dve, "dn_qk")
            dve.wait_ge(ba_mm, 1)
            ba = psum[:, BA0:BA0 + 4 * NBA].rearrange("p (a n) -> p a n", a=4)
            row = lambda r: dncol[:, r, :].rearrange("p (a n) -> p a n", a=4)
            dve.wait_ge(sp_s, 1)
            link(dve, "dve", nc.vector.tensor_tensor(row(SPX), ba[:, :, 4:8], mid(cols[:, DTB:DTB + 4], 4), ALU.add))
            link(dve, "dve", nc.vector.tensor_scalar(dncol[:, NAB, :], dncol[:, SPX, :], -1.0, None, ALU.mult))
            nc.vector.tensor_tensor(dncol[:, SPM, :], dncol[:, SPX, :], dncol[:, NAB, :], ALU.min).then_inc(sp_d, 1)
            link(dve, "dve", nc.vector.tensor_scalar(dncol[:, SPX, :], dncol[:, SPX, :], 0.0, -1.0, ALU.max, ALU.mult))
            dve.wait_ge(sp_s, 2)
            link(dve, "dve", nc.vector.tensor_tensor(dncol[:, SPX, :], dncol[:, SPX, :], dncol[:, SPE, :], ALU.subtract))
            nc.vector.memset(state[:, 0], 0.0).then_inc(s_zero, 1)
            ins = nc.vector.tensor_tensor(row(GG), row(SPX), mid(dncol[:, EAL, 0:4], 4), ALU.mult)
            ins.then_inc(gates_d, 1)
            dve.wait_ge(gates_d, 1)
            dve.wait_ge(s_zero, 1)
            for a in range(4):
                dn_tile_dve(dve, a)
            dve.wait_ge(da.sem, da.at(3, "o"))
            heads_dve(dve, "dn_o")
            after_heads(dve, "dn_o")
            dve.wait_ge(z_silu, 1)
            nc.vector.tensor_tensor(dz[:], dz[:], dn[:, 0:4, 4:DW], ALU.mult).then_inc(dn_fin, 1)
            dve.wait_ge(dn_hi, 1)
            nc.vector.tensor_tensor(odnl[:], dz[:], odnh[:], ALU.subtract).then_inc(dn_lo, 1)
            dve.wait_ge(dn_lo, 1)

        SW = [ST[f"swa{hd}_in"] for hd in range(4)]
        sw_loaded, svt_tr, svt_cp = S("sw_loaded"), S("swv_transposed"), S("swv_copied")

        def sw_units(hd):
            us = []
            for n in range(4):
                s = slice(n * P, (n + 1) * P)
                lo, n0 = max(n - 1, 0), min(n + 1, 2)
                blocks = [(0, a) for a in range(lo, n + 1)] + [(g, a) for g in (1, 2) for a in range(n + 1)]
                keys = []
                for j, (g, a) in enumerate(blocks):
                    if j and j % 4 and blocks[j - 1][0] == g:
                        q, k, c, w = keys.pop()
                        first = blocks[j - w // P][1]
                        keys.append((q, sx[:, 3 + g, first * P:(a + 1) * P], c, w + P))
                    else:
                        keys.append((sx[:, g, s], sx[:, 3 + g, a * P:(a + 1) * P], j * P, P))
                sg = [(0, n0 * P, smask[:, 2 - n0:2, :].rearrange("p a n -> p (a n)"))]
                for g in (1, 2):
                    e = 2 + 4 * g
                    sg.append(((n0 + (g - 1) * (n + 1)) * P, (n + 1) * P,
                               smask[:, e - n - 1:e, :].rearrange("p a n -> p (a n)")))
                us.append(Unit(keys=keys, segs=sg, scale=float(P) ** -0.5, s=sw_s, pt=sw_pt,
                                    vals=[svt[:, g, a, :] for g, a in blocks],
                                    out=(slice(0, P), oswa[:, hd, s])))
            return us

        for hd in range(4):
            add_units(f"swa{hd}", sw_units(hd))

        def swa_pool(pool):
            pool.wait_ge(dn_lo, 1)
            pool.dma_start(smask[:], t["c_smask"]).then_inc(sw_loaded, 16)
            pool.dma_start(ropeb[:], t["c_ropeb"]).then_inc(sw_loaded, 16)

        def swa_pe(pe):
            pe.wait_ge(dn_lo, 1)
            for hd in range(4):
                products(pe, SW[hd], zh, zl)
                pe.wait_ge(drained, all_drained(SW[hd]))
                for g in range(3):
                    if g >= 2:
                        pe.wait_ge(svt_cp, 3 * hd + g - 1)
                    for a in range(4):
                        last = nc.tensor.transpose(psum[:, 3072 + g % 2 * 512 + a * P:3072 + g % 2 * 512 + (a + 1) * P],
                                                   sx[:, 6 + g, a * P:(a + 1) * P], ident[:])
                    last.then_inc(svt_tr, 1)
                heads_pe(pe, f"swa{hd}")
                after_heads(pe, f"swa{hd}")
                pe.wait_ge(svt_cp, 3 * hd + 3)
                att_pe(pe, f"swa{hd}")
                pe.wait_ge(at_o, NU_ODD + 4 * (hd + 1))

        def swa_act(act):
            for hd in range(4):
                act_tiles(act, SW[hd])
                act.wait_ge(drained, all_drained(SW[hd]))
                heads_act(act, f"swa{hd}")
                att_act(act, f"swa{hd}")

        def swa_dve(dve):
            for hd in range(4):
                drain_to(dve, SW[hd], sx)
                for g in range(3):
                    dve.wait_ge(svt_tr, 3 * hd + g + 1)
                    nc.vector.tensor_copy(svt[:, g], psum[:, 3072 + g % 2 * 512:3584 + g % 2 * 512]
                                          .rearrange("p (a n) -> p a n", a=4)).then_inc(svt_cp, 1)
                dve.wait_ge(sw_loaded, 32)
                heads_dve(dve, f"swa{hd}")
                att_dve(dve, f"swa{hd}", NU_ODD)

        SZ, GA, BD, BS, OU = ST["swa_z"], ST["gates"], ST["br_dn"], ST["br_swa"], ST["out"]
        sz_silu, sz_m, os_hi, os_lo, g_sig, mg_d, mg_hi, mg_lo, o_tr, o_cp, o_st = [S(x) for x in
            ("swz_silu", "sw_gated", "sw_hi", "sw_lo", "gates_sig", "merged", "merged_hi", "merged_lo",
             "out_transposed", "out_copied", "out_stored0")]
        o_st = [o_st, S("out_stored1")]

        def tail_pe(pe):
            products(pe, SZ, zh, zl)
            pe.wait_ge(os_lo, 1)
            products(pe, GA, zh, zl)
            products(pe, BD, odnh, odnl)
            products(pe, BS, osh, osl)
            pe.wait_ge(mg_lo, KD)
            products(pe, OU, zh, zl)
            pe.wait_ge(drained, all_drained(OU))
            for a in range(4):
                if a >= 2:
                    pe.wait_ge(o_cp, a - 1)
                for c in range(KD):
                    last = nc.tensor.transpose(psum[:, a % 2 * 1024 + c * P:a % 2 * 1024 + (c + 1) * P],
                                               h[:, c, a * P:(a + 1) * P], ident[:])
                last.then_inc(o_tr, 1)

        def tail_act(act):
            act_tiles(act, SZ)
            act.wait_ge(drained, all_drained(SZ))
            nc.scalar.activation(szt[:], szt[:], ACT.Silu).then_inc(sz_silu, 1)
            act.wait_ge(sz_m, 1)
            nc.scalar.activation(osh[:], oswa[:], ACT.Copy).then_inc(os_hi, 1)
            act_tiles(act, GA)
            act.wait_ge(drained, all_drained(GA))
            for j in range(4):
                nc.scalar.activation(gt[:, 4 * j:4 * j + 4, :], gt[:, 4 * j:4 * j + 4, :], ACT.Sigmoid)\
                    .then_inc(g_sig, 1)
            act_tiles(act, BD)

            def upper(n, k, c, i):
                act.wait_ge(mg_d, k + 1)
                nc.scalar.activation(zh[:, k, 0:TX], gt[:, k, :], ACT.Copy).then_inc(mg_hi, 1)
            act_tiles(act, BS, upper)
            act_tiles(act, OU)

        def tail_dve(dve):
            drain_to(dve, SZ, szt)
            dve.wait_ge(sz_silu, 1)
            nc.vector.tensor_tensor(oswa[:], oswa[:], szt[:], ALU.mult).then_inc(sz_m, 1)
            dve.wait_ge(os_hi, 1)
            nc.vector.tensor_tensor(osl[:], oswa[:], osh[:], ALU.subtract).then_inc(os_lo, 1)
            dve.wait_ge(os_lo, 1)
            drain_to(dve, GA, gt)
            dve.wait_ge(g_sig, 4)

            def gate_dn(n, k, c, i):
                dve.wait_ge(tile_done, sum_ready(n))
                nc.vector.tensor_tensor(gt[:, k, :], acc(c, TX), gt[:, k, :], ALU.mult).then_inc(drained, 1)
            dve_tiles(dve, BD, gate_dn)

            def gate_swa(n, k, c, i):
                dve.wait_ge(tile_done, sum_ready(n))
                nc.vector.tensor_tensor(gt[:, 8 + k, :], acc(c, TX), gt[:, 8 + k, :], ALU.mult)\
                    .then_inc(drained, 1)
                dve.wait_ge(drained, n + 5)
                nc.vector.tensor_tensor(gt[:, k, :], gt[:, k, :], gt[:, 8 + k, :], ALU.add).then_inc(mg_d, 1)
                dve.wait_ge(mg_hi, k + 1)
                nc.vector.tensor_tensor(zl[:, k, 0:TX], gt[:, k, :], zh[:, k, 0:TX], ALU.subtract)\
                    .then_inc(mg_lo, 1)
            dve_tiles(dve, BS, gate_swa)
            drain_residual(dve, OU, lambda c, g: None)
            for a in range(4):
                dve.wait_ge(o_tr, a + 1)
                if a >= 2:
                    dve.wait_ge(o_st[a % 2], 16)
                nc.vector.tensor_copy(outb[:, a % 2, :], psum[:, a % 2 * 1024:a % 2 * 1024 + 1024])\
                    .then_inc(o_cp, 1)

        def tail_sp(sp):
            for a in range(4):
                sp.wait_ge(o_cp, a + 1)
                sp.dma_start(t["out"][a * P:(a + 1) * P, :], outb[:, a % 2, :]).then_inc(o_st[a % 2], 16)
            sp.wait_ge(o_st[0], 32)
            sp.wait_ge(o_st[1], 32)

        block = ctx.enter_context(nc.Block())

        @block.sync
        def _(sp):
            start_sp(sp)
            ffn_sp(sp, 0)
            load_tiles(sp, EI, t["ev_in"])
            load_tiles(sp, EO, t["ev_out"])
            ffn_sp(sp, 1)
            ffn_sp(sp, 2)
            load_tiles(sp, OX, t["od_in"][0:8])
            load_tiles(sp, OKV, t["od_in"][8:16])
            load_tiles(sp, OO, t["od_out"])
            ffn_sp(sp, 3)
            load_tiles(sp, DI, t["w2_dn"])
            load_tiles(sp, DZ, t["w2_z"])
            for hd in range(4):
                load_tiles(sp, SW[hd], t["w2_sw"][hd])
            load_tiles(sp, SZ, t["w2_sz"])
            load_tiles(sp, GA, t["w2_ga"])
            load_tiles(sp, BD, t["w2_bd"])
            load_tiles(sp, BS, t["w2_bs"])
            load_tiles(sp, OU, t["w2_out"])
            tail_sp(sp)

        @block.gpsimd
        def _(pool):
            start_pool(pool)
            even_pool(pool)
            odd_pool(pool)
            dn_pool(pool)
            swa_pool(pool)

        @block.scalar
        def _(act):
            start_act(act)
            split_hi(act, 0, 0, None)
            act.wait_ge(mod_done, 1)
            ffn_act(act, 0)
            even_act(act)
            ffn_act(act, 1)
            ffn_act(act, 2)
            odd_act(act)
            ffn_act(act, 3)
            dn_act(act)
            swa_act(act)
            tail_act(act)

        @block.vector
        def _(dve):
            dve.sem_inc(w_lo, 4)
            start_dve(dve)
            split_lo(dve, 0, 0, None)
            ffn_dve(dve, 0)
            even_dve(dve)
            ffn_dve(dve, 1)
            ffn_dve(dve, 2)
            odd_dve(dve)
            ffn_dve(dve, 3)
            dn_dve(dve)
            swa_dve(dve)
            tail_dve(dve)

        @block.tensor
        def _(pe):
            pe.sem_inc(tile_done, 2)
            pe.sem_inc(drained, 4)
            start_pe(pe)
            ffn_pe(pe, 0)
            even_pe(pe)
            ffn_pe(pe, 1)
            ffn_pe(pe, 2)
            odd_pe(pe)
            ffn_pe(pe, 3)
            dn_pe(pe)
            swa_pe(pe)
            tail_pe(pe)


def shape_constants():
    f = np.float32
    i = np.arange(P)
    c = {"c_ident": np.eye(P, dtype=f), "c_ones": np.ones((P, P), f)}
    x = np.arange(38)[None]
    c["c_sel64"] = (x == 18 + i[:, None] // 64).astype(f)
    c["c_sel128"] = np.repeat((x == 18).astype(f), P, 0)

    def partners(heads, half):
        w = np.zeros((P, P), f)
        for first in heads:
            for m in range(half):
                w[first + m + half, first + m] = -1.0
                w[first + m, first + m + half] = 1.0
        return w
    c["c_perm_a"] = partners(range(0, P, 32), 16)
    c["c_perm_b"] = partners([0], 16)
    c["c_eps"] = np.tile(np.array([EPS, 1.0, 0.0, 0.0], f), (P, 1))
    tok = np.arange(TX)
    m = 16
    inv = (1.0 / (np.float32(10000.0) ** (np.arange(m, dtype=f) / f(m)))).astype(f)
    row, col = (tok // 64).astype(f), (tok % 64).astype(f)
    ang = np.zeros((P, TX), f)
    for p in range(P):
        d = p % 64
        ang[p] = (row if d < 32 else col) * inv[d % 16]
    c["c_ropea"] = np.stack([np.cos(ang), np.sin(ang)], 1).astype(f)
    invb = (np.float32(500000.0) ** (-np.arange(0, 32, 2, dtype=f) / f(32))).astype(f)
    angb = np.zeros((P, TX), f)
    for p in range(32):
        angb[p] = tok.astype(f) * invb[p % 16]
    c["c_ropeb"] = np.stack([np.cos(angb), np.sin(angb)], 1).astype(f)
    q, k = i[:, None], i[None]
    z = np.zeros((P, P), f)

    def neg(valid):
        return np.where(valid, f(0), f(NEG)).astype(f)
    c["c_ev_mask"] = np.concatenate([neg(k >= q), z, z, z, neg(k <= q)], 1)
    sm = [neg(k >= q), neg(k <= q)]
    for dil in (4, 16):
        same = (q - k) % dil == 0
        sm += [neg(same)] * 3 + [neg(same & (k <= q))]
    c["c_smask"] = np.stack(sm, 1)
    cnt = np.zeros((4, TX), f)
    for g, w in enumerate((2, 4, 8, 16)):
        lo, hi = np.clip(tok - w // 2, 0, TX), np.clip(tok + w - w // 2, 0, TX)
        cnt[g] = f(1) / (hi - lo).astype(f)
    c["c_pcnt"] = np.broadcast_to(cnt[None], (P, 4, TX)).copy()
    same = q // 64 == k // 64
    dm = [neg(same & (k >= q)), (same & (k >= q)).astype(f), same.astype(f)]
    for lv in range(6):
        b = 1 << lv
        dm.append(((k // (2 * b) == q // (2 * b)) & (k // b % 2 == 1) & (q // b % 2 == 0)).astype(f))
    c["c_dmask"] = np.stack(dm, 1).astype(f)
    return c


def tiles(w, chunks):
    k, n = w.shape
    return np.ascontiguousarray(w.reshape(chunks, P, n // P, P).transpose(2, 1, 0, 3).reshape(n // P, P, chunks * P))


def lay_out(inp):
    f = {k: np.asarray(v) for k, v in inp.items()}
    a = shape_constants()
    a["xin"] = np.ascontiguousarray(np.concatenate([f["x"][0], f["ctx"][0]]).reshape(6, P, D).transpose(1, 0, 2))
    a["csc"] = np.ascontiguousarray(np.stack([f["c"][0], f["c_ctx"]], -1).reshape(KD, P, 2).transpose(1, 0, 2))
    a["ada_w"] = np.ascontiguousarray(
        f["ada_w"].reshape(2, KD, P, 18, 512).transpose(0, 3, 2, 1, 4).reshape(36, P, KD, 512))
    a["adab"] = np.ascontiguousarray(f["ada_b"].reshape(2, NMOD * KD, P).transpose(2, 0, 1))
    a["ngain"] = np.ascontiguousarray(f["norm_g"].reshape(2, 3, KD, P).transpose(3, 0, 1, 2))

    gu, wd = f["ffn_w_gu"].reshape(4, D, 2 * DFF), f["ffn_w_down"].reshape(4, DFF, D)
    up = np.stack([np.stack([tiles(g[:, :DFF], KD), tiles(g[:, DFF:], KD)], 1) for g in gu])
    a["wup_a"] = np.ascontiguousarray(up[:, :JA].reshape(4, 2 * JA, P, D))
    a["wup_b"] = np.ascontiguousarray(up[:, JA:].reshape(4, 2 * JB, P, D))
    a["wdn_a"] = np.stack([tiles(w[:JA * P], JA) for w in wd])
    a["wdn_b"] = np.stack([tiles(w[JA * P:], JB) for w in wd])

    w = f["ev_w_in"][0]
    k0, k1 = w[:, 512:576], w[:, 576:640]
    a["ev_in"] = tiles(np.concatenate([w[:, :512], k0, k0, k1, k1, w[:, 640:]], 1), KD)
    a["ev_out"] = tiles(f["ev_w_out"][0], KD)
    a["wst"] = np.ascontiguousarray(f["b_ws"][0].transpose(2, 0, 1))
    a["bbias"] = np.ascontiguousarray(np.repeat(f["b_bias"][0].reshape(4, 2, P).transpose(1, 0, 2), 64, 0))
    a["od_in"] = tiles(f["od_w_in"][0], KD)
    a["od_out"] = tiles(f["od_w_out"][0], KD)
    a["wpool"] = np.ascontiguousarray(f["c_w_pool"][0].transpose(1, 0, 2))
    rpb = f["d_rpb"][0]
    half, cq, dr, ck = np.ix_(np.arange(2), np.arange(64), np.arange(16), np.arange(64))
    start = np.clip(cq - 8, 0, 48)
    di, ci = dr - half, ck - cq + 15
    ok = (di >= 0) & (di < 15) & (ck >= start) & (ck < start + 16)
    nb = rpb[:, np.clip(di, 0, 14), np.clip(ci, 0, 30)]
    a["nbias"] = np.ascontiguousarray(np.where(ok, nb, np.float32(NEG)).reshape(8, P, 1024))

    w2 = f["w_in_2"][0]
    a["w2_dn"] = tiles(w2[:, 0:1536], KD)
    a["w2_z"] = tiles(w2[:, 1536:2048], KD)
    a["wba"] = np.ascontiguousarray(w2[:, 2048:2056].reshape(KD, P, NBA).transpose(1, 0, 2))
    qkv = w2[:, 2056:2056 + 4608].reshape(D, 3, 3, 4, P)
    a["w2_sw"] = np.stack([tiles(qkv[:, :, :, hd].reshape(D, 9 * P), KD) for hd in range(4)])
    a["w2_sz"] = tiles(w2[:, 6664:7176], KD)
    a["w2_ga"] = tiles(w2[:, 7176:9224], KD)
    a["w2_bd"] = tiles(f["w_branch_dn_2"][0], 4)
    a["w2_bs"] = tiles(f["w_branch_swa_2"][0], 4)
    a["w2_out"] = tiles(f["w_out_2"][0], KD)
    a["wconv"] = np.ascontiguousarray(f["conv_w_2"][0, :, 0].reshape(4, 12, P).transpose(2, 1, 0))

    def down(v):
        return np.asarray(v).reshape(-1, P).T

    def wide(v):
        return np.broadcast_to(np.asarray(v).reshape(1, -1), (P, np.asarray(v).size))
    cols = [np.tile(f["a_q_gain"][0], 2)[:, None], np.tile(f["a_k_gain"][0], 2)[:, None],
            down(f["b_v_gain"][0]), np.tile(f["d_q_gain"][0], 2)[:, None], np.tile(f["d_k_gain"][0], 2)[:, None],
            down(f["c_scale"][0]), down(f["norm_w_2"][0]), down(f["dn_norm_w_2"][0]),
            down(f["q_norm_w_2"][0]), down(f["k_norm_w_2"][0]), wide(f["a_sink"][0]),
            wide(f["dn_a_log_2"][0]), wide(f["dn_dt_bias_2"][0])]
    c = np.concatenate(cols, 1)
    a["cols"] = np.ascontiguousarray(np.concatenate([c, np.zeros((P, 64 - c.shape[1]), np.float32)], 1))
    return a


def kernel(**inputs):
    import concourse.bacc as bacc
    from concourse.bass_utils import run_bass_kernel_spmd

    arrays = lay_out(inputs)
    nc = bacc.Bacc("TRN2", target_bir_lowering=False, num_devices=1)
    t = {k: nc.dram_tensor("in_" + k, v.shape, mybir.dt.from_np(v.dtype), kind="ExternalInput").ap()
         for k, v in arrays.items()}
    t["out"] = nc.dram_tensor("out_x", (TX, D), mybir.dt.float32, kind="ExternalOutput").ap()
    build(nc, t)
    r = run_bass_kernel_spmd(nc, [{"in_" + k: v for k, v in arrays.items()}], core_ids=[0])
    return np.asarray(r.results[0]["out_x"]).reshape(1, TX, D)
```
